# Optimizing a Trainium2 kernel written in Bass

```python
import math
import jax, jax.numpy as jnp
from jax import lax
import numpy as np

D_MODEL = 1024
BATCH = 1
SEQ = 1024
DEPTH = 1

NORM_EPS = 1e-6
GLA_HEADS = 4
GLA_DK = 64
GLA_DV = 128
GLA_GATE_RANK = 16
GLA_GATE_TEMP = 16.0
GLA_CHUNK = 64
GLA_KW = GLA_HEADS * GLA_DK
GLA_VW = GLA_HEADS * GLA_DV
HGRN_HEADS = 4
HGRN_DIM = 128
HGRN_CHUNK = 64
HGRN_W = HGRN_HEADS * HGRN_DIM
SSM_D_INNER = D_MODEL
SSM_HEAD_DIM = 64
SSM_HEADS = SSM_D_INNER // SSM_HEAD_DIM
SSM_GROUPS = 4
SSM_STATE = 128
SSM_CONV = 4
SSM_CHUNK = 128
SSM_CONV_DIM = SSM_D_INNER + 2 * SSM_GROUPS * SSM_STATE
N_BRANCHES = 3
MOE_GROUPS = 4
MOE_EXPERTS_PER_GROUP = 8
MOE_EXPERTS = MOE_GROUPS * MOE_EXPERTS_PER_GROUP
MOE_TOP_K = 2
MOE_FF = 512
MOE_BLOCK = 128
IN_SPLITS = (GLA_KW, GLA_KW, GLA_VW, GLA_GATE_RANK, GLA_VW,
             HGRN_W, HGRN_W, HGRN_W, HGRN_W,
             SSM_D_INNER, SSM_CONV_DIM, SSM_HEADS,
             N_BRANCHES * D_MODEL)
IN_PROJ_WIDTH = (2 * GLA_KW + 2 * GLA_VW + GLA_GATE_RANK + 4 * HGRN_W
                 + SSM_D_INNER + SSM_CONV_DIM + SSM_HEADS + N_BRANCHES * D_MODEL)

kernel_name = "hybrid_gla_hgrn2_ssd_hmoe"

def rms_norm(x, w):
    xf = x.astype(jnp.float32)
    y = xf * lax.rsqrt(jnp.mean(xf * xf, axis=-1, keepdims=True) + NORM_EPS)
    return (y * w.astype(jnp.float32)).astype(x.dtype)

def _to_chunks(t, chunk):
    b, t_len, h, d = t.shape
    return jnp.transpose(t.reshape(b, t_len // chunk, chunk, h, d), (1, 0, 3, 2, 4))

def _from_chunks(t):
    n, b, h, c, d = t.shape
    return jnp.transpose(t, (1, 0, 3, 2, 4)).reshape(b, n * c, h, d)

def chunked_gated_linear_attention(q, k, v, log_decay, chunk):
    bsz, _, h, dk = q.shape
    dv = v.shape[-1]
    qc, kc, vc, gc = (_to_chunks(t.astype(jnp.float32), chunk) for t in (q, k, v, log_decay))
    causal = jnp.tril(jnp.ones((chunk, chunk), dtype=bool))[:, :, None]

    def step(state, inp):
        qi, ki, vi, gi = inp
        b = jnp.cumsum(gi, axis=2)
        o_inter = jnp.einsum('bhcd,bhde->bhce', qi * jnp.exp(b), state)
        rel = b[:, :, :, None, :] - b[:, :, None, :, :]
        rel_decay = jnp.where(causal, jnp.exp(jnp.where(causal, rel, 0.0)), 0.0)
        scores = jnp.einsum('bhid,bhjd,bhijd->bhij', qi, ki, rel_decay)
        o_intra = jnp.einsum('bhij,bhje->bhie', scores, vi)
        b_last = b[:, :, -1, :]
        k_to_end = ki * jnp.exp(b_last[:, :, None, :] - b)
        state = state * jnp.exp(b_last)[..., None] + jnp.einsum('bhcd,bhce->bhde', k_to_end, vi)
        return state, o_inter + o_intra

    s0 = jnp.zeros((bsz, h, dk, dv), jnp.float32)
    _, o = lax.scan(step, s0, (qc, kc, vc, gc))
    return _from_chunks(o)

def ssd_chunked_scan(x, dt, a_neg, bm, cm, chunk):
    bsz, t_len, h, p = x.shape
    g, n_state = bm.shape[2], bm.shape[3]
    rep = h // g
    n = t_len // chunk
    xc = jnp.transpose(x.reshape(bsz, n, chunk, g, rep, p), (1, 0, 3, 4, 2, 5))
    dtc = jnp.transpose(dt.reshape(bsz, n, chunk, g, rep), (1, 0, 3, 4, 2))
    bc = jnp.transpose(bm.reshape(bsz, n, chunk, g, n_state), (1, 0, 3, 2, 4))
    cc = jnp.transpose(cm.reshape(bsz, n, chunk, g, n_state), (1, 0, 3, 2, 4))
    ac = dtc * a_neg.reshape(g, rep)[None, None, :, :, None]
    causal = jnp.tril(jnp.ones((chunk, chunk), dtype=bool))

    def step(state, inp):
        xi, dti, ai, bi, ci = inp
        b = jnp.cumsum(ai, axis=-1)
        seg = b[..., :, None] - b[..., None, :]
        decay = jnp.where(causal, jnp.exp(jnp.where(causal, seg, 0.0)), 0.0)
        cb = jnp.einsum('bgin,bgjn->bgij', ci, bi)
        w = decay * cb[:, :, None] * dti[..., None, :]
        y = jnp.einsum('bgrij,bgrjp->bgrip', w, xi)
        y = y + jnp.einsum('bgin,bgrpn->bgrip', ci, state) * jnp.exp(b)[..., None]
        b_last = b[..., -1:]
        wts = jnp.exp(b_last - b) * dti
        state = state * jnp.exp(b_last)[..., None] + jnp.einsum('bgrc,bgrcp,bgcn->bgrpn', wts, xi, bi)
        return state, y

    s0 = jnp.zeros((bsz, g, rep, p, n_state), jnp.float32)
    _, y = lax.scan(step, s0, (xc, dtc, ac, bc, cc))
    return jnp.transpose(y, (1, 0, 4, 2, 3, 5)).reshape(bsz, t_len, h, p)

def causal_depthwise_conv(u, w, b):
    c = u.shape[-1]
    out = lax.conv_general_dilated(
        u, w[:, None, :].astype(u.dtype), window_strides=(1,),
        padding=((w.shape[0] - 1, 0),), dimension_numbers=('NWC', 'WIO', 'NWC'),
        feature_group_count=c)
    return out + b.astype(u.dtype)

def hybrid_mixer(h, w_in, gla_gk_up, gla_gk_bias, gla_norm_w, lb, hgrn_norm_w,
                 ssm_conv_w, ssm_conv_b, ssm_dt_bias, ssm_a_log, ssm_d, ssm_norm_w,
                 w_br_gla, w_br_hgrn, w_br_ssm, w_out):
    f32 = jnp.float32
    dtype = h.dtype
    bsz, t_len, _ = h.shape
    proj = h @ w_in
    offs = np.cumsum(IN_SPLITS)[:-1].tolist()
    (gq, gk, gv, g_low, gr, hq, hf, hi, hg, sz, sxbc, sdt, gates) = jnp.split(proj, offs, axis=-1)

    q = gq.astype(f32).reshape(bsz, t_len, GLA_HEADS, GLA_DK) * GLA_DK ** -0.5
    k = gk.astype(f32).reshape(bsz, t_len, GLA_HEADS, GLA_DK)
    v = gv.astype(f32).reshape(bsz, t_len, GLA_HEADS, GLA_DV)
    gate_logit = (g_low @ gla_gk_up + gla_gk_bias).astype(f32)
    log_a = (jax.nn.log_sigmoid(gate_logit) / GLA_GATE_TEMP).reshape(bsz, t_len, GLA_HEADS, GLA_DK)
    o = chunked_gated_linear_attention(q, k, v, log_a, GLA_CHUNK)
    o = rms_norm(o, gla_norm_w.reshape(GLA_HEADS, GLA_DV)).reshape(bsz, t_len, GLA_VW)
    y_gla = (o * jax.nn.silu(gr.astype(f32))).astype(dtype)

    lbh = lb.reshape(HGRN_HEADS, HGRN_DIM)
    q = jax.nn.silu(hq.astype(f32)).reshape(bsz, t_len, HGRN_HEADS, HGRN_DIM) * HGRN_DIM ** -0.5
    f_raw = hf.astype(f32).reshape(bsz, t_len, HGRN_HEADS, HGRN_DIM)
    log_f = jnp.logaddexp(jnp.log(lbh), jnp.log1p(-lbh) + jax.nn.log_sigmoid(f_raw))
    k = (1.0 - lbh) * jax.nn.sigmoid(-f_raw)
    v = hi.astype(f32).reshape(bsz, t_len, HGRN_HEADS, HGRN_DIM)
    o = chunked_gated_linear_attention(q, k, v, log_f, HGRN_CHUNK)
    o = rms_norm(o, hgrn_norm_w.reshape(HGRN_HEADS, HGRN_DIM)).reshape(bsz, t_len, HGRN_W)
    y_hgrn = (o * jax.nn.silu(hg.astype(f32))).astype(dtype)

    xbc = jax.nn.silu(causal_depthwise_conv(sxbc, ssm_conv_w, ssm_conv_b))
    xs, bm, cm = jnp.split(xbc, [SSM_D_INNER, SSM_D_INNER + SSM_GROUPS * SSM_STATE], axis=-1)
    xs = xs.astype(f32).reshape(bsz, t_len, SSM_HEADS, SSM_HEAD_DIM)
    bm = bm.astype(f32).reshape(bsz, t_len, SSM_GROUPS, SSM_STATE)
    cm = cm.astype(f32).reshape(bsz, t_len, SSM_GROUPS, SSM_STATE)
    dt = jax.nn.softplus(sdt.astype(f32) + ssm_dt_bias.astype(f32))
    a_neg = -jnp.exp(ssm_a_log.astype(f32))
    y = ssd_chunked_scan(xs, dt, a_neg, bm, cm, SSM_CHUNK)
    y = y + ssm_d.astype(f32)[:, None] * xs
    y = y.reshape(bsz, t_len, SSM_D_INNER) * jax.nn.silu(sz.astype(f32))
    y = rms_norm(y.reshape(bsz, t_len, SSM_GROUPS, SSM_D_INNER // SSM_GROUPS),
                 ssm_norm_w.reshape(SSM_GROUPS, SSM_D_INNER // SSM_GROUPS))
    y_ssm = y.reshape(bsz, t_len, SSM_D_INNER).astype(dtype)

    g = jax.nn.sigmoid(gates.astype(f32)).reshape(bsz, t_len, N_BRANCHES, D_MODEL).astype(dtype)
    merged = (g[:, :, 0] * (y_gla @ w_br_gla)
              + g[:, :, 1] * (y_hgrn @ w_br_hgrn)
              + g[:, :, 2] * (y_ssm @ w_br_ssm))
    return merged @ w_out

def grouped_expert_ffn(tokens, expert_ids, w_gate, w_up, w_down):
    n, d = tokens.shape
    e_count = w_gate.shape[0]
    flat_e = expert_ids.reshape(-1)
    n_assign = flat_e.shape[0]
    order = jnp.argsort(flat_e)
    sorted_e = flat_e[order]
    sorted_tok = order // MOE_TOP_K
    counts = jnp.bincount(flat_e, length=e_count)
    starts = jnp.cumsum(counts) - counts
    padded = (counts + MOE_BLOCK - 1) // MOE_BLOCK * MOE_BLOCK
    padded_ends = jnp.cumsum(padded)
    padded_starts = padded_ends - padded
    dest = padded_starts[sorted_e] + jnp.arange(n_assign) - starts[sorted_e]
    rows = n_assign + e_count * MOE_BLOCK
    n_blocks = rows // MOE_BLOCK
    buf_tok = jnp.full((rows,), n, jnp.int32).at[dest].set(sorted_tok.astype(jnp.int32))
    tok_pad = jnp.concatenate([tokens, jnp.zeros((1, d), tokens.dtype)], axis=0)
    xb = tok_pad[buf_tok].reshape(n_blocks, MOE_BLOCK, d)
    block_e = jnp.minimum(jnp.searchsorted(padded_ends, jnp.arange(n_blocks) * MOE_BLOCK, side='right'),
                          e_count - 1)

    def block_ffn(args):
        xblk, e = args
        hid = jax.nn.silu(xblk @ w_gate[e]) * (xblk @ w_up[e])
        return hid @ w_down[e]

    yb = lax.map(block_ffn, (xb, block_e)).reshape(rows, d)
    y = jnp.zeros((n_assign, d), yb.dtype).at[order].set(yb[dest])
    return y.reshape(n, MOE_TOP_K, d)

def hierarchical_moe(h, rg_w, rg_b, re_w, re_b, w_gate, w_up, w_down):
    f32 = jnp.float32
    bsz, t_len, d = h.shape
    tokens = h.reshape(-1, d)
    n = tokens.shape[0]
    g_prob = jax.nn.softmax((tokens @ rg_w).astype(f32) + rg_b.astype(f32), axis=-1)
    g_p, g_idx = lax.top_k(g_prob, 1)
    e_logits = ((tokens @ re_w).astype(f32) + re_b.astype(f32)).reshape(n, MOE_GROUPS, MOE_EXPERTS_PER_GROUP)
    e_logits = jnp.take_along_axis(e_logits, g_idx[:, :, None], axis=1)[:, 0]
    e_p, e_local = lax.top_k(jax.nn.softmax(e_logits, axis=-1), MOE_TOP_K)
    e_p = e_p / jnp.sum(e_p, axis=-1, keepdims=True)
    weights = g_p * e_p
    expert_ids = g_idx * MOE_EXPERTS_PER_GROUP + e_local
    y = grouped_expert_ffn(tokens, expert_ids, w_gate, w_up, w_down)
    out = jnp.einsum('nk,nkd->nd', weights.astype(y.dtype), y)
    return out.reshape(bsz, t_len, d)

def setup_inputs(seed: int = 0) -> dict:
    key = jax.random.key(seed)
    ks = jax.random.split(key, 32)
    f32 = jnp.float32
    L, D = DEPTH, D_MODEL
    res_scale = (2.0 * DEPTH) ** -0.5

    def nrm(k, shape, scale):
        return jax.random.normal(k, shape, f32) * scale

    dt0 = jnp.exp(jax.random.uniform(ks[10], (L, SSM_HEADS), f32, math.log(1e-3), math.log(1e-1)))
    return {
        "x": jax.random.normal(ks[0], (BATCH, SEQ, D), f32),
        "norm1_w": 1.0 + nrm(ks[1], (L, D), 0.02),
        "w_in": nrm(ks[2], (L, D, IN_PROJ_WIDTH), D ** -0.5),
        "gla_gk_up": nrm(ks[3], (L, GLA_GATE_RANK, GLA_KW), GLA_GATE_RANK ** -0.5),
        "gla_gk_bias": nrm(ks[4], (L, GLA_KW), 0.1),
        "gla_norm_w": 1.0 + nrm(ks[5], (L, GLA_VW), 0.02),
        "hgrn_lb_logits": nrm(ks[6], (L, HGRN_W), 0.5),
        "hgrn_norm_w": 1.0 + nrm(ks[7], (L, HGRN_W), 0.02),
        "ssm_conv_w": nrm(ks[8], (L, SSM_CONV, SSM_CONV_DIM), SSM_CONV ** -0.5),
        "ssm_conv_b": nrm(ks[9], (L, SSM_CONV_DIM), 0.02),
        "ssm_dt_bias": dt0 + jnp.log(-jnp.expm1(-dt0)),
        "ssm_a_log": jnp.log(jax.random.uniform(ks[11], (L, SSM_HEADS), f32, 1.0, 16.0)),
        "ssm_d": 1.0 + nrm(ks[12], (L, SSM_HEADS), 0.02),
        "ssm_norm_w": 1.0 + nrm(ks[13], (L, SSM_D_INNER), 0.02),
        "w_br_gla": nrm(ks[14], (L, GLA_VW, D), GLA_VW ** -0.5),
        "w_br_hgrn": nrm(ks[15], (L, HGRN_W, D), HGRN_W ** -0.5),
        "w_br_ssm": nrm(ks[16], (L, SSM_D_INNER, D), SSM_D_INNER ** -0.5),
        "w_out": nrm(ks[17], (L, D, D), D ** -0.5 * res_scale),
        "norm2_w": 1.0 + nrm(ks[18], (L, D), 0.02),
        "router_group_w": nrm(ks[19], (L, D, MOE_GROUPS), D ** -0.5),
        "router_group_b": nrm(ks[20], (L, MOE_GROUPS), 0.01),
        "router_expert_w": nrm(ks[21], (L, D, MOE_EXPERTS), D ** -0.5),
        "router_expert_b": nrm(ks[22], (L, MOE_EXPERTS), 0.01),
        "moe_w_gate": nrm(ks[23], (L, MOE_EXPERTS, D, MOE_FF), D ** -0.5),
        "moe_w_up": nrm(ks[24], (L, MOE_EXPERTS, D, MOE_FF), D ** -0.5),
        "moe_w_down": nrm(ks[25], (L, MOE_EXPERTS, MOE_FF, D), MOE_FF ** -0.5 * res_scale),
        "final_norm_w": 1.0 + nrm(ks[26], (D,), 0.02),
    }

def reference(x, norm1_w, w_in, gla_gk_up, gla_gk_bias, gla_norm_w, hgrn_lb_logits, hgrn_norm_w,
              ssm_conv_w, ssm_conv_b, ssm_dt_bias, ssm_a_log, ssm_d, ssm_norm_w,
              w_br_gla, w_br_hgrn, w_br_ssm, w_out, norm2_w,
              router_group_w, router_group_b, router_expert_w, router_expert_b,
              moe_w_gate, moe_w_up, moe_w_down, final_norm_w):
    lower_bounds = jnp.cumsum(jax.nn.softmax(hgrn_lb_logits.astype(jnp.float32), axis=0), axis=0)
    for l in range(DEPTH):
        lb = lower_bounds[l] - lower_bounds[0]
        h = rms_norm(x, norm1_w[l])
        x = x + hybrid_mixer(h, w_in[l], gla_gk_up[l], gla_gk_bias[l], gla_norm_w[l], lb, hgrn_norm_w[l],
                             ssm_conv_w[l], ssm_conv_b[l], ssm_dt_bias[l], ssm_a_log[l], ssm_d[l],
                             ssm_norm_w[l], w_br_gla[l], w_br_hgrn[l], w_br_ssm[l], w_out[l])
        h = rms_norm(x, norm2_w[l])
        x = x + hierarchical_moe(h, router_group_w[l], router_group_b[l], router_expert_w[l],
                                 router_expert_b[l], moe_w_gate[l], moe_w_up[l], moe_w_down[l])
    return rms_norm(x, final_norm_w)


_drawn_inputs = setup_inputs


def setup_inputs(seed=0):
    import zlib

    import numpy as np

    out = dict(_drawn_inputs(seed))
    spreads = {}
    factors = {'gla_gk_bias': 3.767,
     'gla_norm_w': 32.029,
     'hgrn_norm_w': 32.368,
     'ssm_conv_b': 3.462,
     'ssm_d': 32.717,
     'ssm_norm_w': 18.901,
     'router_group_b': 64.0,
     'router_expert_b': 39.791,
     'final_norm_w': 7.836,
     'norm2_w': 7.842}
    for name, (base, spread) in spreads.items():
        noise = np.random.default_rng([zlib.crc32(name.encode()), seed]).standard_normal(out[name].shape)
        drawn = base * np.exp(spread * noise) if base else spread * noise
        out[name] = __import__('jax').numpy.asarray(drawn.astype(out[name].dtype))
    for name, factor in factors.items():
        out[name] = (out[name] * factor).astype(out[name].dtype)
    return out
```

```python
import math
from contextlib import ExitStack

import numpy as np

import concourse.bass as bass
from concourse import mybir

F32 = mybir.dt.float32
F32R = mybir.dt.float32r
I32 = mybir.dt.int32
U32 = mybir.dt.uint32
U8 = mybir.dt.uint8
ALU = mybir.AluOpType
ACT = mybir.ActivationFunctionType
AX = mybir.AxisListType

P = 128
T = 1024
D = 1024
CH = 128
NCH = T // CH
KT = D // P
EPS = 1e-6
EXP_LN_SET = "natural_log_exp_and_others"

GLA_HEADS, GLA_DK, GLA_DV, GLA_RANK, GLA_TEMP = 4, 64, 128, 16, 16.0
HG_HEADS, HG_DIM = 4, 128
SSM_HEADS, SSM_HD, SSM_GROUPS, SSM_STATE, SSM_CONV = 16, 64, 4, 128, 4
N_GROUPS, PER_GROUP = 4, 8
N_EXPERTS, FF = 32, 512
SLAB = 128
N_EXTRA = 2 * T // SLAB - 1
EMPTY = 1 << 20

WIDTHS = dict(gq=256, gk=256, gv=512, glow=16, gr=512, hq=512, hf=512, hi=512, hg=512,
              sz=1024, sxbc=2048, sdt=16, gates=3072)
COL = {}
_at = 0
for _name, _w in WIDTHS.items():
    COL[_name] = _at
    _at += _w
IN_W = _at


def semaphores(nc, ctx):
    made = []

    def clear():
        numbers = sorted(s.num for s in made)
        first = [n for n in numbers if n - 1 not in numbers]
        last = [n for n in numbers if n + 1 not in numbers]
        for a, z in zip(first, last):
            nc.gpsimd.sem_clear(range(a, z + 1))
        nc.all_engine_barrier()
    ctx.callback(clear)

    def sem(name):
        made.append(ctx.enter_context(nc.semaphore(name)))
        return made[-1]
    return sem


PAIR = 256


class Chain:

    def __init__(self, eng, sem):
        self.eng, self.sem, self.base, self.n = eng, sem, 0, 0

    def link(self, ins):
        self.n += 1
        ins.then_inc(self.sem, 1)
        self.eng.wait_ge(self.sem, self.base + self.n)

    def turn(self, i, each):
        self.base, self.n = i * each, 0


def norm1_and_decays(nc, io, dr, ident, h_hi, h_lo):
    HF_T = WIDTHS["hf"] // P
    GK_T = GLA_HEADS * GLA_DK // P
    DT = 32
    N_CHAIN = 1 + HF_T + GK_T
    N_PAR = 6
    with ExitStack() as ctx:
        sb = lambda name, shape, dt=F32: ctx.enter_context(nc.sbuf_tensor(name, shape, dt))
        sem = semaphores(nc, ctx)
        x_in = [sb(f"x_in{b}", [P, D]) for b in range(2)]
        x_n = [sb(f"x_n{b}", [P, D]) for b in range(2)]
        h_f = sb("h_f", [P, KT, CH])
        w_raw = sb("wa_raw", [P, KT, 512])
        w_hi = sb("wa_hi", [P, KT, 512], F32R)
        w_lo = sb("wa_lo", [P, KT, 512], F32R)
        v_raw = sb("va_raw", [P, KT, P])
        v_hi = sb("va_hi", [P, KT, P], F32R)
        v_lo = sb("va_lo", [P, KT, P], F32R)
        xs = [sb(f"xs{b}", [P, T]) for b in range(2)]
        ab = [sb(f"ab{b}", [P, T]) for b in range(2)]
        ld = [sb(f"ld{b}", [P, T]) for b in range(2)]
        cum = [sb(f"cum{b}", [P, T]) for b in range(2)]
        keys = [sb(f"keys{b}", [P, T]) for b in range(2)]
        seg0 = sb("seg0", [P, T])
        norm_w = sb("norm_w", [P, KT])
        stat = sb("stat", [P, NCH, 2])
        gk_up = sb("gk_up", [GLA_RANK, GLA_HEADS * GLA_DK])
        gk_bias = sb("gk_bias", [P, GK_T])
        dt_bias = sb("dt_bias", [64, 1])
        a_neg = sb("a_neg", [64, 1])
        lb_in = sb("lb_in", [P, HF_T])
        lb = sb("lb", [P, 6, HF_T])
        cst = sb("cst", [P, 2])
        glow = sb("glow", [GLA_RANK, T])
        acc = [ctx.enter_context(nc.psum_tensor(f"acc{b}", [P, T], F32)) for b in range(3)]
        tr = ctx.enter_context(nc.psum_tensor("tr", [P, T], F32))

        ident0 = sem("ident0")
        ident_ready = sem("ident_ready")
        c_ready = sem("c_ready")
        v_zero = sem("v_zero")
        seg_ready = sem("seg_ready")
        par_in = sem("par_in")
        x_loaded = [sem(f"x_loaded{b}") for b in range(2)]
        rstd_ready = sem("rstd_ready")
        xn_ready = sem("xn_ready")
        xT_ready = sem("xT_ready")
        h_ready = sem("h_ready")
        v_loaded = sem("v_loaded")
        w_loaded = sem("w_loaded")
        v_split = sem("v_split")
        w_split = sem("w_split")
        mm_done = sem("mm_done")
        acc_free = sem("acc_free")
        glow_ready = sem("glow_ready")
        abs_ready = sem("abs_ready")
        log1p_ready = sem("log1p_ready")
        karg_ready = sem("karg_ready")
        keys_ready = sem("keys_ready")
        cum_ready = sem("cum_ready")
        aneg_ready = sem("aneg_ready")
        lbarg_ready = sem("lbarg_ready")
        lbexp_ready = sem("lbexp_ready")
        oml_ready = sem("oml_ready")
        keybias_ready = sem("keybias_ready")
        cum_stored = [sem(f"cum_stored{b}") for b in range(2)]
        keys_stored = [sem(f"keys_stored{b}") for b in range(2)]
        dt_stored = sem("dt_stored")
        dve_own = sem("dve_own")
        act_own = sem("act_own")
        pool_own = sem("pool_own")
        block = ctx.enter_context(nc.Block())

        @block.sync
        def _(sp):
            for c in range(NCH):
                if c >= 2:
                    sp.wait_ge(xn_ready, c - 1)
                sp.dma_start(x_in[c % 2][:], io["x"][c * CH:(c + 1) * CH, :]).then_inc(x_loaded[c % 2], 16)
                if c == 1:
                    sp.dma_start(norm_w[:], io["norm1_w"].rearrange("(k p) -> p k", p=P)).then_inc(par_in, 16)
                    sp.dma_start(gk_up[:], io["gla_gk_up"]).then_inc(par_in, 16)
                    sp.dma_start(gk_bias[:], io["gla_gk_bias"].rearrange("(k p) -> p k", p=P)).then_inc(par_in, 16)
                    sp.dma_start(dt_bias[DT:DT + 16, :], io["ssm_dt_bias"].rearrange("(p a) -> p a", a=1)).then_inc(par_in, 16)
                    sp.dma_start(a_neg[DT:DT + 16, :], io["ssm_a_log"].rearrange("(p a) -> p a", a=1)).then_inc(par_in, 16)
                    sp.dma_start(lb_in[:], io["hgrn_lb_logits"].rearrange("(k p) -> p k", p=P)).then_inc(par_in, 16)
                    sp.wait_ge(v_zero, 1)
                    for at, name in ((0, "glow"), (DT, "sdt")):
                        sp.dma_start(v_raw[:, :, at:at + 16], io["w_in"][:, COL[name]:COL[name] + 16]
                                     .rearrange("(k p) n -> p k n", p=P)).then_inc(v_loaded, 16)
                    sp.dma_start(w_raw[:], io["w_in"][:, COL["hf"]:COL["hf"] + 512]
                                 .rearrange("(k p) n -> p k n", p=P)).then_inc(w_loaded, 16)
            sp.wait_ge(cum_ready, 1)
            sp.dma_start(dr["b_ssm"], cum[0][DT:DT + 16, :]).then_inc(cum_stored[0], 16)
            sp.dma_start(dr["dt"], ld[0][DT:DT + 16, :]).then_inc(dt_stored, 16)
            for q in range(1, N_CHAIN):
                if q <= HF_T:
                    sp.wait_ge(keys_ready, q)
                    sp.dma_start(dr["k_hg"][(q - 1) * P:q * P, :], keys[q % 2][:]).then_inc(keys_stored[q % 2], 16)
                sp.wait_ge(cum_ready, q + 1)
                row = (GK_T + q - 1) * P if q <= HF_T else (q - 1 - HF_T) * P
                sp.dma_start(dr["cum"][row:row + P, :], cum[q % 2][:]).then_inc(cum_stored[q % 2], 16)
            sp.wait_ge(cum_stored[0], 16 * ((N_CHAIN + 1) // 2))
            sp.wait_ge(cum_stored[1], 16 * (N_CHAIN // 2))
            sp.wait_ge(keys_stored[0], 16 * (HF_T // 2))
            sp.wait_ge(keys_stored[1], 16 * (HF_T // 2))
            sp.wait_ge(dt_stored, 16)

        @block.gpsimd
        def _(pool):
            nc.gpsimd.memset(ident[:], 0.0).then_inc(ident0, 1)
            pool.wait_ge(ident0, 1)
            nc.gpsimd.affine_select(out=ident[:], in_=ident[:], compare_op=ALU.not_equal, fill=1.0, base=0,
                                    pattern=[[-1, P]], channel_multiplier=1).then_inc(ident_ready, 1)
            nc.gpsimd.memset(v_raw[:], 0.0).then_inc(v_zero, 1)
            nc.gpsimd.memset(seg0[:], 1.0).then_inc(pool_own, 1)
            pool.wait_ge(pool_own, 1)
            nc.gpsimd.memset(seg0[:, 0:T:CH], 0.0).then_inc(seg_ready, 1)
            pool.wait_ge(v_loaded, 32)
            nc.gpsimd.tensor_copy(v_hi[:], v_raw[:]).then_inc(pool_own, 1)
            pool.wait_ge(pool_own, 2)
            nc.gpsimd.tensor_tensor(v_lo[:], v_raw[:], v_hi[:].bitcast(F32), ALU.subtract).then_inc(v_split, 1)
            pool.wait_ge(w_loaded, 16)
            nc.gpsimd.tensor_copy(w_hi[:], w_raw[:]).then_inc(pool_own, 1)
            pool.wait_ge(pool_own, 3)
            nc.gpsimd.tensor_tensor(w_lo[:], w_raw[:], w_hi[:].bitcast(F32), ALU.subtract).then_inc(w_split, 1)

        @block.scalar
        def _(act):
            own = Chain(act, act_own)
            nc.scalar.preload_act_table_set(EXP_LN_SET)
            act.wait_ge(c_ready, 2)
            for c in range(NCH):
                act.wait_ge(x_loaded[c % 2], 16 * (c // 2 + 1))
                if c >= 2:
                    act.wait_ge(xT_ready, c - 1)
                own.link(nc.scalar.activation(x_n[c % 2][:], x_in[c % 2][:], ACT.Square, accum_out=stat[:, c, 0:1]))
                own.link(nc.scalar.activation(stat[:, c, 0:1], stat[:, c, 0:1], ACT.Ln, scale=1.0 / D, bias=cst[:, 0:1]))
                nc.scalar.activation(stat[:, c, 1:2], stat[:, c, 0:1], ACT.Exp, scale=-0.5).then_inc(rstd_ready, 1)
            act.wait_ge(par_in, 16 * N_PAR)
            own.link(nc.scalar.activation(a_neg[DT:DT + 16, :], a_neg[DT:DT + 16, :], ACT.Exp))
            nc.scalar.mul(a_neg[DT:DT + 16, :], a_neg[DT:DT + 16, :], -1.0).then_inc(aneg_ready, 1)
            act.wait_ge(lbarg_ready, 1)
            nc.scalar.activation(lb[:, 1, :], lb[:, 0, :], ACT.Exp).then_inc(lbexp_ready, 1)
            act.wait_ge(oml_ready, 1)
            nc.scalar.activation(lb[:, 4, :], lb[:, 3, :], ACT.Ln).then_inc(lbexp_ready, 1)
            for q in range(N_CHAIN):
                b = q % 2
                view = ab[b][DT:DT + 16, :] if q == 0 else ab[b][:]
                one = cst[DT:DT + 16, 1:2] if q == 0 else cst[:, 1:2]
                act.wait_ge(abs_ready, q + 1)
                own.link(nc.scalar.activation(view, view, ACT.Exp))
                nc.scalar.activation(view, view, ACT.Ln, bias=one).then_inc(log1p_ready, 1)
                if 1 <= q <= HF_T:
                    act.wait_ge(karg_ready, q)
                    act.wait_ge(keybias_ready, 1)
                    if q >= 3:
                        act.wait_ge(keys_stored[b], 16 * ((q - 1) // 2))
                    nc.scalar.activation(keys[b][:], keys[b][:], ACT.Exp, bias=lb[:, 5, q - 1:q]).then_inc(keys_ready, 1)

        @block.vector
        def _(dve):
            own = Chain(dve, dve_own)
            nc.vector.memset(cst[:, 0:1], EPS).then_inc(c_ready, 1)
            nc.vector.memset(cst[:, 1:2], 1.0).then_inc(c_ready, 1)

            def normalise(c):
                dve.wait_ge(rstd_ready, c + 1)
                nc.vector.tensor_scalar(x_n[c % 2][:], x_in[c % 2][:], stat[:, c, 1:2], None, ALU.mult).then_inc(xn_ready, 1)

            def split(c):
                dve.wait_ge(xT_ready, c + 1)
                own.link(nc.vector.tensor_tensor(h_f[:], tr[:].rearrange("p (k t) -> p k t", t=CH),
                                                 norm_w[:].unsqueeze(2).to_broadcast([P, KT, CH]), ALU.mult))
                own.link(nc.vector.tensor_copy(h_hi[:, :, c * CH:(c + 1) * CH], h_f[:]))
                nc.vector.tensor_tensor(h_lo[:, :, c * CH:(c + 1) * CH], h_f[:],
                                        h_hi[:, :, c * CH:(c + 1) * CH].bitcast(F32), ALU.subtract).then_inc(h_ready, 1)

            normalise(0)
            dve.wait_ge(par_in, 16 * N_PAR)
            for c in range(NCH):
                if c + 1 < NCH:
                    normalise(c + 1)
                split(c)
            own.link(nc.vector.tensor_tensor(lb[:, 0, :], lb_in[:], lb_in[:], ALU.subtract))
            nc.vector.tensor_copy(lb[:, 0, :], lb[:, 0, :]).then_inc(lbarg_ready, 1)
            dve.wait_ge(lbexp_ready, 1)
            own.link(nc.vector.reciprocal(lb[:, 2, :], lb[:, 1, :]))
            own.link(nc.vector.tensor_tensor(lb[:, 1, :], lb[:, 1, :], lb[:, 2, :], ALU.mult))
            own.link(nc.vector.tensor_tensor(lb[:, 2, :], lb[:, 1, :], lb[:, 1, :], ALU.subtract))
            nc.vector.tensor_scalar(lb[:, 3, :], lb[:, 2, :], -1.0, 1.0, ALU.mult, ALU.add).then_inc(oml_ready, 1)
            dve.wait_ge(lbexp_ready, 2)
            nc.vector.tensor_scalar_add(lb[:, 5, :], lb[:, 4, :], math.log(HG_DIM ** -0.5)).then_inc(keybias_ready, 1)
            dve.wait_ge(seg_ready, 1)
            dve.wait_ge(aneg_ready, 1)

            def to_abs(q):
                b = q % 2
                dve.wait_ge(mm_done, q + 1)
                if q >= 2:
                    dve.wait_ge(cum_ready, q - 1)
                if q == 0:
                    own.link(nc.vector.tensor_copy(glow[:], acc[0][0:GLA_RANK, :]))
                    r = slice(DT, DT + 16)
                    nc.vector.tensor_scalar(xs[b][r, :], acc[0][r, :], dt_bias[r, :], None, ALU.add).then_inc(acc_free, 1)
                    dve.wait_ge(acc_free, 1)
                else:
                    r = slice(0, P)
                    if q <= HF_T:
                        nc.vector.tensor_copy(xs[b][:], acc[q % 3][:]).then_inc(acc_free, 1)
                    else:
                        nc.vector.tensor_scalar(xs[b][:], acc[q % 3][:], gk_bias[:, q - HF_T - 1:q - HF_T], None,
                                                ALU.add).then_inc(acc_free, 1)
                    dve.wait_ge(acc_free, q + 1)
                nc.vector.scalar_tensor_tensor(ab[b][r, :], xs[b][r, :], -1.0, xs[b][r, :], ALU.mult, ALU.min).then_inc(abs_ready, 1)

            to_abs(0)
            for q in range(N_CHAIN):
                b = q % 2
                if q + 1 < N_CHAIN:
                    to_abs(q + 1)
                dve.wait_ge(log1p_ready, q + 1)
                if q >= 2:
                    dve.wait_ge(cum_stored[b], 16 * (q // 2))
                if q == 2:
                    dve.wait_ge(dt_stored, 16)
                if q == 0:
                    r = slice(DT, DT + 16)
                    own.link(nc.vector.scalar_tensor_tensor(ld[b][r, :], xs[b][r, :], 0.0, ab[b][r, :], ALU.max, ALU.add))
                    own.link(nc.vector.tensor_scalar(xs[b][r, :], ld[b][r, :], a_neg[r, :], None, ALU.mult))
                    nc.vector.tensor_tensor_scan(cum[b][r, :], seg0[r, :], xs[b][r, :], 0.0, ALU.mult, ALU.add).then_inc(cum_ready, 1)
                    continue
                own.link(nc.vector.scalar_tensor_tensor(ld[b][:], xs[b][:], 0.0, ab[b][:], ALU.min, ALU.subtract))
                if q <= HF_T:
                    if q >= 3:
                        dve.wait_ge(keys_stored[b], 16 * ((q - 1) // 2))
                    nc.vector.tensor_tensor(keys[b][:], ld[b][:], xs[b][:], ALU.subtract).then_inc(karg_ready, 1)
                    own.link(nc.vector.tensor_scalar(ld[b][:], ld[b][:], lb[:, 4, q - 1:q], None, ALU.add))
                else:
                    own.link(nc.vector.tensor_scalar(ld[b][:], ld[b][:], 1.0 / GLA_TEMP, None, ALU.mult))
                nc.vector.tensor_tensor_scan(cum[b][:], seg0[:], ld[b][:], 0.0, ALU.mult, ALU.add).then_inc(cum_ready, 1)

        @block.tensor
        def _(pe):
            pe.wait_ge(ident_ready, 1)
            for c in range(NCH):
                pe.wait_ge(xn_ready, c + 1)
                if c >= 1:
                    pe.wait_ge(h_ready, c)
                for k in range(KT):
                    ins = nc.tensor.transpose(tr[:, k * P:(k + 1) * P], x_n[c % 2][:, k * P:(k + 1) * P], ident[:])
                ins.then_inc(xT_ready, 1)
            pe.wait_ge(h_ready, NCH)

            def tile(q, hi, lo):
                for k in range(KT):
                    for w, h in ((hi, h_hi), (hi, h_lo), (lo, h_hi)):
                        for half in range(2):
                            hs = slice(half * 512, half * 512 + 512)
                            ins = nc.tensor.matmul(acc[q % 3][:, hs], w[:, k, :], h[:, k, hs],
                                                   start=k == 0 and w is hi and h is h_hi,
                                                   stop=k == KT - 1 and w is lo, skip_group_check=True)
                ins.then_inc(mm_done, 1)

            pe.wait_ge(v_split, 1)
            tile(0, v_hi, v_lo)
            pe.wait_ge(w_split, 1)
            for q in range(1, 1 + HF_T):
                if q >= 3:
                    pe.wait_ge(acc_free, q - 2)
                ws = slice((q - 1) * P, q * P)
                tile(q, w_hi[:, :, ws], w_lo[:, :, ws])
            for g in range(GK_T):
                q = 1 + HF_T + g
                pe.wait_ge(acc_free, q - 2)
                for half in range(2):
                    hs = slice(half * 512, half * 512 + 512)
                    ins = nc.tensor.matmul(acc[q % 3][:, hs], gk_up[:, g * P:(g + 1) * P], glow[:, hs], start=True, stop=True)
                ins.then_inc(mm_done, 1)


def project(nc, io, dr, h_hi, h_lo):
    HEAD = [(COL["gq"], "copy", dr["qk"][0:PAIR]), (COL["gk"], "key", dr["qk"][PAIR:2 * PAIR])]
    LOOPS = [(COL["gr"], 4, "silu", dr["silu_a"]),
             (COL["hg"], 6, "silu", dr["silu_b"]),
             (COL["gv"], 2, "tokens", dr["v"][:, 0:512]),
             (COL["hi"], 2, "tokens", dr["v"][:, 512:1024]),
             (COL["sxbc"], 8, "conv", dr["xbc"]),
             (COL["gates"], 12, "copy", dr["gates"])]
    PAD = SSM_CONV - 1
    TAPS = SSM_CONV + 1
    N_STEPS = len(HEAD) + sum(n for _, n, _, _ in LOOPS)
    with ExitStack() as ctx:
        sb = lambda name, shape, dt=F32: ctx.enter_context(nc.sbuf_tensor(name, shape, dt))
        sem = semaphores(nc, ctx)
        w_raw = [sb(f"w_raw{b}", [P, KT, PAIR]) for b in range(2)]
        w_hi = [sb(f"w_hi{b}", [P, KT, PAIR], F32R) for b in range(2)]
        w_lo = [sb(f"w_lo{b}", [P, KT, PAIR], F32R) for b in range(2)]
        out = [sb(f"out{b}", [P, 2 * T]) for b in range(2)]
        u = [sb(f"u{b}", [P, 2, T + PAD]) for b in range(2)]
        tap = sb("tap", [P, 2, T])
        taps = [sb(f"taps{b}", [P, 2, TAPS]) for b in range(2)]
        ps = [ctx.enter_context(nc.psum_tensor(f"ps{b}", [P, 2 * T], F32)) for b in range(2)]
        w_loaded = [sem(f"w_loaded{b}") for b in range(2)]
        taps_loaded = [sem(f"taps_loaded{b}") for b in range(2)]
        hi_ready = sem("hi_ready")
        split_ready = sem("split_ready")
        mm_done = sem("mm_done")
        out_ready = sem("out_ready")
        stored = [sem(f"stored{b}") for b in range(2)]
        pad_ready = sem("pad_ready")
        u_ready = sem("u_ready")
        conv_ready = sem("conv_ready")
        passed = sem("passed")
        dve_own = sem("dve_own")
        block = ctx.enter_context(nc.Block())

        def steps(eng, body):
            for t, (col, kind, dram) in enumerate(HEAD):
                body(t, t % 2, 0, t // 2, col, kind, dram)
            t0 = len(HEAD)
            for col, n, kind, dram in LOOPS:
                with eng.Fori(0, n // 2) as i:
                    for b in range(2):
                        body(2 * i + (t0 + b), b, 2 * i + b, i + t0 // 2, col, kind, dram)
                t0 += n

        def early(t, n):
            return isinstance(t, int) and t < n

        @block.sync
        def _(sp):
            def body(t, b, j, turn, col, kind, dram):
                if not early(t, 2):
                    sp.wait_ge(split_ready, t - 1)
                sp.dma_start(w_raw[b][:], io["w_in"][:, bass.ds(j * PAIR + col, PAIR)]
                             .rearrange("(k p) n -> p k n", p=P)).then_inc(w_loaded[b], 16)
                if kind == "conv":
                    sp.wait_ge(out_ready, t - 1)
                    sp.dma_start(taps[b][:], io["taps"][bass.ds(j * PAIR, PAIR), :]
                                 .rearrange("(a p) k -> p a k", p=P)).then_inc(taps_loaded[b], 16)
            steps(sp, body)

        @block.gpsimd
        def _(pool):
            def body(t, b, j, turn, col, kind, dram):
                pool.wait_ge(w_loaded[b], 16 * turn + 16)
                if not early(t, 2):
                    pool.wait_ge(mm_done, t - 1)
                pool.sem_inc(passed, 1)
                nc.gpsimd.tensor_copy(w_hi[b][:], w_raw[b][:]).then_inc(hi_ready, 1)
                pool.wait_ge(hi_ready, t + 1)
                nc.gpsimd.tensor_tensor(w_lo[b][:], w_raw[b][:], w_hi[b][:].bitcast(F32), ALU.subtract).then_inc(split_ready, 1)
            steps(pool, body)

        @block.scalar
        def _(act):
            nc.scalar.preload_act_table(ACT.Silu)
            act.wait_ge(pad_ready, 1)

            def body(t, b, j, turn, col, kind, dram):
                act.wait_ge(mm_done, t + 1)
                if kind == "conv":
                    nc.scalar.copy(u[b][:, :, PAD:PAD + T], ps[b][:].rearrange("p (a t) -> p a t", t=T)).then_inc(u_ready, 1)
                    act.wait_ge(conv_ready, j + 1)
                if not early(t, 2):
                    act.wait_ge(stored[b], 16 * turn)
                if kind == "conv":
                    for a in range(2):
                        ins = nc.scalar.activation(out[b][:, a * T:(a + 1) * T], tap[:, a, :], ACT.Silu,
                                                   bias=taps[b][:, a, SSM_CONV:TAPS])
                elif kind == "silu":
                    ins = nc.scalar.activation(out[b][:], ps[b][:], ACT.Silu)
                else:
                    ins = nc.scalar.activation(out[b][:], ps[b][:], ACT.Copy, scale=GLA_DK ** -0.5 if kind == "key" else 1.0)
                ins.then_inc(out_ready, 1)
                act.wait_ge(out_ready, t + 1)
                if kind == "tokens":
                    act.dma_start(dram[:, bass.ds(j * PAIR, PAIR)].rearrange("(c p) n -> p c n", p=P),
                                  out[b][:].rearrange("p (c n) -> p c n", n=PAIR)).then_inc(stored[b], 16)
                else:
                    act.dma_start(dram[bass.ds(j * PAIR, PAIR), :].rearrange("(a p) t -> p a t", p=P),
                                  out[b][:].rearrange("p (a t) -> p a t", t=T)).then_inc(stored[b], 16)
            steps(act, body)
            for b in range(2):
                act.wait_ge(stored[b], 16 * (N_STEPS // 2))

        @block.vector
        def _(dve):
            own = Chain(dve, dve_own)
            nc.vector.memset(u[0][:, :, 0:PAD], 0.0)
            nc.vector.memset(u[1][:, :, 0:PAD], 0.0).then_inc(pad_ready, 1)
            dve.wait_ge(pad_ready, 1)
            pairs, t0 = [(n, sum(m for _, m, _, _ in LOOPS[:q])) for q, (_, n, kind, _) in enumerate(LOOPS) if kind == "conv"][0]
            t0 += len(HEAD)
            with dve.Fori(0, pairs // 2) as i:
                own.turn(i, 2 * 2 * (SSM_CONV - 1))
                for b in range(2):
                    j = 2 * i + b
                    dve.wait_ge(u_ready, j + 1)
                    dve.wait_ge(taps_loaded[b], 16 * i + 16)
                    dve.wait_ge(out_ready, j + t0)
                    for k in range(SSM_CONV):
                        for a in range(2):
                            if k == 0:
                                ins = nc.vector.tensor_scalar(tap[:, a, :], u[b][:, a, 0:T], taps[b][:, a, 0:1], None, ALU.mult)
                            else:
                                ins = nc.vector.scalar_tensor_tensor(tap[:, a, :], u[b][:, a, k:k + T], taps[b][:, a, k:k + 1],
                                                                     tap[:, a, :], ALU.mult, ALU.add)
                            if k < SSM_CONV - 1:
                                own.link(ins) if a == 1 else ins.then_inc(own.sem, 1)
                                own.n += a == 0
                    ins.then_inc(conv_ready, 1)

        @block.tensor
        def _(pe):
            def body(t, b, j, turn, col, kind, dram):
                pe.wait_ge(split_ready, t + 1)
                if not early(t, 2):
                    if kind == "conv":
                        pe.wait_ge(out_ready, t - 1)
                    else:
                        pe.wait_ge(out_ready, t - 1)
                hi, lo = w_hi[b], w_lo[b]
                parts = ((hi, h_hi), (hi, h_lo), (lo, h_hi))
                if kind == "tokens":
                    for c in range(NCH):
                        for k in range(KT):
                            for n, (w, h) in enumerate(parts):
                                ins = nc.tensor.matmul(ps[b][:, c * PAIR:(c + 1) * PAIR], h[:, k, c * CH:(c + 1) * CH], w[:, k, :],
                                                       start=k == 0 and n == 0, stop=k == KT - 1 and n == 2)
                else:
                    for a in range(2):
                        for k in range(KT):
                            for n, (w, h) in enumerate(parts):
                                for half in range(2):
                                    ins = nc.tensor.matmul(ps[b][:, a * T + half * 512:a * T + half * 512 + 512],
                                                           w[:, k, a * P:(a + 1) * P], h[:, k, half * 512:half * 512 + 512],
                                                           start=k == 0 and n == 0, stop=k == KT - 1 and n == 2)
                ins.then_inc(mm_done, 1)
            steps(pe, body)


def mixers(nc, io, dr, ident):
    LEVELS = [64 >> n for n in range(7)]
    NL = len(LEVELS)
    NE = NL + 1
    NEV = NL + 2
    CT = 6
    QT = 8
    NH = GLA_HEADS + HG_HEADS
    N_LOADS = 17
    N_PAR = 5
    HALF = P // 2
    GH = SSM_HEADS // SSM_GROUPS

    with ExitStack() as ctx:
        sb = lambda name, shape, dt=F32: ctx.enter_context(nc.sbuf_tensor(name, shape, dt))
        sem = semaphores(nc, ctx)
        pair = lambda name, shape: [sb(f"{name}{b}", shape) for b in range(2)]
        q_in, k_in, b_in = pair("q_in", [P, QT, CH]), pair("k_in", [P, CT, CH]), pair("b_in", [P, CT, CH])
        v_in = pair("v_in", [P, NH, P])
        g_in = pair("g_in", [P, NH, CH])
        z_in, x_in, bc_in = pair("z_in", [P, 8, CH]), pair("xs_in", [P, 8, CH]), pair("bc_in", [P, 8, CH])
        bb_in = pair("bb_in", [P, SSM_HEADS, CH])
        eb_in = pair("eb_in", [P, 8, CH])
        tok_in = pair("tok_in", [P, 2, SSM_HEADS])
        dec = pair("dec", [P, CT * CH])
        ex = pair("ex", [P, CT * CH])
        k_lv = [sb(f"k_lv{n}", [P, CT * CH]) for n in range(NL)]
        q_lv = pair("q_lv", [P, QT * HALF])
        score = sb("score", [P, NH * CH])
        eb6 = sb("eb6", [P, CT, CH])
        q_dec = sb("q_dec", [P, QT, CH])
        k_dec = sb("k_dec", [P, CT, CH])
        kT = sb("kT", [P, CT, P])
        state = sb("state", [P, CT, P])
        sq = sb("sq", [P, 8 * CH])
        rs = sb("rs", [P, NH * CH])
        gw = sb("gw", [P, NH, CH])
        y_out = sb("y_out", [P, 2 * NH, CH])
        wmat = sb("wmat", [P, SSM_HEADS, CH])
        cbm = sb("cbm", [P, SSM_GROUPS, CH])
        xdt = sb("xdt", [P, SSM_HEADS, SSM_HD])
        xw = sb("xw", [P, SSM_HEADS, SSM_HD])
        bT = sb("bT", [P, SSM_GROUPS, P])
        hst = sb("hst", [P, SSM_HEADS, SSM_HD])
        yt = sb("yt", [P, 8, CH])
        xd = sb("xd", [P, 8, CH])
        wd = sb("wd", [P, 3, SSM_HEADS])
        rs2 = sb("rs2", [P, SSM_GROUPS, CH])
        mask_f = sb("mask_f", [P, HALF])
        mask = [sb(f"mask{n}", [P, NH * HALF], U8) for n in range(NL)]
        mask_d = sb("mask_d", [P, 4 * CH], U8)
        tri = sb("tri", [P, SSM_GROUPS, CH])
        mean_a = sb("mean_a", [P, P])
        mean_b = sb("mean_b", [P, P])
        eps = sb("eps", [P, 1])
        nw = sb("nw", [P, NH])
        nw_s = sb("nw_s", [P, 8])
        d_col = sb("d_col", [P, 8])
        psum = ctx.enter_context(nc.psum_tensor("psum", [P, 8, 512], F32))
        two = lambda n: psum[:, n:n + 2, :].rearrange("p a b -> p (a b)")
        sc_ps = [psum[:, 0, :], psum[:, 1, :]]
        inter_ps = two(0)
        mid_ps = two(2)
        o_ps = two(4)
        cb_ps, bT_ps, intra_ps = psum[:, 6, :], psum[:, 7, :], two(6)

        loaded = [sem(f"loaded{b}") for b in range(2)]
        par_in = sem("par_in")
        mask_sem = sem("mask_sem")
        mask_ready = sem("mask_ready")
        q_zeroed = sem("q_zeroed")
        zeroed = sem("zeroed")
        const_ready = sem("const_ready")
        d_ready = sem("d_ready")
        e_ready = sem("e_ready")
        qk_ready = sem("qk_ready")
        sc_ready = sem("sc_ready")
        score_ready = sem("score_ready")
        eb6_ready = sem("eb6_ready")
        state_ready = sem("state_ready")
        kT_ps_ready = sem("kT_ps_ready")
        kT_ready = sem("kT_ready")
        o_ready = sem("o_ready")
        upd_ready = sem("upd_ready")
        sq_ready = sem("sq_ready")
        ms_ready = sem("ms_ready")
        ms_read = sem("ms_read")
        rs_ready = sem("rs_ready")
        gw_ready = sem("gw_ready")
        o_used = sem("o_used")
        ya_ready = sem("ya_ready")
        yb_ready = sem("yb_ready")
        ya_stored = sem("ya_stored")
        yb_stored = sem("yb_stored")
        seg_ready = sem("seg_ready")
        wexp_ready = sem("wexp_ready")
        cb_ready = sem("cb_ready")
        cbm_ready = sem("cbm_ready")
        w_ready = sem("w_ready")
        xT_ready = sem("xT_ready")
        xdt_ready = sem("xdt_ready")
        bT_ps_ready = sem("bT_ps_ready")
        bT_ready = sem("bT_ready")
        wdarg_ready = sem("wdarg_ready")
        small_ready = sem("small_ready")
        xw_ready = sem("xw_ready")
        xd_ready = sem("xd_ready")
        intra_ready = sem("intra_ready")
        inter_ready = sem("inter_ready")
        inter_used = sem("inter_used")
        intra_used = sem("intra_used")
        yt_ready = sem("yt_ready")
        sq2_ready = sem("sq2_ready")
        ms2_ready = sem("ms2_ready")
        ms2_read = sem("ms2_read")
        rs2_ready = sem("rs2_ready")
        hupd_ready = sem("hupd_ready")
        hst_ready = sem("hst_ready")
        passed = sem("passed")
        dve_own = sem("dve_own")
        act_own = sem("act_own")
        block = ctx.enter_context(nc.Block())

        E0, QK0 = 2, 2

        def chunks(eng, body):
            with eng.Fori(0, NCH // 2) as i:
                for b in range(2):
                    body(2 * i + b, b, i)

        @block.sync
        def _(sp):
            sp.dma_start(nw[:, 0:4], io["gla_norm_w"].rearrange("(k p) -> p k", p=P)).then_inc(par_in, 16)
            sp.dma_start(nw[:, 4:8], io["hgrn_norm_w"].rearrange("(k p) -> p k", p=P)).then_inc(par_in, 16)
            sp.dma_start(nw_s[:], io["ssm_norm_w"].rearrange("(k p) -> p k", p=P)).then_inc(par_in, 16)
            for a in range(2):
                sp.dma_start(d_col[a * HALF:(a + 1) * HALF, :], io["ssm_d"][a::2].unsqueeze(0).to_broadcast([HALF, 8]))\
                    .then_inc(par_in, 16)

            def load(c, b):
                t = bass.ds(c * CH, CH)
                tiles = lambda ap: ap[:, t].rearrange("(k p) t -> p k t", p=P)
                put = lambda dst, src: sp.dma_start(dst, src).then_inc(loaded[b], 16)
                put(b_in[b][:], tiles(dr["cum"]))
                gq = tiles(dr["qk"][0:256])
                for a in range(2):
                    r = slice(a * HALF, (a + 1) * HALF)
                    put(q_in[b][r, 2 * a:2 * a + 2, :], gq[r])
                put(q_in[b][:, 4:8, :], tiles(dr["silu_a"][512:1024]))
                put(k_in[b][:, 0:2, :], tiles(dr["qk"][256:512]))
                put(k_in[b][:, 2:6, :], tiles(dr["k_hg"]))
                put(bb_in[b][:], dr["b_ssm"][:, t].unsqueeze(0).to_broadcast([P, SSM_HEADS, CH]))
                put(tok_in[b][:, 0, :], dr["b_ssm"][:, t].rearrange("h t -> t h"))
                put(tok_in[b][:, 1, :], dr["dt"][:, t].rearrange("h t -> t h"))
                put(bc_in[b][:], tiles(dr["xbc"][1024:2048]))
                put(x_in[b][:], tiles(dr["xbc"][0:1024]))
                put(v_in[b][:], dr["v"][t, :].rearrange("t (h e) -> t h e", e=P))
                for a in range(2):
                    put(eb_in[b][a * HALF:(a + 1) * HALF, :, :], dr["b_ssm"][a::2, t].unsqueeze(0).to_broadcast([HALF, 8, CH]))
                put(g_in[b][:, 0:4, :], tiles(dr["silu_a"][0:512]))
                put(g_in[b][:, 4:8, :], tiles(dr["silu_b"][0:512]))
                put(z_in[b][:], tiles(dr["silu_b"][512:1536]))

            def store(c):
                t = bass.ds(c * CH, CH)
                sp.wait_ge(ya_ready, c + 1)
                sp.dma_start(dr["y"][0:1024, t].rearrange("(k p) t -> p k t", p=P), y_out[:, 0:8, :]).then_inc(ya_stored, 16)
                sp.wait_ge(yb_ready, c + 1)
                sp.dma_start(dr["y"][1024:2048, t].rearrange("(k p) t -> p k t", p=P), y_out[:, 8:16, :]).then_inc(yb_stored, 16)

            sp.wait_ge(q_zeroed, 2)
            load(0, 0)
            load(1, 1)
            with sp.Fori(0, NCH // 2 - 1) as i:
                for b in range(2):
                    store(2 * i + b)
                    load(2 * i + (b + 2), b)
            store(NCH - 2)
            store(NCH - 1)
            sp.wait_ge(ya_stored, 16 * NCH + 16)
            sp.wait_ge(yb_stored, 16 * NCH + 16)

        @block.gpsimd
        def _(pool):
            for b in range(2):
                nc.gpsimd.memset(q_in[b][:, 0:4, :], 0.0).then_inc(q_zeroed, 1)
            n = 0
            for lv, h in enumerate(LEVELS):
                nb = CH // (2 * h)
                if lv:
                    pool.wait_ge(mask_ready, lv)
                nc.gpsimd.memset(mask_f[:], 1.0).then_inc(mask_sem, 1)
                n += 1
                pool.wait_ge(mask_sem, n)
                view = mask_f[:].rearrange("p (n h) -> p n h", h=h)
                nc.gpsimd.affine_select(out=view, in_=view, compare_op=ALU.is_ge, fill=0.0, base=0,
                                        pattern=[[-2 * h, nb], [0, h]], channel_multiplier=1).then_inc(mask_sem, 1)
                n += 1
                pool.wait_ge(mask_sem, n)
                nc.gpsimd.affine_select(out=view, in_=view, compare_op=ALU.is_ge, fill=0.0, base=h - 1,
                                        pattern=[[2 * h, nb], [0, h]], channel_multiplier=-1).then_inc(mask_sem, 1)
                n += 1
            nc.gpsimd.memset(tri[:], 1.0).then_inc(zeroed, 1)
            pool.wait_ge(zeroed, 1)
            nc.gpsimd.affine_select(out=tri[:], in_=tri[:], compare_op=ALU.is_ge, fill=0.0, base=0,
                                    pattern=[[0, SSM_GROUPS], [1, CH]], channel_multiplier=-1).then_inc(const_ready, 1)
            nc.gpsimd.memset(mean_a[:], 1.0 / GLA_DV).then_inc(const_ready, 1)
            nc.gpsimd.memset(mean_b[:], 1.0 / 256).then_inc(const_ready, 1)
            for n in range(NL):
                nc.gpsimd.memset(k_lv[n][:], 0.0).then_inc(const_ready, 1)
            pool.wait_ge(par_in, 16 * N_PAR)

            def body(c, b, turn):
                pool.wait_ge(loaded[b], 16 * N_LOADS * turn + 16 * N_LOADS)
                for lv, h in enumerate(LEVELS):
                    pool.wait_ge(e_ready, NE * c + (lv - 1 + E0))
                    view = b_in[b][:].rearrange("p a (n w) -> p (a n) w", w=2 * h)
                    at_m = view[:, :, h - 1:h].to_broadcast([P, CT * CH // (2 * h), 2 * h])
                    nc.gpsimd.tensor_tensor(dec[lv % 2][:].rearrange("p (n w) -> p n w", w=2 * h), view, at_m,
                                            ALU.subtract).then_inc(d_ready, 1)
                pool.wait_ge(e_ready, NE * c + (NL - 1 + E0))
                nc.gpsimd.tensor_tensor(dec[NL % 2][:].rearrange("p (a w) -> p a w", w=CH),
                                        b_in[b][:, :, CH - 1:CH].to_broadcast([P, CT, CH]), b_in[b][:],
                                        ALU.subtract).then_inc(d_ready, 1)
                pool.wait_ge(wexp_ready, c + 1)
                pool.wait_ge(cbm_ready, c + 1)
                w4 = wmat[:].rearrange("p (g r) t -> p g r t", r=GH)
                nc.gpsimd.tensor_tensor(w4, w4, cbm[:].unsqueeze(2).to_broadcast([P, SSM_GROUPS, GH, CH]),
                                        ALU.mult).then_inc(w_ready, 1)
                pool.wait_ge(small_ready, c + 1)
                pool.wait_ge(xdt_ready, c + 1)
                nc.gpsimd.tensor_tensor(xw[:], xdt[:], wd[:, 1, :].unsqueeze(2).to_broadcast([P, SSM_HEADS, SSM_HD]),
                                        ALU.mult).then_inc(xw_ready, 1)
                nc.gpsimd.tensor_tensor(xd[:], x_in[b][:], d_col[:].unsqueeze(2).to_broadcast([P, 8, CH]),
                                        ALU.mult).then_inc(xd_ready, 1)
                nc.gpsimd.tensor_tensor(gw[:], g_in[b][:], nw[:].unsqueeze(2).to_broadcast([P, NH, CH]),
                                        ALU.mult).then_inc(gw_ready, 1)
            chunks(pool, body)

        @block.scalar
        def _(act):
            own = Chain(act, act_own)
            nc.scalar.preload_act_table_set(EXP_LN_SET)
            act.sem_inc(e_ready, E0)
            act.wait_ge(zeroed, 1)

            def body(c, b, turn):
                
                def relative(lv):
                    h = LEVELS[lv]
                    act.wait_ge(d_ready, NE * c + (lv + 1))
                    act.wait_ge(qk_ready, NE * c + (lv - 1 + QK0))
                    d = dec[lv % 2][:].rearrange("p (n w) -> p n w", w=2 * h)
                    e = ex[lv % 2][:].rearrange("p (n w) -> p n w", w=2 * h)
                    nc.scalar.activation(e[:, :, 0:h], d[:, :, 0:h], ACT.Exp, scale=-1.0)
                    nc.scalar.activation(e[:, :, h:2 * h], d[:, :, h:2 * h], ACT.Exp).then_inc(e_ready, 1)

                relative(0)
                relative(1)
                act.wait_ge(seg_ready, c + 1)
                nc.scalar.activation(wmat[:], wmat[:], ACT.Exp).then_inc(wexp_ready, 1)
                relative(2)
                act.wait_ge(wdarg_ready, c + 1)
                nc.scalar.activation(wd[:, 1, :], wd[:, 0, :], ACT.Exp)
                nc.scalar.activation(wd[:, 2, :], bb_in[b][:, :, CH - 1], ACT.Exp)
                nc.scalar.activation(eb_in[b][:], eb_in[b][:], ACT.Exp).then_inc(small_ready, 1)
                relative(3)
                act.wait_ge(bT_ps_ready, c + 1)
                nc.scalar.copy(bT[:].rearrange("p g n -> p (g n)"), bT_ps).then_inc(bT_ready, 1)
                for lv in range(4, NL):
                    relative(lv)
                act.wait_ge(d_ready, NE * c + NE)
                act.wait_ge(qk_ready, NE * c + (NL - 1 + QK0))
                nc.scalar.activation(ex[NL % 2][:], dec[NL % 2][:], ACT.Exp).then_inc(e_ready, 1)
                act.wait_ge(state_ready, c + 1)
                nc.scalar.activation(eb6[:], b_in[b][:], ACT.Exp).then_inc(eb6_ready, 1)
                act.wait_ge(kT_ps_ready, c + 1)
                nc.scalar.copy(kT[:].rearrange("p a n -> p (a n)"), mid_ps[:, 0:CT * P]).then_inc(kT_ready, 1)
                act.wait_ge(o_ready, c + 1)
                nc.scalar.activation(sq[:], o_ps, ACT.Square).then_inc(sq_ready, 1)
                act.wait_ge(ms_ready, c + 1)
                nc.scalar.activation(rs[:], mid_ps, ACT.Ln, bias=eps[:]).then_inc(ms_read, 1)
                act.wait_ge(ms_read, c + 1)
                nc.scalar.activation(rs[:], rs[:], ACT.Exp, scale=-0.5).then_inc(rs_ready, 1)
                act.wait_ge(yt_ready, c + 1)
                nc.scalar.activation(sq[:], yt[:].rearrange("p k t -> p (k t)"), ACT.Square).then_inc(sq2_ready, 1)
                act.wait_ge(ms2_ready, c + 1)
                nc.scalar.activation(rs2[:].rearrange("p g t -> p (g t)"), mid_ps[:, 0:512], ACT.Ln, bias=eps[:]).then_inc(ms2_read, 1)
                act.wait_ge(ms2_read, c + 2)
                nc.scalar.activation(rs2[:], rs2[:], ACT.Exp, scale=-0.5).then_inc(rs2_ready, 1)
            chunks(act, body)

        @block.vector
        def _(dve):
            own = Chain(dve, dve_own)
            for s, n in ((qk_ready, QK0), (state_ready, 1), (intra_used, 1), (inter_used, 1), (hst_ready, 1),
                         (ms2_read, 1), (ya_stored, 16), (yb_stored, 16)):
                dve.sem_inc(s, n)
            own.link(nc.vector.memset(eps[:], EPS))
            own.link(nc.vector.memset(state[:], 0.0))
            own.link(nc.vector.memset(hst[:], 0.0))
            own.link(nc.vector.memset(score[:], 0.0))
            for lv in range(NL):
                dve.wait_ge(mask_sem, 3 * lv + 3)
                nc.vector.tensor_copy(mask[lv][:].rearrange("p (a h) -> p a h", h=HALF),
                                      mask_f[:].unsqueeze(1).to_broadcast([P, NH, HALF])).then_inc(mask_ready, 1)
            dve.wait_ge(mask_ready, NL)
            own.link(nc.vector.tensor_copy(mask_d[:].rearrange("p (a h) -> p a h", h=CH),
                                           ident[:].unsqueeze(1).to_broadcast([P, 4, CH])))
            dve.wait_ge(const_ready, 3 + NL)
            START = own.n

            def body(c, b, turn):
                own.turn(c, LINKS)
                own.n = START
                dve.wait_ge(loaded[b], 16 * N_LOADS * turn + 16 * N_LOADS)
                for h in range(SSM_HEADS):
                    ins = nc.vector.tensor_scalar(wmat[:, h, :], bb_in[b][:, h, :], tok_in[b][:, 0, h:h + 1], 0.0,
                                                  ALU.subtract, ALU.min)
                ins.then_inc(seg_ready, 1)
                nc.vector.tensor_tensor(wd[:, 0, :], bb_in[b][:, :, CH - 1], tok_in[b][:, 0, :], ALU.subtract).then_inc(wdarg_ready, 1)
                dve.wait_ge(cb_ready, c + 1)
                nc.vector.tensor_tensor(cbm[:], cb_ps.rearrange("p (g t) -> p g t", t=CH), tri[:], ALU.mult).then_inc(cbm_ready, 1)
                dve.wait_ge(xT_ready, c + 1)
                nc.vector.tensor_tensor(xdt[:], mid_ps.rearrange("p (h e) -> p h e", e=SSM_HD),
                                        tok_in[b][:, 1, :].unsqueeze(2).to_broadcast([P, SSM_HEADS, SSM_HD]),
                                        ALU.mult).then_inc(xdt_ready, 1)

                def factors(lv):
                    h = LEVELS[lv]
                    dve.wait_ge(e_ready, NE * c + (lv + 1 + E0))
                    v = lambda x: x.rearrange("p (n w) -> p n w", w=2 * h)
                    k6 = v(k_in[b][:].rearrange("p a t -> p (a t)"))
                    q8 = q_in[b][:].rearrange("p a (n w) -> p a n w", w=2 * h)
                    e6 = ex[lv % 2][:].rearrange("p (a n w) -> p a n w", a=CT, w=2 * h)
                    ql = q_lv[lv % 2][:].rearrange("p (a n h) -> p a n h", a=QT, h=h)
                    nc.vector.tensor_tensor(v(k_lv[lv][:])[:, :, 0:h], k6[:, :, 0:h], v(ex[lv % 2][:])[:, :, 0:h], ALU.mult)
                    nc.vector.tensor_tensor(ql[:, 0:2], q8[:, 0:2, :, h:2 * h], e6[:, 0:2, :, h:2 * h], ALU.mult)
                    nc.vector.tensor_tensor(ql[:, 2:8], q8[:, 2:8, :, h:2 * h], e6[:, :, :, h:2 * h], ALU.mult).then_inc(qk_ready, 1)

                def scores_in(lv):
                    h = LEVELS[lv]
                    dve.wait_ge(sc_ready, NEV * c + (lv + 1))
                    if lv:
                        dve.wait_ge(score_ready, NEV * c + lv)
                    dve.sem_inc(passed, 1)
                    v = lambda x: x.rearrange("p (n h) -> p n h", h=h)
                    nc.vector.copy_predicated(score[:].rearrange("p (n w) -> p n w", w=2 * h)[:, :, h:2 * h],
                                              v(mask[lv][:]), v(sc_ps[lv % 2])).then_inc(score_ready, 1)

                factors(0)
                for lv in range(1, NL):
                    factors(lv)
                    scores_in(lv - 1)
                dve.wait_ge(e_ready, NE * c + (NE + E0))
                nc.vector.tensor_tensor(k_dec[:], k_in[b][:], ex[NL % 2][:].rearrange("p (a t) -> p a t", t=CH), ALU.mult)\
                    .then_inc(qk_ready, 1)
                scores_in(NL - 1)
                dve.wait_ge(eb6_ready, c + 1)
                nc.vector.tensor_tensor(q_dec[:, 0:2, :], q_in[b][:, 0:2, :], eb6[:, 0:2, :], ALU.mult)
                own.link(nc.vector.tensor_tensor(q_dec[:, 2:8, :], q_in[b][:, 2:8, :], eb6[:], ALU.mult))
                for a in range(2):
                    dve.wait_ge(sc_ready, NEV * c + (NL + 1 + a))
                    dve.wait_ge(score_ready, NEV * c + (NL + a))
                    dve.sem_inc(passed, 1)
                    nc.vector.copy_predicated(score[:, a * 512:(a + 1) * 512], mask_d[:], sc_ps[a]).then_inc(score_ready, 1)
                dve.wait_ge(upd_ready, c + 1)
                own.link(nc.vector.tensor_tensor(state[:], state[:], eb6[:, :, CH - 1:CH].to_broadcast([P, CT, P]), ALU.mult))
                nc.vector.tensor_tensor(state[:], state[:], mid_ps[:, 0:CT * P].rearrange("p (a e) -> p a e", e=P), ALU.add)\
                    .then_inc(state_ready, 1)
                dve.wait_ge(small_ready, c + 1)
                dve.wait_ge(inter_ready, c + 1)
                nc.vector.tensor_tensor(yt[:], inter_ps.rearrange("p (k t) -> p k t", t=CH), eb_in[b][:], ALU.mult).then_inc(inter_used, 1)
                dve.wait_ge(inter_used, c + 2)
                nc.vector.tensor_tensor(yt[:], intra_ps.rearrange("p (k t) -> p k t", t=CH), yt[:], ALU.add).then_inc(intra_used, 1)
                dve.wait_ge(intra_used, c + 2)
                dve.wait_ge(xd_ready, c + 1)
                own.link(nc.vector.tensor_tensor(yt[:], yt[:], xd[:], ALU.add))
                nc.vector.tensor_tensor(yt[:], yt[:], z_in[b][:], ALU.mult).then_inc(yt_ready, 1)
                dve.wait_ge(yt_ready, c + 1)
                dve.wait_ge(rs_ready, c + 1)
                dve.wait_ge(ya_stored, 16 * c + 16)
                ya = y_out[:, 0:8, :]
                nc.vector.tensor_tensor(ya, o_ps.rearrange("p (k t) -> p k t", t=CH), rs[:].rearrange("p (k t) -> p k t", t=CH),
                                        ALU.mult).then_inc(o_used, 1)
                dve.wait_ge(o_used, c + 1)
                dve.wait_ge(gw_ready, c + 1)
                nc.vector.tensor_tensor(ya, ya, gw[:], ALU.mult).then_inc(ya_ready, 1)
                dve.wait_ge(hupd_ready, c + 1)
                own.link(nc.vector.tensor_tensor(hst[:], hst[:], wd[:, 2, :].unsqueeze(2).to_broadcast([P, SSM_HEADS, SSM_HD]),
                                                 ALU.mult))
                nc.vector.tensor_tensor(hst[:], hst[:], o_ps.rearrange("p (h e) -> p h e", e=SSM_HD), ALU.add).then_inc(hst_ready, 1)
                dve.wait_ge(rs2_ready, c + 1)
                dve.wait_ge(yb_stored, 16 * c + 16)
                yb = y_out[:, 8:16, :]
                own.link(nc.vector.tensor_tensor(yb.rearrange("p (g a) t -> p g a t", a=2), yt[:].rearrange("p (g a) t -> p g a t", a=2),
                                                 rs2[:].unsqueeze(2).to_broadcast([P, SSM_GROUPS, 2, CH]), ALU.mult))
                nc.vector.tensor_tensor(yb, yb, nw_s[:].unsqueeze(2).to_broadcast([P, 8, CH]), ALU.mult).then_inc(yb_ready, 1)
                dve.wait_ge(yb_ready, c + 1)
                assert own.n - START == LINKS
            LINKS = 5
            chunks(dve, body)

        @block.tensor
        def _(pe):
            pe.wait_ge(const_ready, 3 + NL)

            def body(c, b, turn):
                pe.wait_ge(loaded[b], 16 * N_LOADS * turn + 16 * N_LOADS)
                pe.wait_ge(intra_used, c + 1)
                for g in range(SSM_GROUPS):
                    ins = nc.tensor.matmul(cb_ps[:, g * CH:(g + 1) * CH], bc_in[b][:, g, :], bc_in[b][:, 4 + g, :], start=True, stop=True)
                ins.then_inc(cb_ready, 1)
                for g in range(SSM_GROUPS):
                    ins = nc.tensor.transpose(bT_ps[:, g * P:(g + 1) * P], bc_in[b][:, g, :], ident[:])
                ins.then_inc(bT_ps_ready, 1)
                pe.wait_ge(ms2_read, c + 1)
                for k in range(8):
                    ins = nc.tensor.transpose(mid_ps[:, k * P:(k + 1) * P], x_in[b][:, k, :], ident[:])
                ins.then_inc(xT_ready, 1)

                def heads():
                    for h in range(GLA_HEADS):
                        yield h, h // 2 + 2 * (h % 2), h // 2, slice(HALF * (h % 2), HALF * (h % 2) + HALF)
                    for h in range(HG_HEADS):
                        yield GLA_HEADS + h, 4 + h, 2 + h, slice(0, P)

                pe.wait_ge(inter_used, c + 1)
                for lv in range(NL):
                    pe.wait_ge(qk_ready, NE * c + (lv + 1 + QK0))
                    if lv >= 2:
                        pe.wait_ge(score_ready, NEV * c + (lv - 1))
                    for h, qa, a, r in heads():
                        ins = nc.tensor.matmul(sc_ps[lv % 2][:, h * HALF:(h + 1) * HALF], k_lv[lv][:, a * CH:(a + 1) * CH],
                                               q_lv[lv % 2][:, qa * HALF:(qa + 1) * HALF], start=True, stop=True)
                    ins.then_inc(sc_ready, 1)
                for half in range(2):
                    pe.wait_ge(score_ready, NEV * c + NL)
                    for h, qa, a, r in heads():
                        if h // 4 == half:
                            ins = nc.tensor.matmul(sc_ps[half][:, (h % 4) * CH:(h % 4 + 1) * CH], k_in[b][:, a, :], q_in[b][:, qa, :],
                                                   start=True, stop=True)
                    ins.then_inc(sc_ready, 1)
                pe.wait_ge(qk_ready, NE * c + (NE + QK0))
                pe.wait_ge(xdt_ready, c + 1)
                for a in range(CT):
                    ins = nc.tensor.transpose(mid_ps[:, a * P:(a + 1) * P], k_dec[:, a, :], ident[:])
                ins.then_inc(kT_ps_ready, 1)
                pe.wait_ge(score_ready, NEV * c + NEV)
                pe.wait_ge(state_ready, c + 1)
                pe.wait_ge(hst_ready, c + 1)
                for h, qa, a, r in heads():
                    nc.tensor.matmul(o_ps[:, h * CH:(h + 1) * CH], v_in[b][:, h, :], score[:, h * CH:(h + 1) * CH], start=True, stop=False)
                    ins = nc.tensor.matmul(o_ps[:, h * CH:(h + 1) * CH], state[:, a, :], q_dec[:, qa, :], start=False, stop=True)
                ins.then_inc(o_ready, 1)
                pe.wait_ge(kT_ready, c + 1)
                for h, qa, a, r in heads():
                    ins = nc.tensor.matmul(mid_ps[r, a * P:(a + 1) * P], kT[:, a, r], v_in[b][:, h, :], start=True, stop=True,
                                           skip_group_check=True)
                ins.then_inc(upd_ready, 1)
                pe.wait_ge(w_ready, c + 1)
                pe.wait_ge(bT_ready, c + 1)
                for h in range(SSM_HEADS):
                    r = slice(HALF * (h % 2), HALF * (h % 2) + HALF)
                    ins = nc.tensor.matmul(intra_ps[r, (h // 2) * CH:(h // 2 + 1) * CH], xdt[:, h, :], wmat[:, h, :], start=True, stop=True,
                                           skip_group_check=True)
                ins.then_inc(intra_ready, 1)
                pe.wait_ge(score_ready, NEV * c + NEV)
                hs = hst[:].rearrange("p h e -> p (h e)")
                for k in range(8):
                    ins = nc.tensor.matmul(inter_ps[:, k * CH:(k + 1) * CH], hs[:, k * P:(k + 1) * P], bc_in[b][:, 4 + k // 2, :],
                                           start=True, stop=True)
                ins.then_inc(inter_ready, 1)
                pe.wait_ge(state_ready, c + 2)
                pe.wait_ge(sq_ready, c + 1)
                for half in range(2):
                    ins = nc.tensor.matmul(mid_ps[:, half * 512:(half + 1) * 512], mean_a[:], sq[:, half * 512:(half + 1) * 512],
                                           start=True, stop=True)
                ins.then_inc(ms_ready, 1)
                pe.wait_ge(xw_ready, c + 1)
                pe.wait_ge(o_used, c + 1)
                for g in range(SSM_GROUPS):
                    ins = nc.tensor.matmul(o_ps[:, g * 256:(g + 1) * 256], bT[:, g, :], xw[:, g * GH:(g + 1) * GH, :], start=True, stop=True)
                ins.then_inc(hupd_ready, 1)
                pe.wait_ge(sq2_ready, c + 1)
                s2 = sq[:].rearrange("p (g a t) -> p a g t", a=2, t=CH)
                for a in range(2):
                    ins = nc.tensor.matmul(mid_ps[:, 0:512], mean_b[:], s2[:, a], start=a == 0, stop=a == 1)
                ins.then_inc(ms2_ready, 1)
            chunks(pe, body)


def merge(nc, io, dr, m_hi, m_lo):
    HT = T // 2
    YK = 16
    BRANCH = ((0, 4), (4, 8), (8, 16))
    DM = D // P
    PIECES, PK = 4, YK // 4
    LINKS = 6
    with ExitStack() as ctx:
        sb = lambda name, shape, dt=F32: ctx.enter_context(nc.sbuf_tensor(name, shape, dt))
        sem = semaphores(nc, ctx)
        y_raw = [sb(f"y_raw{b}", [P, PK, HT]) for b in range(2)]
        y_hi = sb("y_hi", [P, YK, HT], F32R)
        y_lo = sb("y_lo", [P, YK, HT], F32R)
        w_raw = [sb(f"wb_raw{b}", [P, YK, P]) for b in range(2)]
        w_hi = [sb(f"wb_hi{b}", [P, YK, P], F32R) for b in range(2)]
        w_lo = sb("wb_lo", [P, YK, P], F32R)
        gate = [sb(f"gate{b}", [P, 3, HT]) for b in range(2)]
        part = sb("part", [P, 2, HT])
        ps = [ctx.enter_context(nc.psum_tensor(f"br{b}", [P, 3, HT], F32)) for b in range(2)]
        y_loaded = [sem(f"y_loaded{b}") for b in range(2)]
        y_hi_ready = sem("y_hi_ready")
        y_ready = sem("y_ready")
        w_loaded = [sem(f"w_loaded{b}") for b in range(2)]
        gate_loaded = [sem(f"gate_loaded{b}") for b in range(2)]
        w_hi_ready = sem("w_hi_ready")
        w_ready = sem("w_ready")
        gate_ready = sem("gate_ready")
        mm_done = sem("mm_done")
        merged_ready = sem("merged_ready")
        dve_own = sem("dve_own")
        block = ctx.enter_context(nc.Block())
        ONE = 1

        def tiles(eng, before, body):
            with eng.Fori(0, 2) as half:
                before(half)
                with eng.Fori(0, DM // 2) as i:
                    for b in range(2):
                        body(DM * half + 2 * i + b, b, half, 2 * i + b, (DM // 2) * half + i)

        @block.sync
        def _(sp):
            def before(half):
                for p in range(PIECES):
                    sp.wait_ge(y_ready, PIECES * half + (p - 1 + ONE + 1))
                    sp.dma_start(y_raw[p % 2][:], dr["y"][p * PK * P:(p + 1) * PK * P, bass.ds(half * HT, HT)]
                                 .rearrange("(k p) t -> p k t", p=P)).then_inc(y_loaded[p % 2], 16)

            def body(n, b, half, d, turn):
                sp.wait_ge(w_ready, n + (ONE + 1) - 1)
                col = bass.ds(d * P, P)
                for name, (k0, k1) in zip(("w_br_gla", "w_br_hgrn", "w_br_ssm"), BRANCH):
                    sp.dma_start(w_raw[b][:, k0:k1, :], io[name][:, col].rearrange("(k p) n -> p k n", p=P)).then_inc(w_loaded[b], 16)
                sp.wait_ge(merged_ready, n + (ONE + 1) - 1)
                sp.dma_start(gate[b][:], dr["gates"].rearrange("(g r) t -> r g t", g=3)[col, :, bass.ds(half * HT, HT)])\
                    .then_inc(gate_loaded[b], 16)
            sp.sem_inc(y_ready, ONE + 1)
            tiles(sp, before, body)

        @block.scalar
        def _(act):
            nc.scalar.preload_act_table(ACT.Sigmoid)

            def before(half):
                act.wait_ge(mm_done, DM * half + ONE)
                for p in range(PIECES):
                    act.wait_ge(y_loaded[p % 2], 32 * half + 16 * (p // 2 + 1))
                    nc.scalar.copy(y_hi[:, p * PK:(p + 1) * PK, :], y_raw[p % 2][:]).then_inc(y_hi_ready, 1)

            def body(n, b, half, d, turn):
                act.wait_ge(w_loaded[b], 48 * turn + 48)
                act.wait_ge(mm_done, n + (ONE + 1) - 1)
                nc.scalar.copy(w_hi[b][:], w_raw[b][:]).then_inc(w_hi_ready, 1)
                act.wait_ge(gate_loaded[b], 16 * turn + 16)
                nc.scalar.activation(gate[b][:], gate[b][:], ACT.Sigmoid).then_inc(gate_ready, 1)
            tiles(act, before, body)

        @block.vector
        def _(dve):
            own = Chain(dve, dve_own)
            dve.sem_inc(merged_ready, ONE + 1)
            dve.sem_inc(w_ready, ONE + 1)

            def before(half):
                dve.wait_ge(mm_done, DM * half + ONE)
                for p in range(PIECES):
                    dve.wait_ge(y_hi_ready, PIECES * half + (p + 1))
                    ks = slice(p * PK, (p + 1) * PK)
                    nc.vector.tensor_tensor(y_lo[:, ks, :], y_raw[p % 2][:], y_hi[:, ks, :].bitcast(F32), ALU.subtract).then_inc(y_ready, 1)

            def body(n, b, half, d, turn):
                own.turn(n, LINKS)
                dve.wait_ge(w_hi_ready, n + 1)
                dve.wait_ge(mm_done, n + ONE)
                nc.vector.tensor_tensor(w_lo[:], w_raw[b][:], w_hi[b][:].bitcast(F32), ALU.subtract).then_inc(w_ready, 1)
                dve.wait_ge(gate_ready, n + 1)
                dve.wait_ge(mm_done, n + 1 + ONE)
                nc.vector.tensor_tensor(part[:, 0, :], ps[b][:, 0, :], gate[b][:, 0, :], ALU.mult).then_inc(dve_own, 1)
                own.n += 1
                own.link(nc.vector.tensor_tensor(part[:, 1, :], ps[b][:, 1, :], gate[b][:, 1, :], ALU.mult))
                own.link(nc.vector.tensor_tensor(part[:, 0, :], part[:, 0, :], part[:, 1, :], ALU.add))
                own.link(nc.vector.tensor_tensor(part[:, 1, :], ps[b][:, 2, :], gate[b][:, 2, :], ALU.mult))
                own.link(nc.vector.tensor_tensor(part[:, 0, :], part[:, 0, :], part[:, 1, :], ALU.add))
                ts = bass.ds(half * HT, HT)
                own.link(nc.vector.tensor_copy(m_hi[:, bass.ds(d, 1), ts], part[:, 0:1, :]))
                nc.vector.tensor_tensor(m_lo[:, bass.ds(d, 1), ts], part[:, 0:1, :], m_hi[:, bass.ds(d, 1), ts].bitcast(F32), ALU.subtract)\
                    .then_inc(merged_ready, 1)
                dve.wait_ge(merged_ready, n + 1 + (ONE + 1))
                assert own.n == LINKS
            tiles(dve, before, body)

        @block.tensor
        def _(pe):
            pe.sem_inc(mm_done, ONE)

            def before(half):
                pass

            def body(n, b, half, d, turn):
                pe.wait_ge(y_ready, PIECES * half + (PIECES + ONE + 1))
                pe.wait_ge(w_ready, n + 1 + (ONE + 1))
                pe.wait_ge(merged_ready, n + (ONE + 1) - 1)
                for br, (k0, k1) in enumerate(BRANCH):
                    for k in range(k0, k1):
                        for q, (w, y) in enumerate(((w_hi[b], y_hi), (w_hi[b], y_lo), (w_lo, y_hi))):
                            ins = nc.tensor.matmul(ps[b][:, br, :], w[:, k, :], y[:, k, :], start=k == k0 and q == 0, stop=k == k1 - 1 and q == 2)
                ins.then_inc(mm_done, 1)
            tiles(pe, before, body)


def output_and_route(nc, io, dr, ident, m_hi, m_lo):
    NL = N_GROUPS + N_EXPERTS
    BIG = 3e38
    with ExitStack() as ctx:
        sb = lambda name, shape, dt=F32: ctx.enter_context(nc.sbuf_tensor(name, shape, dt))
        sem = semaphores(nc, ctx)
        w_raw = [sb(f"wo_raw{b}", [P, 2, D]) for b in range(2)]
        w_hi = sb("wo_hi", [P, KT, D], F32R)
        w_lo = sb("wo_lo", [P, KT, D], F32R)
        x_in = [sb(f"xr{b}", [P, D]) for b in range(2)]
        x2 = [sb(f"x2_{b}", [P, D]) for b in range(2)]
        h2 = [sb(f"h2_{b}", [P, D]) for b in range(2)]
        h2T = sb("h2T", [P, KT, P])
        n2 = sb("n2", [P, D])
        stat = sb("stat2", [P, NCH, 2])
        cst = sb("cst2", [P, 1])
        rw = sb("rw", [P, KT, NL])
        rb = sb("rb", [P, NL])
        lg = sb("lg", [P, NCH, NL])
        fill = sb("fill", [P, 1024], U32)
        it32 = sb("it32", [P, N_EXPERTS])
        itg = sb("itg", [P, N_GROUPS])
        grp = sb("grp", [P, N_EXPERTS])
        tok = sb("tok", [P, NCH])
        upper = sb("upper", [P, P])
        ones = sb("ones", [P, P])
        big = lambda name: sb(name, [P, NCH, N_EXPERTS])
        ml, oh1, oh2, tmp, oh, ohp = big("ml"), big("oh1"), big("oh2"), big("tmp"), big("oh"), big("ohp")
        col = lambda name: sb(name, [P, NCH])
        gmax, gsum, gidx, m1, m2, i1, i2, e2, w1, w2, r1, r2 = (col(f"rt_{n}") for n in range(12))
        gt = sb("gt", [P, NCH, N_GROUPS])
        slot = sb("slot", [P, 2, NCH], U32)
        rec = sb("rec", [P, 2, NCH, 4], U32)
        cnt = sb("cnt", [P, N_EXPERTS])
        slab = sb("slab", [P, N_EXPERTS, 7])
        fl, pos, wk, idv = (sb(n, [P, N_EXPERTS * 7]) for n in ("fl", "pos", "wk", "idv"))
        onesf = sb("onesf", [P, N_EXPERTS * 7])
        nth = sb("nth", [P, 1])
        work = sb("work_f", [P, 2])
        work_i = sb("work_i", [P, 2], I32)
        o_ps = [ctx.enter_context(nc.psum_tensor(f"xo{b}", [P, D], F32)) for b in range(2)]
        t_ps = ctx.enter_context(nc.psum_tensor("h2t", [P, D], F32))
        l_ps = ctx.enter_context(nc.psum_tensor("lgp", [P, 512], F32))
        r_ps = ctx.enter_context(nc.psum_tensor("rkp", [P, 512], F32))

        par_in = sem("par_in")
        w_loaded = [sem(f"w_loaded{b}") for b in range(2)]
        x_loaded = [sem(f"x_loaded{b}") for b in range(2)]
        w_hi_ready = sem("w_hi_ready")
        w_ready = sem("w_ready")
        mm_done = sem("mm_done")
        x2_ready = sem("x2_ready")
        rstd_ready = sem("rstd_ready")
        h2_ready = sem("h2_ready")
        h2_scaled = sem("h2_scaled")
        x2_stored = [sem(f"x2_stored{b}") for b in range(2)]
        h2_stored = [sem(f"h2_stored{b}") for b in range(2)]
        hT_ready = sem("hT_ready")
        hT_sb = sem("hT_sb")
        lg_ready = sem("lg_ready")
        lg_in = sem("lg_in")
        pool_own = sem("pool_own")
        const_ready = sem("const_ready")
        filled = sem("filled")
        gate_arg = sem("gate_arg")
        gate_exp = sem("gate_exp")
        pick_arg = sem("pick_arg")
        pick_exp = sem("pick_exp")
        oh_ready = sem("oh_ready")
        rank_ready = sem("rank_ready")
        cnt_ready = sem("cnt_ready")
        rank_read = sem("rank_read")
        rec_ready = sem("rec_ready")
        scattered = sem("scattered")
        work_ready = sem("work_ready")
        work_stored = sem("work_stored")
        dve_own = sem("dve_own")
        act_own = sem("act_own")
        block = ctx.enter_context(nc.Block())

        @block.sync
        def _(sp):
            for p in range(KT // 2):
                if p >= 2:
                    sp.wait_ge(w_ready, p - 1)
                sp.dma_start(w_raw[p % 2][:], io["w_out"][p * 2 * P:(p + 1) * 2 * P, :].rearrange("(k p) n -> p k n", p=P))\
                    .then_inc(w_loaded[p % 2], 16)
            sp.dma_start(n2[:], io["norm2_w"].unsqueeze(0).to_broadcast([P, D])).then_inc(par_in, 16)
            sp.dma_start(rw[:, :, 0:N_GROUPS], io["router_group_w"].rearrange("(k p) n -> p k n", p=P)).then_inc(par_in, 16)
            sp.dma_start(rw[:, :, N_GROUPS:NL], io["router_expert_w"].rearrange("(k p) n -> p k n", p=P)).then_inc(par_in, 16)
            sp.dma_start(rb[:, 0:N_GROUPS], io["router_group_b"].unsqueeze(0).to_broadcast([P, N_GROUPS])).then_inc(par_in, 16)
            sp.dma_start(rb[:, N_GROUPS:NL], io["router_expert_b"].unsqueeze(0).to_broadcast([P, N_EXPERTS])).then_inc(par_in, 16)
            sp.wait_ge(const_ready, 1)
            sp.dma_start(dr["table"].rearrange("(p n) w -> p (n w)", p=P), fill[:]).then_inc(filled, 16)
            for c in range(NCH):
                if c >= 2:
                    sp.wait_ge(x2_ready, c - 1)
                sp.dma_start(x_in[c % 2][:], io["x"][c * CH:(c + 1) * CH, :]).then_inc(x_loaded[c % 2], 16)
                if c >= 1:
                    p = c - 1
                    sp.wait_ge(x2_ready, p + 1)
                    sp.dma_start(dr["x2"][p * CH:(p + 1) * CH, :], x2[p % 2][:]).then_inc(x2_stored[p % 2], 16)
                    sp.wait_ge(h2_ready, p + 1)
                    sp.dma_start(dr["h2"][p * CH:(p + 1) * CH, :], h2[p % 2][:]).then_inc(h2_stored[p % 2], 16)
            p = NCH - 1
            sp.wait_ge(x2_ready, p + 1)
            sp.dma_start(dr["x2"][p * CH:(p + 1) * CH, :], x2[p % 2][:]).then_inc(x2_stored[p % 2], 16)
            sp.wait_ge(h2_ready, p + 1)
            sp.dma_start(dr["h2"][p * CH:(p + 1) * CH, :], h2[p % 2][:]).then_inc(h2_stored[p % 2], 16)
            sp.wait_ge(work_ready, 1)
            sp.dma_start(dr["work"], work_i[0:16, :]).then_inc(work_stored, 16)
            sp.wait_ge(work_stored, 16)
            for b in range(2):
                sp.wait_ge(x2_stored[b], 16 * NCH // 2)
                sp.wait_ge(h2_stored[b], 16 * NCH // 2)

        @block.gpsimd
        def _(pool):
            nc.gpsimd.memset(fill[:], EMPTY).then_inc(const_ready, 1)
            nc.gpsimd.iota(it32[:], pattern=[[1, N_EXPERTS]], base=0, channel_multiplier=0, allow_small_or_imprecise_dtypes=True).then_inc(const_ready, 1)
            nc.gpsimd.iota(itg[:], pattern=[[1, N_GROUPS]], base=0, channel_multiplier=0, allow_small_or_imprecise_dtypes=True).then_inc(const_ready, 1)
            nc.gpsimd.iota(grp[:], pattern=[[1, N_GROUPS], [0, PER_GROUP]], base=0, channel_multiplier=0, allow_small_or_imprecise_dtypes=True).then_inc(const_ready, 1)
            nc.gpsimd.iota(tok[:], pattern=[[CH, NCH]], base=0, channel_multiplier=1, allow_small_or_imprecise_dtypes=True).then_inc(const_ready, 1)
            nc.gpsimd.iota(nth[:], pattern=[[0, 1]], base=1, channel_multiplier=1, allow_small_or_imprecise_dtypes=True).then_inc(const_ready, 1)
            nc.gpsimd.iota(slab[:], pattern=[[0, N_EXPERTS], [SLAB, 7]], base=SLAB, channel_multiplier=0, allow_small_or_imprecise_dtypes=True).then_inc(const_ready, 1)
            nc.gpsimd.iota(idv[:].rearrange("p (e s) -> p e s", s=7), pattern=[[T, N_EXPERTS], [SLAB, 7]], base=SLAB, channel_multiplier=0,
                           allow_small_or_imprecise_dtypes=True).then_inc(const_ready, 1)
            nc.gpsimd.memset(ones[:], 1.0).then_inc(const_ready, 1)
            nc.gpsimd.memset(onesf[:], 1.0).then_inc(const_ready, 1)
            nc.gpsimd.memset(cst[:], EPS).then_inc(const_ready, 1)
            nc.gpsimd.memset(rec[:], 0).then_inc(const_ready, 1)
            nc.gpsimd.memset(upper[:], 1.0).then_inc(pool_own, 1)
            pool.wait_ge(pool_own, 1)
            nc.gpsimd.affine_select(out=upper[:], in_=upper[:], compare_op=ALU.is_gt, fill=0.0, base=0,
                                    pattern=[[1, P]], channel_multiplier=-1).then_inc(const_ready, 1)
            pool.wait_ge(filled, 16)
            pool.wait_ge(rec_ready, 2)
            for pick in range(2):
                for c in range(NCH):
                    pool.indirect_dma_start(out=dr["table"], out_offset=bass.IndirectOffsetOnAxis(ap=slot[:, pick, c:c + 1], axis=0),
                                            in_=rec[:, pick, c, :], in_offset=None).then_inc(scattered, 16)
            pool.wait_ge(scattered, 16 * 2 * NCH)

        N_CONST = 13

        @block.scalar
        def _(act):
            own = Chain(act, act_own)
            nc.scalar.preload_act_table_set(EXP_LN_SET)
            for p in range(KT // 2):
                act.wait_ge(w_loaded[p % 2], 16 * (p // 2 + 1))
                nc.scalar.copy(w_hi[:, 2 * p:2 * p + 2, :], w_raw[p % 2][:]).then_inc(w_hi_ready, 1)
            act.wait_ge(const_ready, N_CONST)
            for c in range(NCH):
                act.wait_ge(x2_ready, c + 1)
                if c >= 2:
                    act.wait_ge(h2_stored[c % 2], 16 * (c // 2))
                    act.wait_ge(hT_ready, c - 1)
                own.link(nc.scalar.activation(h2[c % 2][:], x2[c % 2][:], ACT.Square, accum_out=stat[:, c, 0:1]))
                own.link(nc.scalar.activation(stat[:, c, 0:1], stat[:, c, 0:1], ACT.Ln, scale=1.0 / D, bias=cst[:]))
                nc.scalar.activation(stat[:, c, 1:2], stat[:, c, 0:1], ACT.Exp, scale=-0.5).then_inc(rstd_ready, 1)
                act.wait_ge(hT_ready, c + 1)
                nc.scalar.copy(h2T[:].rearrange("p k t -> p (k t)"), t_ps[:]).then_inc(hT_sb, 1)
            act.wait_ge(gate_arg, 1)
            nc.scalar.activation(gt[:], gt[:], ACT.Exp).then_inc(gate_exp, 1)
            act.wait_ge(pick_arg, 1)
            nc.scalar.activation(e2[:], e2[:], ACT.Exp).then_inc(pick_exp, 1)

        @block.vector
        def _(dve):
            own = Chain(dve, dve_own)
            L = own.link
            tt, ts = nc.vector.tensor_tensor, nc.vector.tensor_scalar
            for p in range(KT // 2):
                dve.wait_ge(w_hi_ready, p + 1)
                tt(w_lo[:, 2 * p:2 * p + 2, :], w_raw[p % 2][:], w_hi[:, 2 * p:2 * p + 2, :].bitcast(F32), ALU.subtract).then_inc(w_ready, 1)
            dve.wait_ge(par_in, 16 * 5)
            dve.wait_ge(const_ready, N_CONST)
            for c in range(NCH):
                b = c % 2
                dve.wait_ge(x_loaded[b], 16 * (c // 2 + 1))
                dve.wait_ge(mm_done, c + 1)
                if c >= 2:
                    dve.wait_ge(x2_stored[b], 16 * (c // 2))
                tt(x2[b][:], o_ps[b][:], x_in[b][:], ALU.add).then_inc(x2_ready, 1)
                dve.wait_ge(rstd_ready, c + 1)
                nc.vector.scalar_tensor_tensor(h2[b][:], x2[b][:], stat[:, c, 1:2], n2[:], ALU.mult, ALU.mult).then_inc(h2_ready, 1)
                dve.wait_ge(lg_ready, c + 1)
                tt(lg[:, c, :], l_ps[:, 0:NL], rb[:], ALU.add).then_inc(lg_in, 1)
            dve.wait_ge(lg_in, NCH)
            g4, e32 = lg[:, :, 0:N_GROUPS], lg[:, :, N_GROUPS:NL]
            b4 = lambda x: x[:].unsqueeze(2).to_broadcast([P, NCH, N_GROUPS])
            b32 = lambda x: x[:].unsqueeze(2).to_broadcast([P, NCH, N_EXPERTS])
            bc = lambda x, n: x[:].unsqueeze(1).to_broadcast([P, NCH, n])
            red = lambda out, in_, op: nc.vector.tensor_reduce(out[:], in_, AX.X, op)
            L(red(gmax, g4, ALU.max))
            tt(gt[:], g4, b4(gmax), ALU.subtract).then_inc(gate_arg, 1)
            dve.wait_ge(gate_exp, 1)
            L(red(gsum, gt[:], ALU.add))
            L(nc.vector.reciprocal(gsum[:], gsum[:]))

            def first_max(index, values, top, iota, n, scratch, wide):
                L(tt(scratch, values, wide(top), ALU.is_equal))
                L(ts(scratch, scratch, -1000.0, 1000.0, ALU.mult, ALU.add))
                L(tt(scratch, scratch, bc(iota, n), ALU.add))
                L(red(index, scratch, ALU.min))

            first_max(gidx, g4, gmax, itg, N_GROUPS, gt[:], b4)
            L(tt(tmp[:], bc(grp, N_EXPERTS), b32(gidx), ALU.is_equal))
            L(tt(ml[:], e32, tmp[:], ALU.mult))
            L(ts(tmp[:], tmp[:], BIG, -BIG, ALU.mult, ALU.add))
            L(tt(ml[:], ml[:], tmp[:], ALU.add))
            L(red(m1, ml[:], ALU.max))
            first_max(i1, ml[:], m1, it32, N_EXPERTS, tmp[:], b32)
            L(tt(oh1[:], bc(it32, N_EXPERTS), b32(i1), ALU.is_equal))
            L(ts(tmp[:], oh1[:], -BIG, None, ALU.mult))
            L(tt(ml[:], ml[:], tmp[:], ALU.add))
            L(red(m2, ml[:], ALU.max))
            first_max(i2, ml[:], m2, it32, N_EXPERTS, tmp[:], b32)
            L(tt(oh2[:], bc(it32, N_EXPERTS), b32(i2), ALU.is_equal))
            L(tt(oh[:], oh1[:], oh2[:], ALU.add))
            L(nc.vector.memset(ohp[:, 0, :], 0.0))
            for c in range(1, NCH):
                L(tt(ohp[:, c, :], ohp[:, c - 1, :], oh[:, c - 1, :], ALU.add))
            tt(e2[:], m2[:], m1[:], ALU.subtract).then_inc(pick_arg, 1)
            tt(cnt[:], ohp[:, NCH - 1, :], oh[:, NCH - 1, :], ALU.add).then_inc(oh_ready, 1)
            dve.wait_ge(pick_exp, 1)
            L(nc.vector.tensor_scalar_add(w1[:], e2[:], 1.0))
            L(nc.vector.reciprocal(w1[:], w1[:]))
            L(tt(w1[:], w1[:], gsum[:], ALU.mult))
            L(tt(w2[:], w1[:], e2[:], ALU.mult))
            dve.wait_ge(rank_ready, 1)
            rank = r_ps[:, 0:NCH * N_EXPERTS].rearrange("p (c e) -> p c e", e=N_EXPERTS)
            for pick, (o1, ix, r, w) in enumerate(((oh1, i1, r1, w1), (oh2, i2, r2, w2))):
                L(tt(ml[:], rank, o1[:], ALU.mult))
                L(red(r, ml[:], ALU.add))
                L(nc.vector.scalar_tensor_tensor(r[:], ix[:], float(T), r[:], ALU.mult, ALU.add))
                L(nc.vector.tensor_copy(slot[:, pick, :], r[:]))
                L(nc.vector.tensor_copy(rec[:, pick, :, 0], tok[:]))
                L(nc.vector.tensor_scalar_add(rec[:, pick, :, 1], tok[:], float(pick * T)))
                nc.vector.tensor_copy(rec[:, pick, :, 2].bitcast(F32), w[:]).then_inc(rec_ready, 1)
            dve.wait_ge(cnt_ready, 1)
            L(nc.vector.tensor_copy(cnt[:], l_ps[:, 0:N_EXPERTS]))
            f3 = fl[:].rearrange("p (e s) -> p e s", s=7)
            L(tt(f3, cnt[:].unsqueeze(2).to_broadcast([P, N_EXPERTS, 7]), slab[:], ALU.is_gt))
            L(nc.vector.tensor_tensor_scan(pos[:], onesf[:], fl[:], 0.0, ALU.mult, ALU.add))
            L(ts(pos[:], pos[:], nth[:], None, ALU.is_equal))
            L(tt(fl[:], fl[:], pos[:], ALU.mult))
            L(tt(wk[:], fl[:], idv[:], ALU.mult))
            L(nc.vector.reduce_sum(work[:, 0:1], wk[:], AX.X))
            L(tt(wk[:].rearrange("p (e s) -> p e s", s=7), f3, it32[:].unsqueeze(2).to_broadcast([P, N_EXPERTS, 7]), ALU.mult))
            L(nc.vector.reduce_sum(work[:, 1:2], wk[:], AX.X))
            nc.vector.tensor_copy(work_i[:], work[:]).then_inc(work_ready, 1)

        @block.tensor
        def _(pe):
            pe.wait_ge(w_ready, KT // 2)
            pe.wait_ge(const_ready, N_CONST)
            pe.wait_ge(par_in, 16 * 5)

            def product(c):
                if c >= 2:
                    pe.wait_ge(x2_ready, c - 1)
                cs = slice(c * CH, (c + 1) * CH)
                for k in range(KT):
                    for q, (m, w) in enumerate(((m_hi, w_hi), (m_hi, w_lo), (m_lo, w_hi))):
                        for half in range(2):
                            hs = slice(half * 512, half * 512 + 512)
                            ins = nc.tensor.matmul(o_ps[c % 2][:, hs], m[:, k, cs], w[:, k, hs],
                                                   start=k == 0 and q == 0, stop=k == KT - 1 and q == 2)
                ins.then_inc(mm_done, 1)

            def route(c):
                pe.wait_ge(h2_ready, c + 1)
                if c >= 1:
                    pe.wait_ge(hT_sb, c)
                for k in range(KT):
                    ins = nc.tensor.transpose(t_ps[:, k * P:(k + 1) * P], h2[c % 2][:, k * P:(k + 1) * P], ident[:])
                ins.then_inc(hT_ready, 1)
                pe.wait_ge(hT_sb, c + 1)
                if c >= 1:
                    pe.wait_ge(lg_in, c)
                for k in range(KT):
                    ins = nc.tensor.matmul(l_ps[:, 0:NL], h2T[:, k, :], rw[:, k, :], start=k == 0, stop=k == KT - 1)
                ins.then_inc(lg_ready, 1)

            product(0)
            for c in range(1, NCH):
                product(c)
                route(c - 1)
            route(NCH - 1)
            pe.wait_ge(oh_ready, 1)
            n = NCH * N_EXPERTS
            nc.tensor.matmul(r_ps[:, 0:n], upper[:], oh[:].rearrange("p c e -> p (c e)"), start=True, stop=False)
            nc.tensor.matmul(r_ps[:, 0:n], ones[:], ohp[:].rearrange("p c e -> p (c e)"), start=False, stop=True).then_inc(rank_ready, 1)
            nc.tensor.matmul(l_ps[:, 0:N_EXPERTS], ones[:], cnt[:], start=True, stop=True).then_inc(cnt_ready, 1)


def wait_past(eng, sem, value):
    if not isinstance(value, int) or value > 0:
        eng.wait_ge(sem, value)


def experts_first_slabs(nc, io, dr, ident):
    LAST = N_EXPERTS - 1
    FK = FF // P
    with ExitStack() as ctx:
        sb = lambda name, shape, dt=F32: ctx.enter_context(nc.sbuf_tensor(name, shape, dt))
        sem = semaphores(nc, ctx)
        pair = lambda name, shape, dt=F32: [sb(f"{name}{b}", shape, dt) for b in range(2)]
        wg, wu = pair("wg", [P, KT, FF]), pair("wu", [P, KT, FF])
        wdn = pair("wdn", [P, FK, D])
        recs = sb("recs", [P, N_EXPERTS, 4], U32)
        g_idx, s_idx = pair("g_idx", [P, 1], U32), pair("s_idx", [P, 1], U32)
        xe, ye = pair("xe", [P, D]), pair("ye", [P, D])
        xT = sb("xeT", [P, KT, P])
        sg = sb("sg", [P, FF])
        hid = sb("hid", [P, FF])
        hT = sb("hidT", [P, FK, P])
        g_ps = ctx.enter_context(nc.psum_tensor("g_ps", [P, FF], F32))
        u_ps = ctx.enter_context(nc.psum_tensor("u_ps", [P, FF], F32))
        y_ps = ctx.enter_context(nc.psum_tensor("y_ps", [P, D], F32))
        xT_ps = ctx.enter_context(nc.psum_tensor("xT_ps", [P, D], F32))
        hT_ps = ctx.enter_context(nc.psum_tensor("hT_ps", [P, FF], F32))
        recs_in = sem("recs_in")
        zeroed = sem("xe_zeroed")
        wg_in, wu_in, wd_in = ([sem(f"{n}_in{b}") for b in range(2)] for n in ("wg", "wu", "wd"))
        gi_ready = sem("gi_ready")
        si_ready = sem("si_ready")
        gathered = [sem(f"gathered{b}") for b in range(2)]
        scattered = [sem(f"scattered{b}") for b in range(2)]
        xT_ready = sem("xT_ready")
        xT_sb = sem("xT_sb")
        g_done = sem("g_done")
        u_done = sem("u_done")
        silu_ready = sem("silu_ready")
        hid_ready = sem("hid_ready")
        hT_ready = sem("hT_ready")
        hT_sb = sem("hT_sb")
        d_done = sem("d_done")
        y_ready = sem("y_ready")
        passed = sem("passed")
        block = ctx.enter_context(nc.Block())

        def experts(eng, body):
            for e in range(2):
                body(e, e, 0)
            with eng.Fori(0, (N_EXPERTS - 4) // 2) as i:
                for b in range(2):
                    body(2 * i + (2 + b), b, i + 1)
            for e in (LAST - 1, LAST):
                body(e, e % 2, e // 2)

        @block.sync
        def _(sp):
            sp.dma_start(recs[:], dr["table"].rearrange("(e s) w -> s e w", s=T)[0:SLAB]).then_inc(recs_in, 16)

            def body(e, b, turn):
                one = bass.ds(e, 1)
                wait_past(sp, g_done, e - 1)
                sp.dma_start(wg[b][:], io["moe_w_gate"][one].rearrange("o (k p) f -> p (o k) f", p=P)).then_inc(wg_in[b], 16)
                wait_past(sp, u_done, e - 1)
                sp.dma_start(wu[b][:], io["moe_w_up"][one].rearrange("o (k p) f -> p (o k) f", p=P)).then_inc(wu_in[b], 16)
                wait_past(sp, d_done, e - 1)
                sp.dma_start(wdn[b][:], io["moe_w_down"][one].rearrange("o (k p) d -> p (o k) d", p=P)).then_inc(wd_in[b], 16)
            experts(sp, body)

        @block.gpsimd
        def _(pool):
            for b in range(2):
                nc.gpsimd.memset(xe[b][:], 0.0).then_inc(zeroed, 1)
            pool.wait_ge(zeroed, 2)
            pool.wait_ge(recs_in, 16)

            def gather(e, b):
                wait_past(pool, xT_ready, e - 1)
                pool.sem_inc(passed, 1)
                nc.gpsimd.tensor_copy(g_idx[b][:], recs[:, bass.ds(e, 1), 0]).then_inc(gi_ready, 1)
                pool.wait_ge(gi_ready, e + 1)
                pool.sem_inc(passed, 1)
                pool.indirect_dma_start(out=xe[b][:], out_offset=None, in_=dr["h2"],
                                        in_offset=bass.IndirectOffsetOnAxis(ap=g_idx[b][:], axis=0),
                                        bounds_check=T - 1, oob_is_err=False).then_inc(gathered[b], 16)

            def scatter(e, b, turn):
                wait_past(pool, scattered[b], 16 * turn)
                pool.sem_inc(passed, 1)
                nc.gpsimd.tensor_copy(s_idx[b][:], recs[:, bass.ds(e, 1), 1]).then_inc(si_ready, 1)
                pool.wait_ge(si_ready, e + 1)
                pool.wait_ge(y_ready, e + 1)
                pool.sem_inc(passed, 1)
                pool.indirect_dma_start(out=dr["pairs"], out_offset=bass.IndirectOffsetOnAxis(ap=s_idx[b][:], axis=0),
                                        in_=ye[b][:], in_offset=None, bounds_check=2 * T - 1, oob_is_err=False)\
                    .then_inc(scattered[b], 16)

            def body(e, b, turn):
                if not (isinstance(e, int) and e == LAST):
                    gather(e + 1, 1 - b)
                if not (isinstance(e, int) and e == 0):
                    scatter(e - 1, 1 - b, turn - 1 + b)
            gather(0, 0)
            experts(pool, body)
            scatter(LAST, 1, LAST // 2)
            for b in range(2):
                pool.wait_ge(scattered[b], 16 * N_EXPERTS // 2)

        @block.scalar
        def _(act):
            nc.scalar.preload_act_table(ACT.Silu)

            def rows(e):
                act.wait_ge(xT_ready, e + 1)
                wait_past(act, u_done, e)
                nc.scalar.copy(xT[:].rearrange("p k t -> p (k t)"), xT_ps[:]).then_inc(xT_sb, 1)

            def body(e, b, turn):
                act.wait_ge(g_done, e + 1)
                wait_past(act, hid_ready, e)
                nc.scalar.activation(sg[:], g_ps[:], ACT.Silu).then_inc(silu_ready, 1)
                if not (isinstance(e, int) and e == LAST):
                    rows(e + 1)
                act.wait_ge(hT_ready, e + 1)
                wait_past(act, d_done, e)
                nc.scalar.copy(hT[:].rearrange("p k t -> p (k t)"), hT_ps[:]).then_inc(hT_sb, 1)
            rows(0)
            experts(act, body)

        @block.vector
        def _(dve):
            dve.wait_ge(recs_in, 16)

            def weigh(e, b, turn):
                dve.wait_ge(d_done, e + 1)
                wait_past(dve, scattered[b], 16 * turn)
                w = recs[:, bass.ds(e, 1), 2].bitcast(F32).to_broadcast([P, D])
                nc.vector.tensor_tensor(ye[b][:], y_ps[:], w, ALU.mult).then_inc(y_ready, 1)

            def body(e, b, turn):
                dve.wait_ge(silu_ready, e + 1)
                dve.wait_ge(u_done, e + 1)
                wait_past(dve, hT_ready, e)
                nc.vector.tensor_tensor(hid[:], u_ps[:], sg[:], ALU.mult).then_inc(hid_ready, 1)
                if not (isinstance(e, int) and e == 0):
                    weigh(e - 1, 1 - b, turn - 1 + b)
            experts(dve, body)
            weigh(LAST, 1, LAST // 2)

        @block.tensor
        def _(pe):
            def rows(e, b, turn):
                pe.wait_ge(gathered[b], 16 * turn + 16)
                wait_past(pe, xT_sb, e)
                for k in range(KT):
                    ins = nc.tensor.transpose(xT_ps[:, k * P:(k + 1) * P], xe[b][:, k * P:(k + 1) * P], ident[:])
                ins.then_inc(xT_ready, 1)

            def down(e, b, turn):
                pe.wait_ge(hT_sb, e + 1)
                pe.wait_ge(wd_in[b], 16 * turn + 16)
                wait_past(pe, y_ready, e)
                for k in range(FK):
                    for half in range(2):
                        hs = slice(half * 512, half * 512 + 512)
                        ins = nc.tensor.matmul(y_ps[:, hs], hT[:, k, :], wdn[b][:, k, hs], start=k == 0, stop=k == FK - 1)
                ins.then_inc(d_done, 1)

            def body(e, b, turn):
                pe.wait_ge(xT_sb, e + 1)
                pe.wait_ge(wg_in[b], 16 * turn + 16)
                wait_past(pe, silu_ready, e)
                for k in range(KT):
                    ins = nc.tensor.matmul(g_ps[:], xT[:, k, :], wg[b][:, k, :], start=k == 0, stop=k == KT - 1)
                ins.then_inc(g_done, 1)
                pe.wait_ge(wu_in[b], 16 * turn + 16)
                wait_past(pe, hid_ready, e)
                for k in range(KT):
                    ins = nc.tensor.matmul(u_ps[:], xT[:, k, :], wu[b][:, k, :], start=k == 0, stop=k == KT - 1)
                ins.then_inc(u_done, 1)
                if not (isinstance(e, int) and e == 0):
                    down(e - 1, 1 - b, turn - 1 + b)
                if not (isinstance(e, int) and e == LAST):
                    rows(e + 1, 1 - b, turn + b)
                pe.wait_ge(hid_ready, e + 1)
                wait_past(pe, hT_sb, e)
                for k in range(FK):
                    ins = nc.tensor.transpose(hT_ps[:, k * P:(k + 1) * P], hid[:, k * P:(k + 1) * P], ident[:])
                ins.then_inc(hT_ready, 1)
            rows(0, 0, 0)
            experts(pe, body)
            down(LAST, 1, LAST // 2)


def experts_further_slabs(nc, io, dr, ident):
    FK = FF // P
    with ExitStack() as ctx:
        sb = lambda name, shape, dt=F32: ctx.enter_context(nc.sbuf_tensor(name, shape, dt))
        sem = semaphores(nc, ctx)
        wg, wu, wdn = sb("xwg", [P, KT, FF]), sb("xwu", [P, KT, FF]), sb("xwd", [P, FK, D])
        todo = sb("todo", [1, 2 * 16], I32)
        rec = sb("xrec", [P, 4], U32)
        xe, ye = sb("xxe", [P, D]), sb("xye", [P, D])
        xT = sb("xxT", [P, KT, P])
        sg, hid = sb("xsg", [P, FF]), sb("xhid", [P, FF])
        hT = sb("xhT", [P, FK, P])
        g_ps = ctx.enter_context(nc.psum_tensor("xg_ps", [P, FF], F32))
        u_ps = ctx.enter_context(nc.psum_tensor("xu_ps", [P, FF], F32))
        y_ps = ctx.enter_context(nc.psum_tensor("xy_ps", [P, D], F32))
        xT_ps = ctx.enter_context(nc.psum_tensor("xxT_ps", [P, D], F32))
        hT_ps = ctx.enter_context(nc.psum_tensor("xhT_ps", [P, FF], F32))
        todo_in = sem("todo_in")
        zeroed = sem("xe_zeroed")
        rec_in = sem("rec_in")
        w_in = sem("w_in")
        gathered = sem("gathered")
        xT_ready = sem("xT_ready")
        xT_sb = sem("xT_sb")
        gu_done = sem("gu_done")
        silu_ready = sem("silu_ready")
        hid_ready = sem("hid_ready")
        hT_ready = sem("hT_ready")
        hT_sb = sem("hT_sb")
        d_done = sem("d_done")
        y_ready = sem("y_ready")
        scattered = sem("scattered")
        passed = sem("passed")
        block = ctx.enter_context(nc.Block())

        def slabs(eng, body):
            eng.wait_ge(todo_in, 16)
            with eng.Fori(0, N_EXTRA) as n:
                place = eng.value_load(todo[0:1, bass.ds(2 * n, 1)], min_val=0, max_val=N_EXPERTS * T - SLAB)
                expert = eng.value_load(todo[0:1, bass.ds(2 * n + 1, 1)], min_val=0, max_val=N_EXPERTS - 1)
                with eng.If(place > 0):
                    body(n, place, expert)

        @block.sync
        def _(sp):
            sp.sem_inc(scattered, 16)
            sp.dma_start(todo[:], dr["work"].rearrange("(o n) w -> o (n w)", o=1)).then_inc(todo_in, 16)

            def body(n, place, expert):
                sp.wait_ge(scattered, 16 * n + 16)
                sp.dma_start(rec[:], dr["table"][bass.ds(place, SLAB), :]).then_inc(rec_in, 16)
                one = bass.ds(expert, 1)
                sp.dma_start(wg[:], io["moe_w_gate"][one].rearrange("o (k p) f -> p (o k) f", p=P)).then_inc(w_in, 16)
                sp.dma_start(wu[:], io["moe_w_up"][one].rearrange("o (k p) f -> p (o k) f", p=P)).then_inc(w_in, 16)
                sp.dma_start(wdn[:], io["moe_w_down"][one].rearrange("o (k p) d -> p (o k) d", p=P)).then_inc(w_in, 16)
            slabs(sp, body)

        @block.gpsimd
        def _(pool):
            nc.gpsimd.memset(xe[:], 0.0).then_inc(zeroed, 1)
            pool.wait_ge(zeroed, 1)

            def body(n, place, expert):
                pool.wait_ge(rec_in, 16 * n + 16)
                pool.sem_inc(passed, 1)
                pool.indirect_dma_start(out=xe[:], out_offset=None, in_=dr["h2"],
                                        in_offset=bass.IndirectOffsetOnAxis(ap=rec[:, 0:1], axis=0),
                                        bounds_check=T - 1, oob_is_err=False).then_inc(gathered, 16)
                pool.wait_ge(y_ready, n + 1)
                pool.sem_inc(passed, 1)
                pool.indirect_dma_start(out=dr["pairs"], out_offset=bass.IndirectOffsetOnAxis(ap=rec[:, 1:2], axis=0),
                                        in_=ye[:], in_offset=None, bounds_check=2 * T - 1, oob_is_err=False)\
                    .then_inc(scattered, 16)
                pool.wait_ge(scattered, 16 * n + 32)
            slabs(pool, body)

        @block.scalar
        def _(act):
            nc.scalar.preload_act_table(ACT.Silu)

            def body(n, place, expert):
                act.wait_ge(xT_ready, n + 1)
                nc.scalar.copy(xT[:].rearrange("p k t -> p (k t)"), xT_ps[:]).then_inc(xT_sb, 1)
                act.wait_ge(gu_done, n + 1)
                nc.scalar.activation(sg[:], g_ps[:], ACT.Silu).then_inc(silu_ready, 1)
                act.wait_ge(hT_ready, n + 1)
                nc.scalar.copy(hT[:].rearrange("p k t -> p (k t)"), hT_ps[:]).then_inc(hT_sb, 1)
            slabs(act, body)

        @block.vector
        def _(dve):
            def body(n, place, expert):
                dve.wait_ge(silu_ready, n + 1)
                nc.vector.tensor_tensor(hid[:], u_ps[:], sg[:], ALU.mult).then_inc(hid_ready, 1)
                dve.wait_ge(d_done, n + 1)
                nc.vector.tensor_tensor(ye[:], y_ps[:], rec[:, 2:3].bitcast(F32).to_broadcast([P, D]), ALU.mult).then_inc(y_ready, 1)
            slabs(dve, body)

        @block.tensor
        def _(pe):
            def body(n, place, expert):
                pe.wait_ge(gathered, 16 * n + 16)
                for k in range(KT):
                    ins = nc.tensor.transpose(xT_ps[:, k * P:(k + 1) * P], xe[:, k * P:(k + 1) * P], ident[:])
                ins.then_inc(xT_ready, 1)
                pe.wait_ge(xT_sb, n + 1)
                pe.wait_ge(w_in, 48 * n + 48)
                for ps, w in ((g_ps, wg), (u_ps, wu)):
                    for k in range(KT):
                        ins = nc.tensor.matmul(ps[:], xT[:, k, :], w[:, k, :], start=k == 0, stop=k == KT - 1)
                ins.then_inc(gu_done, 1)
                pe.wait_ge(hid_ready, n + 1)
                for k in range(FK):
                    ins = nc.tensor.transpose(hT_ps[:, k * P:(k + 1) * P], hid[:, k * P:(k + 1) * P], ident[:])
                ins.then_inc(hT_ready, 1)
                pe.wait_ge(hT_sb, n + 1)
                for k in range(FK):
                    for half in range(2):
                        hs = slice(half * 512, half * 512 + 512)
                        ins = nc.tensor.matmul(y_ps[:, hs], hT[:, k, :], wdn[:, k, hs], start=k == 0, stop=k == FK - 1)
                ins.then_inc(d_done, 1)
            slabs(pe, body)


def finish(nc, io, dr, out):
    with ExitStack() as ctx:
        sb = lambda name, shape, dt=F32: ctx.enter_context(nc.sbuf_tensor(name, shape, dt))
        sem = semaphores(nc, ctx)
        NB = 4
        rows = [sb(f"rows{b}", [P, 3, D]) for b in range(NB)]
        sq = sb("fsq", [P, D])
        fw = sb("fw", [P, D])
        stat = sb("fstat", [P, NCH, 2])
        cst = sb("fcst", [P, 1])
        loaded = [sem(f"loaded{b}") for b in range(NB)]
        fw_in = sem("fw_in")
        c_ready = sem("c_ready")
        sum_ready = sem("sum_ready")
        rstd_ready = sem("rstd_ready")
        y_ready = sem("y_ready")
        stored = [sem(f"stored{b}") for b in range(NB)]
        dve_own = sem("dve_own")
        act_own = sem("act_own")
        block = ctx.enter_context(nc.Block())

        @block.sync
        def _(sp):
            for c in range(NCH):
                b, cs = c % NB, slice(c * CH, (c + 1) * CH)
                if c >= NB:
                    sp.wait_ge(stored[b], 16 * (c // NB))
                sp.dma_start(rows[b][:, 0, :], dr["x2"][cs, :]).then_inc(loaded[b], 16)
                sp.dma_start(rows[b][:, 1:3, :], dr["pairs"].rearrange("(a t) d -> t a d", a=2)[cs]).then_inc(loaded[b], 16)
                if c == 0:
                    sp.dma_start(fw[:], io["final_norm_w"].unsqueeze(0).to_broadcast([P, D])).then_inc(fw_in, 16)

        @block.vector
        def _(dve):
            own = Chain(dve, dve_own)
            nc.vector.memset(cst[:], EPS).then_inc(c_ready, 1)
            dve.wait_ge(fw_in, 16)

            def add(c):
                b = c % NB
                dve.wait_ge(loaded[b], 32 * (c // NB + 1))
                own.link(nc.vector.tensor_tensor(rows[b][:, 1, :], rows[b][:, 1, :], rows[b][:, 2, :], ALU.add))
                nc.vector.tensor_tensor(rows[b][:, 0, :], rows[b][:, 0, :], rows[b][:, 1, :], ALU.add).then_inc(sum_ready, 1)

            add(0)
            for c in range(NCH):
                if c + 1 < NCH:
                    add(c + 1)
                b = c % NB
                dve.wait_ge(rstd_ready, c + 1)
                nc.vector.scalar_tensor_tensor(rows[b][:, 2, :], rows[b][:, 0, :], stat[:, c, 1:2], fw[:], ALU.mult, ALU.mult)\
                    .then_inc(y_ready, 1)

        @block.scalar
        def _(act):
            own = Chain(act, act_own)
            nc.scalar.preload_act_table_set(EXP_LN_SET)
            act.wait_ge(c_ready, 1)
            for c in range(NCH):
                b = c % NB
                act.wait_ge(sum_ready, c + 1)
                own.link(nc.scalar.activation(sq[:], rows[b][:, 0, :], ACT.Square, accum_out=stat[:, c, 0:1]))
                own.link(nc.scalar.activation(stat[:, c, 0:1], stat[:, c, 0:1], ACT.Ln, scale=1.0 / D, bias=cst[:]))
                nc.scalar.activation(stat[:, c, 1:2], stat[:, c, 0:1], ACT.Exp, scale=-0.5).then_inc(rstd_ready, 1)
                act.wait_ge(y_ready, c + 1)
                act.dma_start(out[c * CH:(c + 1) * CH, :], rows[b][:, 2, :]).then_inc(stored[b], 16)
            for b in range(NB):
                act.wait_ge(stored[b], 16 * NCH // NB)


def build(nc, io, out):
    dr = {name: nc.dram_tensor(f"s_{name}", shape, dt).ap() for name, shape, dt in (
        ("qk", [512, T], F32),
        ("silu_a", [1024, T], F32),
        ("silu_b", [1536, T], F32),
        ("v", [T, 1024], F32),
        ("xbc", [2048, T], F32),
        ("gates", [3072, T], F32),
        ("k_hg", [512, T], F32),
        ("cum", [768, T], F32),
        ("dt", [16, T], F32), ("b_ssm", [16, T], F32),
        ("y", [2048, T], F32),
        ("x2", [T, D], F32), ("h2", [T, D], F32),
        ("table", [N_EXPERTS * T, 4], U32),
        ("work", [16, 2], I32),
        ("pairs", [2 * T, D], F32))}
    with ExitStack() as ctx:
        ctx.enter_context(nc.allow_non_contiguous_dma(reason="small parameters, one element for a partition"))
        ident = ctx.enter_context(nc.sbuf_tensor("ident", [P, P], F32))
        with nc.sbuf_tensor("h_hi", [P, KT, T], F32R) as h_hi, nc.sbuf_tensor("h_lo", [P, KT, T], F32R) as h_lo:
            norm1_and_decays(nc, io, dr, ident, h_hi, h_lo)
            project(nc, io, dr, h_hi, h_lo)
        mixers(nc, io, dr, ident)
        with nc.sbuf_tensor("m_hi", [P, KT, T], F32R) as m_hi, nc.sbuf_tensor("m_lo", [P, KT, T], F32R) as m_lo:
            merge(nc, io, dr, m_hi, m_lo)
            output_and_route(nc, io, dr, ident, m_hi, m_lo)
        experts_first_slabs(nc, io, dr, ident)
        experts_further_slabs(nc, io, dr, ident)
        finish(nc, io, dr, out)


def kernel(**inputs):
    import concourse.bacc as bacc
    from concourse.bass_utils import run_bass_kernel_spmd

    layer = {name: np.ascontiguousarray(a[0]) for name, a in inputs.items() if name != "final_norm_w"}
    layer["final_norm_w"] = np.ascontiguousarray(inputs["final_norm_w"])
    layer["taps"] = np.ascontiguousarray(np.concatenate([layer.pop("ssm_conv_w"), layer.pop("ssm_conv_b")[None]]).T)
    nc = bacc.Bacc("TRN2", target_bir_lowering=False, num_devices=1)
    io = {name: nc.dram_tensor(name, a.shape, mybir.dt.from_np(a.dtype), kind="ExternalInput").ap() for name, a in layer.items()}
    out = nc.dram_tensor("out", (T, D), F32, kind="ExternalOutput").ap()
    build(nc, io, out)
    r = run_bass_kernel_spmd(nc, [layer], core_ids=[0])
    return r.results[0]["out"].reshape(1, T, D)
```

```python
import math
from contextlib import ExitStack

import numpy as np

import concourse.bass as bass
from concourse import mybir

F32 = mybir.dt.float32
F32R = mybir.dt.float32r
I32 = mybir.dt.int32
U32 = mybir.dt.uint32
U8 = mybir.dt.uint8
ALU = mybir.AluOpType
ACT = mybir.ActivationFunctionType
AX = mybir.AxisListType

P = 128
T = 1024
D = 1024
CH = 128
NCH = T // CH
KT = D // P
EPS = 1e-6
EXP_LN_SET = "natural_log_exp_and_others"

GLA_HEADS, GLA_DK, GLA_DV, GLA_RANK, GLA_TEMP = 4, 64, 128, 16, 16.0
HG_HEADS, HG_DIM = 4, 128
SSM_HEADS, SSM_HD, SSM_GROUPS, SSM_STATE, SSM_CONV = 16, 64, 4, 128, 4
N_GROUPS, PER_GROUP = 4, 8
N_EXPERTS, FF = 32, 512
SLAB = 128
N_EXTRA = 2 * T // SLAB - 1
EMPTY = 1 << 20

WIDTHS = dict(gq=256, gk=256, gv=512, glow=16, gr=512, hq=512, hf=512, hi=512, hg=512,
              sz=1024, sxbc=2048, sdt=16, gates=3072)
COL = {}
_at = 0
for _name, _w in WIDTHS.items():
    COL[_name] = _at
    _at += _w
IN_W = _at


def semaphores(nc, ctx):
    made = []

    def clear():
        numbers = sorted(s.num for s in made)
        first = [n for n in numbers if n - 1 not in numbers]
        last = [n for n in numbers if n + 1 not in numbers]
        for a, z in zip(first, last):
            nc.gpsimd.sem_clear(range(a, z + 1))
        nc.all_engine_barrier()
    ctx.callback(clear)

    def sem(name):
        made.append(ctx.enter_context(nc.semaphore(name)))
        return made[-1]
    return sem


PAIR = 256
FIRST_PAIR = COL["gr"]


class Chain:

    def __init__(self, eng, sem):
        self.eng, self.sem, self.base, self.n = eng, sem, 0, 0

    def link(self, ins):
        self.n += 1
        ins.then_inc(self.sem, 1)
        self.eng.wait_ge(self.sem, self.base + self.n)

    def turn(self, i, each):
        self.base, self.n = i * each, 0


def wait_past(eng, sem, value):
    if not isinstance(value, int) or value > 0:
        eng.wait_ge(sem, value)


def norm1_and_decays(nc, io, dr, ident, h_hi, h_lo, w_raw, w_hi, w_lo):
    HF_T = WIDTHS["hf"] // P
    GK_T = GLA_HEADS * GLA_DK // P
    DT = 32
    N_CHAIN = 1 + HF_T + GK_T
    N_PAR = 6
    PAIRS = [COL["hf"], COL["hf"] + PAIR, COL["gq"], COL["gk"], FIRST_PAIR]
    QK_T = 2 * PAIR // P
    with ExitStack() as ctx:
        sb = lambda name, shape, dt=F32: ctx.enter_context(nc.sbuf_tensor(name, shape, dt))
        sem = semaphores(nc, ctx)
        x_in = [sb(f"x_in{b}", [P, D]) for b in range(2)]
        x_n = [sb(f"x_n{b}", [P, D]) for b in range(2)]
        h_f = sb("h_f", [P, KT, CH])
        v_raw = sb("va_raw", [P, KT, P])
        v_hi = sb("va_hi", [P, KT, P], F32R)
        v_lo = sb("va_lo", [P, KT, P], F32R)
        xs = [sb(f"xs{b}", [P, T]) for b in range(2)]
        ab = [sb(f"ab{b}", [P, T]) for b in range(2)]
        ld = [sb(f"ld{b}", [P, T]) for b in range(2)]
        cum = [sb(f"cum{b}", [P, T]) for b in range(2)]
        keys = [sb(f"keys{b}", [P, T]) for b in range(2)]
        seg0 = sb("seg0", [P, T])
        norm_w = sb("norm_w", [P, KT])
        stat = sb("stat", [P, NCH, 2])
        gk_up = sb("gk_up", [GLA_RANK, GLA_HEADS * GLA_DK])
        gk_bias = sb("gk_bias", [P, GK_T])
        dt_bias = sb("dt_bias", [64, 1])
        a_neg = sb("a_neg", [64, 1])
        lb_in = sb("lb_in", [P, HF_T])
        lb = sb("lb", [P, 6, HF_T])
        cst = sb("cst", [P, 2])
        glow = sb("glow", [GLA_RANK, T])
        acc = [ctx.enter_context(nc.psum_tensor(f"acc{b}", [P, T], F32)) for b in range(3)]
        tr = ctx.enter_context(nc.psum_tensor("tr", [P, T], F32))

        ident0 = sem("ident0")
        ident_ready = sem("ident_ready")
        c_ready = sem("c_ready")
        v_zero = sem("v_zero")
        seg_ready = sem("seg_ready")
        par_in = sem("par_in")
        x_loaded = [sem(f"x_loaded{b}") for b in range(2)]
        rstd_ready = sem("rstd_ready")
        xn_ready = sem("xn_ready")
        xT_ready = sem("xT_ready")
        h_ready = sem("h_ready")
        v_loaded = sem("v_loaded")
        w_loaded = [sem(f"w_loaded{b}") for b in range(2)]
        v_split = sem("v_split")
        w_split = sem("w_split")
        mm_done = sem("mm_done")
        acc_free = sem("acc_free")
        glow_ready = sem("glow_ready")
        abs_ready = sem("abs_ready")
        log1p_ready = sem("log1p_ready")
        karg_ready = sem("karg_ready")
        keys_ready = sem("keys_ready")
        cum_ready = sem("cum_ready")
        aneg_ready = sem("aneg_ready")
        lbarg_ready = sem("lbarg_ready")
        lbexp_ready = sem("lbexp_ready")
        oml_ready = sem("oml_ready")
        keybias_ready = sem("keybias_ready")
        cum_stored = [sem(f"cum_stored{b}") for b in range(2)]
        keys_stored = [sem(f"keys_stored{b}") for b in range(2)]
        dt_stored = sem("dt_stored")
        qk_ready = sem("qk_ready")
        qk_stored = [sem(f"qk_stored{b}") for b in range(2)]
        dve_own = sem("dve_own")
        act_own = sem("act_own")
        pool_own = sem("pool_own")
        block = ctx.enter_context(nc.Block())

        @block.sync
        def _(sp):
            def weights(i):
                if i >= 2:
                    sp.wait_ge(w_split, i - 1)
                sp.dma_start(w_raw[i % 2][:], io["w_in"][:, PAIRS[i]:PAIRS[i] + PAIR]
                             .rearrange("(k p) n -> p k n", p=P)).then_inc(w_loaded[i % 2], 16)

            for c in range(NCH):
                if c >= 2:
                    sp.wait_ge(xn_ready, c - 1)
                sp.dma_start(x_in[c % 2][:], io["x"][c * CH:(c + 1) * CH, :]).then_inc(x_loaded[c % 2], 16)
                if c == 1:
                    sp.dma_start(norm_w[:], io["norm1_w"].rearrange("(k p) -> p k", p=P)).then_inc(par_in, 16)
                    sp.dma_start(gk_up[:], io["gla_gk_up"]).then_inc(par_in, 16)
                    sp.dma_start(gk_bias[:], io["gla_gk_bias"].rearrange("(k p) -> p k", p=P)).then_inc(par_in, 16)
                    sp.dma_start(dt_bias[DT:DT + 16, :], io["ssm_dt_bias"].rearrange("(p a) -> p a", a=1)).then_inc(par_in, 16)
                    sp.dma_start(a_neg[DT:DT + 16, :], io["ssm_a_log"].rearrange("(p a) -> p a", a=1)).then_inc(par_in, 16)
                    sp.dma_start(lb_in[:], io["hgrn_lb_logits"].rearrange("(k p) -> p k", p=P)).then_inc(par_in, 16)
                    sp.wait_ge(v_zero, 1)
                    for at, name in ((0, "glow"), (DT, "sdt")):
                        sp.dma_start(v_raw[:, :, at:at + 16], io["w_in"][:, COL[name]:COL[name] + 16]
                                     .rearrange("(k p) n -> p k n", p=P)).then_inc(v_loaded, 16)
                    for i in range(2):
                        weights(i)
            for i in range(2, len(PAIRS)):
                weights(i)
            sp.wait_ge(cum_ready, 1)
            sp.dma_start(dr["b_ssm"], cum[0][DT:DT + 16, :]).then_inc(cum_stored[0], 16)
            sp.dma_start(dr["dt"], ld[0][DT:DT + 16, :]).then_inc(dt_stored, 16)
            for q in range(1, N_CHAIN):
                if q <= HF_T:
                    sp.wait_ge(keys_ready, q)
                    sp.dma_start(dr["k_hg"][(q - 1) * P:q * P, :], keys[q % 2][:]).then_inc(keys_stored[q % 2], 16)
                sp.wait_ge(cum_ready, q + 1)
                row = (GK_T + q - 1) * P if q <= HF_T else (q - 1 - HF_T) * P
                sp.dma_start(dr["cum"][row:row + P, :], cum[q % 2][:]).then_inc(cum_stored[q % 2], 16)
            sp.wait_ge(cum_stored[0], 16 * ((N_CHAIN + 1) // 2))
            sp.wait_ge(cum_stored[1], 16 * (N_CHAIN // 2))
            sp.wait_ge(keys_stored[0], 16 * (HF_T // 2))
            sp.wait_ge(keys_stored[1], 16 * (HF_T // 2))
            sp.wait_ge(dt_stored, 16)

        @block.gpsimd
        def _(pool):
            nc.gpsimd.memset(ident[:], 0.0).then_inc(ident0, 1)
            pool.wait_ge(ident0, 1)
            nc.gpsimd.affine_select(out=ident[:], in_=ident[:], compare_op=ALU.not_equal, fill=1.0, base=0,
                                    pattern=[[-1, P]], channel_multiplier=1).then_inc(ident_ready, 1)
            nc.gpsimd.memset(v_raw[:], 0.0).then_inc(v_zero, 1)
            nc.gpsimd.memset(seg0[:], 1.0).then_inc(pool_own, 1)
            pool.wait_ge(pool_own, 1)
            nc.gpsimd.memset(seg0[:, 0:T:CH], 0.0).then_inc(seg_ready, 1)
            pool.wait_ge(v_loaded, 32)
            nc.gpsimd.tensor_copy(v_hi[:], v_raw[:]).then_inc(pool_own, 1)
            pool.wait_ge(pool_own, 2)
            nc.gpsimd.tensor_tensor(v_lo[:], v_raw[:], v_hi[:].bitcast(F32), ALU.subtract).then_inc(v_split, 1)
            for i in range(len(PAIRS)):
                b = i % 2
                pool.wait_ge(w_loaded[b], 16 * (i // 2 + 1))
                if i >= 2:
                    pool.wait_ge(mm_done, (3, 5, N_CHAIN + 2)[i - 2])
                nc.gpsimd.tensor_copy(w_hi[b][:], w_raw[b][:]).then_inc(pool_own, 1)
                pool.wait_ge(pool_own, 3 + i)
                nc.gpsimd.tensor_tensor(w_lo[b][:], w_raw[b][:], w_hi[b][:].bitcast(F32), ALU.subtract).then_inc(w_split, 1)

        @block.scalar
        def _(act):
            own = Chain(act, act_own)
            nc.scalar.preload_act_table_set(EXP_LN_SET)
            act.wait_ge(c_ready, 2)
            for c in range(NCH):
                act.wait_ge(x_loaded[c % 2], 16 * (c // 2 + 1))
                if c >= 2:
                    act.wait_ge(xT_ready, c - 1)
                own.link(nc.scalar.activation(x_n[c % 2][:], x_in[c % 2][:], ACT.Square, accum_out=stat[:, c, 0:1]))
                own.link(nc.scalar.activation(stat[:, c, 0:1], stat[:, c, 0:1], ACT.Ln, scale=1.0 / D, bias=cst[:, 0:1]))
                nc.scalar.activation(stat[:, c, 1:2], stat[:, c, 0:1], ACT.Exp, scale=-0.5).then_inc(rstd_ready, 1)
            act.wait_ge(par_in, 16 * N_PAR)
            own.link(nc.scalar.activation(a_neg[DT:DT + 16, :], a_neg[DT:DT + 16, :], ACT.Exp))
            nc.scalar.mul(a_neg[DT:DT + 16, :], a_neg[DT:DT + 16, :], -1.0).then_inc(aneg_ready, 1)
            act.wait_ge(lbarg_ready, 1)
            nc.scalar.activation(lb[:, 1, :], lb[:, 0, :], ACT.Exp).then_inc(lbexp_ready, 1)
            act.wait_ge(oml_ready, 1)
            nc.scalar.activation(lb[:, 4, :], lb[:, 3, :], ACT.Ln).then_inc(lbexp_ready, 1)
            for q in range(N_CHAIN):
                b = q % 2
                view = ab[b][DT:DT + 16, :] if q == 0 else ab[b][:]
                one = cst[DT:DT + 16, 1:2] if q == 0 else cst[:, 1:2]
                act.wait_ge(abs_ready, q + 1)
                own.link(nc.scalar.activation(view, view, ACT.Exp))
                nc.scalar.activation(view, view, ACT.Ln, bias=one).then_inc(log1p_ready, 1)
                if 1 <= q <= HF_T:
                    act.wait_ge(karg_ready, q)
                    act.wait_ge(keybias_ready, 1)
                    if q >= 3:
                        act.wait_ge(keys_stored[b], 16 * ((q - 1) // 2))
                    nc.scalar.activation(keys[b][:], keys[b][:], ACT.Exp, bias=lb[:, 5, q - 1:q]).then_inc(keys_ready, 1)
            for g in range(QK_T):
                act.wait_ge(mm_done, N_CHAIN + g + 1)
                if g >= 2:
                    act.wait_ge(qk_stored[g % 2], 16 * (g // 2))
                nc.scalar.activation(x_n[g % 2][:], acc[(N_CHAIN + g) % 3][:], ACT.Copy,
                                     scale=1.0 if g < QK_T // 2 else GLA_DK ** -0.5).then_inc(qk_ready, 1)
                act.wait_ge(qk_ready, g + 1)
                act.dma_start(dr["qk"][g * P:(g + 1) * P, :], x_n[g % 2][:]).then_inc(qk_stored[g % 2], 16)
            for b in range(2):
                act.wait_ge(qk_stored[b], 16 * QK_T // 2)

        @block.vector
        def _(dve):
            own = Chain(dve, dve_own)
            nc.vector.memset(cst[:, 0:1], EPS).then_inc(c_ready, 1)
            nc.vector.memset(cst[:, 1:2], 1.0).then_inc(c_ready, 1)

            def normalise(c):
                dve.wait_ge(rstd_ready, c + 1)
                nc.vector.tensor_scalar(x_n[c % 2][:], x_in[c % 2][:], stat[:, c, 1:2], None, ALU.mult).then_inc(xn_ready, 1)

            def split(c):
                dve.wait_ge(xT_ready, c + 1)
                own.link(nc.vector.tensor_tensor(h_f[:], tr[:].rearrange("p (k t) -> p k t", t=CH),
                                                 norm_w[:].unsqueeze(2).to_broadcast([P, KT, CH]), ALU.mult))
                own.link(nc.vector.tensor_copy(h_hi[:, :, c * CH:(c + 1) * CH], h_f[:]))
                nc.vector.tensor_tensor(h_lo[:, :, c * CH:(c + 1) * CH], h_f[:],
                                        h_hi[:, :, c * CH:(c + 1) * CH].bitcast(F32), ALU.subtract).then_inc(h_ready, 1)

            normalise(0)
            dve.wait_ge(par_in, 16 * N_PAR)
            for c in range(NCH):
                if c + 1 < NCH:
                    normalise(c + 1)
                split(c)
            own.link(nc.vector.tensor_tensor(lb[:, 0, :], lb_in[:], lb_in[:], ALU.subtract))
            nc.vector.tensor_copy(lb[:, 0, :], lb[:, 0, :]).then_inc(lbarg_ready, 1)
            dve.wait_ge(lbexp_ready, 1)
            own.link(nc.vector.reciprocal(lb[:, 2, :], lb[:, 1, :]))
            own.link(nc.vector.tensor_tensor(lb[:, 1, :], lb[:, 1, :], lb[:, 2, :], ALU.mult))
            own.link(nc.vector.tensor_tensor(lb[:, 2, :], lb[:, 1, :], lb[:, 1, :], ALU.subtract))
            nc.vector.tensor_scalar(lb[:, 3, :], lb[:, 2, :], -1.0, 1.0, ALU.mult, ALU.add).then_inc(oml_ready, 1)
            dve.wait_ge(lbexp_ready, 2)
            nc.vector.tensor_scalar_add(lb[:, 5, :], lb[:, 4, :], math.log(HG_DIM ** -0.5)).then_inc(keybias_ready, 1)
            dve.wait_ge(seg_ready, 1)
            dve.wait_ge(aneg_ready, 1)

            def to_abs(q):
                b = q % 2
                dve.wait_ge(mm_done, q + 1)
                if q >= 2:
                    dve.wait_ge(cum_ready, q - 1)
                if q == 0:
                    own.link(nc.vector.tensor_copy(glow[:], acc[0][0:GLA_RANK, :]))
                    r = slice(DT, DT + 16)
                    nc.vector.tensor_scalar(xs[b][r, :], acc[0][r, :], dt_bias[r, :], None, ALU.add).then_inc(acc_free, 1)
                    dve.wait_ge(acc_free, 1)
                else:
                    r = slice(0, P)
                    if q <= HF_T:
                        nc.vector.tensor_copy(xs[b][:], acc[q % 3][:]).then_inc(acc_free, 1)
                    else:
                        nc.vector.tensor_scalar(xs[b][:], acc[q % 3][:], gk_bias[:, q - HF_T - 1:q - HF_T], None,
                                                ALU.add).then_inc(acc_free, 1)
                    dve.wait_ge(acc_free, q + 1)
                nc.vector.scalar_tensor_tensor(ab[b][r, :], xs[b][r, :], -1.0, xs[b][r, :], ALU.mult, ALU.min).then_inc(abs_ready, 1)

            to_abs(0)
            for q in range(N_CHAIN):
                b = q % 2
                if q + 1 < N_CHAIN:
                    to_abs(q + 1)
                dve.wait_ge(log1p_ready, q + 1)
                if q >= 2:
                    dve.wait_ge(cum_stored[b], 16 * (q // 2))
                if q == 2:
                    dve.wait_ge(dt_stored, 16)
                if q == 0:
                    r = slice(DT, DT + 16)
                    own.link(nc.vector.scalar_tensor_tensor(ld[b][r, :], xs[b][r, :], 0.0, ab[b][r, :], ALU.max, ALU.add))
                    own.link(nc.vector.tensor_scalar(xs[b][r, :], ld[b][r, :], a_neg[r, :], None, ALU.mult))
                    nc.vector.tensor_tensor_scan(cum[b][r, :], seg0[r, :], xs[b][r, :], 0.0, ALU.mult, ALU.add).then_inc(cum_ready, 1)
                    continue
                own.link(nc.vector.scalar_tensor_tensor(ld[b][:], xs[b][:], 0.0, ab[b][:], ALU.min, ALU.subtract))
                if q <= HF_T:
                    if q >= 3:
                        dve.wait_ge(keys_stored[b], 16 * ((q - 1) // 2))
                    nc.vector.tensor_tensor(keys[b][:], ld[b][:], xs[b][:], ALU.subtract).then_inc(karg_ready, 1)
                    own.link(nc.vector.tensor_scalar(ld[b][:], ld[b][:], lb[:, 4, q - 1:q], None, ALU.add))
                else:
                    own.link(nc.vector.tensor_scalar(ld[b][:], ld[b][:], 1.0 / GLA_TEMP, None, ALU.mult))
                nc.vector.tensor_tensor_scan(cum[b][:], seg0[:], ld[b][:], 0.0, ALU.mult, ALU.add).then_inc(cum_ready, 1)

        @block.tensor
        def _(pe):
            pe.wait_ge(ident_ready, 1)
            for c in range(NCH):
                pe.wait_ge(xn_ready, c + 1)
                if c >= 1:
                    pe.wait_ge(h_ready, c)
                for k in range(KT):
                    ins = nc.tensor.transpose(tr[:, k * P:(k + 1) * P], x_n[c % 2][:, k * P:(k + 1) * P], ident[:])
                ins.then_inc(xT_ready, 1)
            pe.wait_ge(h_ready, NCH)

            def tile(q, hi, lo):
                for k in range(KT):
                    for w, h in ((hi, h_hi), (hi, h_lo), (lo, h_hi)):
                        for half in range(2):
                            hs = slice(half * 512, half * 512 + 512)
                            ins = nc.tensor.matmul(acc[q % 3][:, hs], w[:, k, :], h[:, k, hs],
                                                   start=k == 0 and w is hi and h is h_hi,
                                                   stop=k == KT - 1 and w is lo, skip_group_check=True)
                ins.then_inc(mm_done, 1)

            pe.wait_ge(v_split, 1)
            tile(0, v_hi, v_lo)

            def pair(i, q):
                pe.wait_ge(w_split, i + 1)
                for a in range(2):
                    if q + a >= 3:
                        pe.wait_ge(acc_free, min(q + a - 2, N_CHAIN))
                    if q + a - 3 >= N_CHAIN:
                        pe.wait_ge(qk_ready, q + a - 2 - N_CHAIN)
                    ws = slice(a * P, (a + 1) * P)
                    tile(q + a, w_hi[i % 2][:, :, ws], w_lo[i % 2][:, :, ws])

            for i in range(HF_T // 2):
                pair(i, 1 + 2 * i)
            for g in range(GK_T):
                q = 1 + HF_T + g
                pe.wait_ge(acc_free, q - 2)
                for half in range(2):
                    hs = slice(half * 512, half * 512 + 512)
                    ins = nc.tensor.matmul(acc[q % 3][:, hs], gk_up[:, g * P:(g + 1) * P], glow[:, hs], start=True, stop=True)
                ins.then_inc(mm_done, 1)
            for i in range(QK_T // 2):
                pair(HF_T // 2 + i, N_CHAIN + 2 * i)


def project(nc, io, dr, h_hi, h_lo, w_raw, w_hi, w_lo):
    HEAD = [(FIRST_PAIR, "silu", dr["silu_a"][0:PAIR]), (FIRST_PAIR + PAIR, "silu", dr["silu_a"][PAIR:2 * PAIR])]
    LOOPS = [(COL["hq"], 2, "silu", dr["silu_a"][512:1024]),
             (COL["hg"], 6, "silu", dr["silu_b"]),
             (COL["gv"], 2, "tokens", dr["v"][:, 0:512]),
             (COL["hi"], 2, "tokens", dr["v"][:, 512:1024]),
             (COL["sxbc"], 8, "conv", dr["xbc"]),
             (COL["gates"], 12, "copy", dr["gates"])]
    PAD = SSM_CONV - 1
    TAPS = SSM_CONV + 1
    N_STEPS = len(HEAD) + sum(n for _, n, _, _ in LOOPS)
    with ExitStack() as ctx:
        sb = lambda name, shape, dt=F32: ctx.enter_context(nc.sbuf_tensor(name, shape, dt))
        sem = semaphores(nc, ctx)
        out = [sb(f"out{b}", [P, 2 * T]) for b in range(2)]
        u = [sb(f"u{b}", [P, 2, T + PAD]) for b in range(2)]
        tap = sb("tap", [P, 2, T])
        taps = [sb(f"taps{b}", [P, 2, TAPS]) for b in range(2)]
        ps = [ctx.enter_context(nc.psum_tensor(f"ps{b}", [P, 2 * T], F32)) for b in range(2)]
        w_loaded = [sem(f"w_loaded{b}") for b in range(2)]
        taps_loaded = [sem(f"taps_loaded{b}") for b in range(2)]
        hi_ready = sem("hi_ready")
        split_ready = sem("split_ready")
        mm_done = sem("mm_done")
        out_ready = sem("out_ready")
        stored = [sem(f"stored{b}") for b in range(2)]
        pad_ready = sem("pad_ready")
        u_ready = sem("u_ready")
        conv_ready = sem("conv_ready")
        passed = sem("passed")
        dve_own = sem("dve_own")
        block = ctx.enter_context(nc.Block())

        def steps(eng, body):
            for t, (col, kind, dram) in enumerate(HEAD):
                body(t, t % 2, 0, t // 2, col, kind, dram)
            t0 = len(HEAD)
            for col, n, kind, dram in LOOPS:
                with eng.Fori(0, n // 2) as i:
                    for b in range(2):
                        body(2 * i + (t0 + b), b, 2 * i + b, i + t0 // 2, col, kind, dram)
                t0 += n

        def early(t, n):
            return isinstance(t, int) and t < n

        @block.sync
        def _(sp):
            def body(t, b, j, turn, col, kind, dram):
                if not early(t, 2):
                    wait_past(sp, split_ready, t - 2)
                if not early(t, 1):
                    sp.dma_start(w_raw[b][:], io["w_in"][:, bass.ds(j * PAIR + col, PAIR)]
                                 .rearrange("(k p) n -> p k n", p=P)).then_inc(w_loaded[b], 16)
                if kind == "conv":
                    sp.wait_ge(out_ready, t - 1)
                    sp.dma_start(taps[b][:], io["taps"][bass.ds(j * PAIR, PAIR), :]
                                 .rearrange("(a p) k -> p a k", p=P)).then_inc(taps_loaded[b], 16)
            steps(sp, body)

        @block.gpsimd
        def _(pool):
            def body(t, b, j, turn, col, kind, dram):
                if early(t, 1):
                    return
                wait_past(pool, w_loaded[b], 16 * turn + 16 * b)
                if not early(t, 2):
                    pool.wait_ge(mm_done, t - 1)
                pool.sem_inc(passed, 1)
                nc.gpsimd.tensor_copy(w_hi[b][:], w_raw[b][:]).then_inc(hi_ready, 1)
                pool.wait_ge(hi_ready, t)
                nc.gpsimd.tensor_tensor(w_lo[b][:], w_raw[b][:], w_hi[b][:].bitcast(F32), ALU.subtract).then_inc(split_ready, 1)
            steps(pool, body)

        @block.scalar
        def _(act):
            nc.scalar.preload_act_table(ACT.Silu)
            act.wait_ge(pad_ready, 1)

            def body(t, b, j, turn, col, kind, dram):
                act.wait_ge(mm_done, t + 1)
                if kind == "conv":
                    nc.scalar.copy(u[b][:, :, PAD:PAD + T], ps[b][:].rearrange("p (a t) -> p a t", t=T)).then_inc(u_ready, 1)
                    act.wait_ge(conv_ready, j + 1)
                if not early(t, 2):
                    act.wait_ge(stored[b], 16 * turn)
                if kind == "conv":
                    for a in range(2):
                        ins = nc.scalar.activation(out[b][:, a * T:(a + 1) * T], tap[:, a, :], ACT.Silu,
                                                   bias=taps[b][:, a, SSM_CONV:TAPS])
                elif kind == "silu":
                    ins = nc.scalar.activation(out[b][:], ps[b][:], ACT.Silu)
                else:
                    ins = nc.scalar.activation(out[b][:], ps[b][:], ACT.Copy)
                ins.then_inc(out_ready, 1)
                act.wait_ge(out_ready, t + 1)
                if kind == "tokens":
                    act.dma_start(dram[:, bass.ds(j * PAIR, PAIR)].rearrange("(c p) n -> p c n", p=P),
                                  out[b][:].rearrange("p (c n) -> p c n", n=PAIR)).then_inc(stored[b], 16)
                else:
                    act.dma_start(dram[bass.ds(j * PAIR, PAIR), :].rearrange("(a p) t -> p a t", p=P),
                                  out[b][:].rearrange("p (a t) -> p a t", t=T)).then_inc(stored[b], 16)
            steps(act, body)
            for b in range(2):
                act.wait_ge(stored[b], 16 * (N_STEPS // 2))

        @block.vector
        def _(dve):
            own = Chain(dve, dve_own)
            nc.vector.memset(u[0][:, :, 0:PAD], 0.0)
            nc.vector.memset(u[1][:, :, 0:PAD], 0.0).then_inc(pad_ready, 1)
            dve.wait_ge(pad_ready, 1)
            pairs, t0 = [(n, sum(m for _, m, _, _ in LOOPS[:q])) for q, (_, n, kind, _) in enumerate(LOOPS) if kind == "conv"][0]
            t0 += len(HEAD)
            with dve.Fori(0, pairs // 2) as i:
                own.turn(i, 2 * 2 * (SSM_CONV - 1))
                for b in range(2):
                    j = 2 * i + b
                    dve.wait_ge(u_ready, j + 1)
                    dve.wait_ge(taps_loaded[b], 16 * i + 16)
                    dve.wait_ge(out_ready, j + t0)
                    for k in range(SSM_CONV):
                        for a in range(2):
                            if k == 0:
                                ins = nc.vector.tensor_scalar(tap[:, a, :], u[b][:, a, 0:T], taps[b][:, a, 0:1], None, ALU.mult)
                            else:
                                ins = nc.vector.scalar_tensor_tensor(tap[:, a, :], u[b][:, a, k:k + T], taps[b][:, a, k:k + 1],
                                                                     tap[:, a, :], ALU.mult, ALU.add)
                            if k < SSM_CONV - 1:
                                own.link(ins) if a == 1 else ins.then_inc(own.sem, 1)
                                own.n += a == 0
                    ins.then_inc(conv_ready, 1)

        @block.tensor
        def _(pe):
            def body(t, b, j, turn, col, kind, dram):
                wait_past(pe, split_ready, t)
                if not early(t, 2):
                    if kind == "conv":
                        pe.wait_ge(out_ready, t - 1)
                    else:
                        pe.wait_ge(out_ready, t - 1)
                hi, lo = w_hi[b], w_lo[b]
                parts = ((hi, h_hi), (hi, h_lo), (lo, h_hi))
                if kind == "tokens":
                    for c in range(NCH):
                        for k in range(KT):
                            for n, (w, h) in enumerate(parts):
                                ins = nc.tensor.matmul(ps[b][:, c * PAIR:(c + 1) * PAIR], h[:, k, c * CH:(c + 1) * CH], w[:, k, :],
                                                       start=k == 0 and n == 0, stop=k == KT - 1 and n == 2)
                else:
                    for a in range(2):
                        for k in range(KT):
                            for n, (w, h) in enumerate(parts):
                                for half in range(2):
                                    ins = nc.tensor.matmul(ps[b][:, a * T + half * 512:a * T + half * 512 + 512],
                                                           w[:, k, a * P:(a + 1) * P], h[:, k, half * 512:half * 512 + 512],
                                                           start=k == 0 and n == 0, stop=k == KT - 1 and n == 2)
                ins.then_inc(mm_done, 1)
            steps(pe, body)


def mixers(nc, io, dr, ident):
    LEVELS = [64 >> n for n in range(7)]
    NL = len(LEVELS)
    NE = NL + 1
    NEV = NL + 2
    CT = 6
    QT = 8
    NH = GLA_HEADS + HG_HEADS
    N_LOADS = 17
    N_PAR = 5
    HALF = P // 2
    GH = SSM_HEADS // SSM_GROUPS

    with ExitStack() as ctx:
        sb = lambda name, shape, dt=F32: ctx.enter_context(nc.sbuf_tensor(name, shape, dt))
        sem = semaphores(nc, ctx)
        pair = lambda name, shape: [sb(f"{name}{b}", shape) for b in range(2)]
        q_in, k_in, b_in = pair("q_in", [P, QT, CH]), pair("k_in", [P, CT, CH]), pair("b_in", [P, CT, CH])
        v_in = pair("v_in", [P, NH, P])
        g_in = pair("g_in", [P, NH, CH])
        z_in, x_in, bc_in = pair("z_in", [P, 8, CH]), pair("xs_in", [P, 8, CH]), pair("bc_in", [P, 8, CH])
        bb_in = pair("bb_in", [P, SSM_HEADS, CH])
        eb_in = pair("eb_in", [P, 8, CH])
        tok_in = pair("tok_in", [P, 2, SSM_HEADS])
        dec = pair("dec", [P, CT * CH])
        ex = pair("ex", [P, CT * CH])
        k_lv = [sb(f"k_lv{n}", [P, CT * CH]) for n in range(NL)]
        q_lv = pair("q_lv", [P, QT * HALF])
        score = sb("score", [P, NH * CH])
        eb6 = sb("eb6", [P, CT, CH])
        q_dec = sb("q_dec", [P, QT, CH])
        k_dec = sb("k_dec", [P, CT, CH])
        kT = sb("kT", [P, CT, P])
        state = sb("state", [P, CT, P])
        sq = sb("sq", [P, 8 * CH])
        rs = sb("rs", [P, NH * CH])
        gw = sb("gw", [P, NH, CH])
        y_out = sb("y_out", [P, 2 * NH, CH])
        wmat = sb("wmat", [P, SSM_HEADS, CH])
        cbm = sb("cbm", [P, SSM_GROUPS, CH])
        xdt = sb("xdt", [P, SSM_HEADS, SSM_HD])
        xw = sb("xw", [P, SSM_HEADS, SSM_HD])
        bT = sb("bT", [P, SSM_GROUPS, P])
        hst = sb("hst", [P, SSM_HEADS, SSM_HD])
        yt = sb("yt", [P, 8, CH])
        xd = sb("xd", [P, 8, CH])
        wd = pair("wd", [P, 3, SSM_HEADS])
        rs2 = sb("rs2", [P, SSM_GROUPS, CH])
        mask_f = sb("mask_f", [P, HALF])
        mask = [sb(f"mask{n}", [P, NH * HALF], U8) for n in range(NL)]
        mask_d = sb("mask_d", [P, 4 * CH], U8)
        tri = sb("tri", [P, SSM_GROUPS, CH])
        mean_a = sb("mean_a", [P, P])
        mean_b = sb("mean_b", [P, P])
        eps = sb("eps", [P, 1])
        nw = sb("nw", [P, NH])
        nw_s = sb("nw_s", [P, 8])
        d_col = sb("d_col", [P, 8])
        psum = ctx.enter_context(nc.psum_tensor("psum", [P, 8, 512], F32))
        two = lambda n: psum[:, n:n + 2, :].rearrange("p a b -> p (a b)")
        sc_ps = [psum[:, 0, :], psum[:, 1, :]]
        inter_ps = two(0)
        mid_ps = two(2)
        o_ps = two(4)
        cb_ps, bT_ps, intra_ps = psum[:, 6, :], psum[:, 7, :], two(6)

        loaded = [sem(f"loaded{b}") for b in range(2)]
        par_in = sem("par_in")
        mask_sem = sem("mask_sem")
        mask_ready = sem("mask_ready")
        q_zeroed = sem("q_zeroed")
        zeroed = sem("zeroed")
        const_ready = sem("const_ready")
        d_ready = sem("d_ready")
        e_ready = sem("e_ready")
        qk_ready = sem("qk_ready")
        sc_ready = sem("sc_ready")
        score_ready = sem("score_ready")
        eb6_ready = sem("eb6_ready")
        state_ready = sem("state_ready")
        kT_ps_ready = sem("kT_ps_ready")
        kT_ready = sem("kT_ready")
        o_ready = sem("o_ready")
        upd_ready = sem("upd_ready")
        sq_ready = sem("sq_ready")
        ms_ready = sem("ms_ready")
        ms_read = sem("ms_read")
        rs_ready = sem("rs_ready")
        gw_ready = sem("gw_ready")
        o_used = sem("o_used")
        ya_ready = sem("ya_ready")
        yb_ready = sem("yb_ready")
        ya_stored = sem("ya_stored")
        yb_stored = sem("yb_stored")
        seg_ready = sem("seg_ready")
        wexp_ready = sem("wexp_ready")
        cb_ready = sem("cb_ready")
        cbm_ready = sem("cbm_ready")
        w_ready = sem("w_ready")
        xT_ready = sem("xT_ready")
        xdt_ready = sem("xdt_ready")
        bT_ps_ready = sem("bT_ps_ready")
        bT_ready = sem("bT_ready")
        wdarg_ready = sem("wdarg_ready")
        small_ready = sem("small_ready")
        xw_ready = sem("xw_ready")
        xd_ready = sem("xd_ready")
        intra_ready = sem("intra_ready")
        inter_ready = sem("inter_ready")
        inter_used = sem("inter_used")
        intra_used = sem("intra_used")
        yt_ready = sem("yt_ready")
        sq2_ready = sem("sq2_ready")
        ms2_ready = sem("ms2_ready")
        ms2_read = sem("ms2_read")
        rs2_ready = sem("rs2_ready")
        hupd_ready = sem("hupd_ready")
        hst_ready = sem("hst_ready")
        passed = sem("passed")
        dve_own = sem("dve_own")
        dve_tail = sem("dve_tail")
        act_own = sem("act_own")
        block = ctx.enter_context(nc.Block())

        E0, QK0 = 2, 2

        def chunks(eng, body):
            for c in range(2):
                body(c, c, 0)
            with eng.Fori(0, NCH // 2 - 1) as i:
                for b in range(2):
                    body(2 * i + (2 + b), b, i + 1)

        LAST = NCH - 1
        first = lambda c: isinstance(c, int) and c == 0

        @block.sync
        def _(sp):
            sp.dma_start(nw[:, 0:4], io["gla_norm_w"].rearrange("(k p) -> p k", p=P)).then_inc(par_in, 16)
            sp.dma_start(nw[:, 4:8], io["hgrn_norm_w"].rearrange("(k p) -> p k", p=P)).then_inc(par_in, 16)
            sp.dma_start(nw_s[:], io["ssm_norm_w"].rearrange("(k p) -> p k", p=P)).then_inc(par_in, 16)
            for a in range(2):
                sp.dma_start(d_col[a * HALF:(a + 1) * HALF, :], io["ssm_d"][a::2].unsqueeze(0).to_broadcast([HALF, 8]))\
                    .then_inc(par_in, 16)

            def load(c, b):
                t = bass.ds(c * CH, CH)
                tiles = lambda ap: ap[:, t].rearrange("(k p) t -> p k t", p=P)
                put = lambda dst, src: sp.dma_start(dst, src).then_inc(loaded[b], 16)
                put(b_in[b][:], tiles(dr["cum"]))
                gq = tiles(dr["qk"][0:256])
                for a in range(2):
                    r = slice(a * HALF, (a + 1) * HALF)
                    put(q_in[b][r, 2 * a:2 * a + 2, :], gq[r])
                put(q_in[b][:, 4:8, :], tiles(dr["silu_a"][512:1024]))
                put(k_in[b][:, 0:2, :], tiles(dr["qk"][256:512]))
                put(k_in[b][:, 2:6, :], tiles(dr["k_hg"]))
                put(bb_in[b][:], dr["b_ssm"][:, t].unsqueeze(0).to_broadcast([P, SSM_HEADS, CH]))
                put(tok_in[b][:, 0, :], dr["b_ssm"][:, t].rearrange("h t -> t h"))
                put(tok_in[b][:, 1, :], dr["dt"][:, t].rearrange("h t -> t h"))
                put(bc_in[b][:], tiles(dr["xbc"][1024:2048]))
                put(x_in[b][:], tiles(dr["xbc"][0:1024]))
                put(v_in[b][:], dr["v"][t, :].rearrange("t (h e) -> t h e", e=P))
                for a in range(2):
                    put(eb_in[b][a * HALF:(a + 1) * HALF, :, :], dr["b_ssm"][a::2, t].unsqueeze(0).to_broadcast([HALF, 8, CH]))
                put(g_in[b][:, 0:4, :], tiles(dr["silu_a"][0:512]))
                put(g_in[b][:, 4:8, :], tiles(dr["silu_b"][0:512]))
                put(z_in[b][:], tiles(dr["silu_b"][512:1536]))

            def store(c):
                t = bass.ds(c * CH, CH)
                sp.wait_ge(ya_ready, c + 1)
                sp.dma_start(dr["y"][0:1024, t].rearrange("(k p) t -> p k t", p=P), y_out[:, 0:8, :]).then_inc(ya_stored, 16)
                sp.wait_ge(yb_ready, c + 1)
                sp.dma_start(dr["y"][1024:2048, t].rearrange("(k p) t -> p k t", p=P), y_out[:, 8:16, :]).then_inc(yb_stored, 16)

            def used(c):
                sp.wait_ge(yt_ready, c + 1)
                sp.wait_ge(gw_ready, c + 1)

            sp.wait_ge(q_zeroed, 2)
            load(0, 0)
            load(1, 1)
            with sp.Fori(0, NCH // 2 - 1) as i:
                for b in range(2):
                    used(2 * i + b)
                    load(2 * i + (b + 2), b)
                    store(2 * i + b)
            store(LAST - 1)
            store(LAST)
            sp.wait_ge(ya_stored, 16 * NCH + 16)
            sp.wait_ge(yb_stored, 16 * NCH + 16)

        @block.gpsimd
        def _(pool):
            for b in range(2):
                nc.gpsimd.memset(q_in[b][:, 0:4, :], 0.0).then_inc(q_zeroed, 1)
            n = 0
            for lv, h in enumerate(LEVELS):
                nb = CH // (2 * h)
                if lv:
                    pool.wait_ge(mask_ready, lv)
                nc.gpsimd.memset(mask_f[:], 1.0).then_inc(mask_sem, 1)
                n += 1
                pool.wait_ge(mask_sem, n)
                view = mask_f[:].rearrange("p (n h) -> p n h", h=h)
                nc.gpsimd.affine_select(out=view, in_=view, compare_op=ALU.is_ge, fill=0.0, base=0,
                                        pattern=[[-2 * h, nb], [0, h]], channel_multiplier=1).then_inc(mask_sem, 1)
                n += 1
                pool.wait_ge(mask_sem, n)
                nc.gpsimd.affine_select(out=view, in_=view, compare_op=ALU.is_ge, fill=0.0, base=h - 1,
                                        pattern=[[2 * h, nb], [0, h]], channel_multiplier=-1).then_inc(mask_sem, 1)
                n += 1
            nc.gpsimd.memset(tri[:], 1.0).then_inc(zeroed, 1)
            pool.wait_ge(zeroed, 1)
            nc.gpsimd.affine_select(out=tri[:], in_=tri[:], compare_op=ALU.is_ge, fill=0.0, base=0,
                                    pattern=[[0, SSM_GROUPS], [1, CH]], channel_multiplier=-1).then_inc(const_ready, 1)
            nc.gpsimd.memset(mean_a[:], 1.0 / GLA_DV).then_inc(const_ready, 1)
            nc.gpsimd.memset(mean_b[:], 1.0 / 256).then_inc(const_ready, 1)
            for n in range(NL):
                nc.gpsimd.memset(k_lv[n][:], 0.0).then_inc(const_ready, 1)
            pool.wait_ge(par_in, 16 * N_PAR)

            def body(c, b, turn):
                pool.wait_ge(loaded[b], 16 * N_LOADS * turn + 16 * N_LOADS)
                for lv, h in enumerate(LEVELS):
                    pool.wait_ge(e_ready, NE * c + (lv - 1 + E0))
                    view = b_in[b][:].rearrange("p a (n w) -> p (a n) w", w=2 * h)
                    at_m = view[:, :, h - 1:h].to_broadcast([P, CT * CH // (2 * h), 2 * h])
                    nc.gpsimd.tensor_tensor(dec[lv % 2][:].rearrange("p (n w) -> p n w", w=2 * h), view, at_m,
                                            ALU.subtract).then_inc(d_ready, 1)
                pool.wait_ge(e_ready, NE * c + (NL - 1 + E0))
                nc.gpsimd.tensor_tensor(dec[NL % 2][:].rearrange("p (a w) -> p a w", w=CH),
                                        b_in[b][:, :, CH - 1:CH].to_broadcast([P, CT, CH]), b_in[b][:],
                                        ALU.subtract).then_inc(d_ready, 1)
                pool.wait_ge(wexp_ready, c + 1)
                pool.wait_ge(cbm_ready, c + 1)
                w4 = wmat[:].rearrange("p (g r) t -> p g r t", r=GH)
                nc.gpsimd.tensor_tensor(w4, w4, cbm[:].unsqueeze(2).to_broadcast([P, SSM_GROUPS, GH, CH]),
                                        ALU.mult).then_inc(w_ready, 1)
                pool.wait_ge(small_ready, c + 1)
                pool.wait_ge(xdt_ready, c + 1)
                wait_past(pool, hupd_ready, c)
                nc.gpsimd.tensor_tensor(xw[:], xdt[:], wd[b][:, 1, :].unsqueeze(2).to_broadcast([P, SSM_HEADS, SSM_HD]),
                                        ALU.mult).then_inc(xw_ready, 1)
                wait_past(pool, yt_ready, c)
                nc.gpsimd.tensor_tensor(xd[:], x_in[b][:], d_col[:].unsqueeze(2).to_broadcast([P, 8, CH]),
                                        ALU.mult).then_inc(xd_ready, 1)
                wait_past(pool, ya_ready, c)
                nc.gpsimd.tensor_tensor(gw[:], g_in[b][:], nw[:].unsqueeze(2).to_broadcast([P, NH, CH]),
                                        ALU.mult).then_inc(gw_ready, 1)
            chunks(pool, body)

        @block.scalar
        def _(act):
            own = Chain(act, act_own)
            nc.scalar.preload_act_table_set(EXP_LN_SET)
            act.sem_inc(e_ready, E0)
            act.wait_ge(zeroed, 1)

            def gla_hgrn_scale(p):
                act.wait_ge(ms_ready, p + 1)
                nc.scalar.activation(rs[:], mid_ps, ACT.Ln, bias=eps[:]).then_inc(ms_read, 1)
                act.wait_ge(ms_read, p + 1)
                nc.scalar.activation(rs[:], rs[:], ACT.Exp, scale=-0.5).then_inc(rs_ready, 1)

            def squares(p):
                act.wait_ge(yt_ready, p + 1)
                nc.scalar.activation(sq[:], yt[:].rearrange("p k t -> p (k t)"), ACT.Square).then_inc(sq2_ready, 1)

            def scale(p):
                act.wait_ge(ms2_ready, p + 1)
                nc.scalar.activation(rs2[:].rearrange("p g t -> p (g t)"), mid_ps[:, 0:512], ACT.Ln, bias=eps[:]).then_inc(ms2_read, 1)
                act.wait_ge(ms2_read, p + 2)
                nc.scalar.activation(rs2[:], rs2[:], ACT.Exp, scale=-0.5).then_inc(rs2_ready, 1)

            def body(c, b, turn):
                def relative(lv):
                    h = LEVELS[lv]
                    act.wait_ge(d_ready, NE * c + (lv + 1))
                    act.wait_ge(qk_ready, NE * c + (lv - 1 + QK0))
                    d = dec[lv % 2][:].rearrange("p (n w) -> p n w", w=2 * h)
                    e = ex[lv % 2][:].rearrange("p (n w) -> p n w", w=2 * h)
                    nc.scalar.activation(e[:, :, 0:h], d[:, :, 0:h], ACT.Exp, scale=-1.0)
                    nc.scalar.activation(e[:, :, h:2 * h], d[:, :, h:2 * h], ACT.Exp).then_inc(e_ready, 1)

                relative(0)
                relative(1)
                if not first(c):
                    gla_hgrn_scale(c - 1)
                    squares(c - 1)
                relative(2)
                act.wait_ge(seg_ready, c + 1)
                nc.scalar.activation(wmat[:], wmat[:], ACT.Exp).then_inc(wexp_ready, 1)
                relative(3)
                act.wait_ge(wdarg_ready, c + 1)
                nc.scalar.activation(wd[b][:, 1, :], wd[b][:, 0, :], ACT.Exp)
                nc.scalar.activation(wd[b][:, 2, :], bb_in[b][:, :, CH - 1], ACT.Exp)
                nc.scalar.activation(eb_in[b][:], eb_in[b][:], ACT.Exp).then_inc(small_ready, 1)
                relative(4)
                if not first(c):
                    scale(c - 1)
                act.wait_ge(bT_ps_ready, c + 1)
                wait_past(act, hupd_ready, c)
                nc.scalar.copy(bT[:].rearrange("p g n -> p (g n)"), bT_ps).then_inc(bT_ready, 1)
                for lv in range(5, NL):
                    relative(lv)
                act.wait_ge(d_ready, NE * c + NE)
                act.wait_ge(qk_ready, NE * c + (NL - 1 + QK0))
                nc.scalar.activation(ex[NL % 2][:], dec[NL % 2][:], ACT.Exp).then_inc(e_ready, 1)
                act.wait_ge(state_ready, c + 1)
                nc.scalar.activation(eb6[:], b_in[b][:], ACT.Exp).then_inc(eb6_ready, 1)
                act.wait_ge(kT_ps_ready, c + 1)
                nc.scalar.copy(kT[:].rearrange("p a n -> p (a n)"), mid_ps[:, 0:CT * P]).then_inc(kT_ready, 1)
                act.wait_ge(o_ready, c + 1)
                nc.scalar.activation(sq[:], o_ps, ACT.Square).then_inc(sq_ready, 1)
            chunks(act, body)
            gla_hgrn_scale(LAST)
            squares(LAST)
            scale(LAST)

        @block.vector
        def _(dve):
            own, tail = Chain(dve, dve_own), Chain(dve, dve_tail)
            for s, n in ((qk_ready, QK0), (state_ready, 1), (intra_used, 1), (inter_used, 1), (hst_ready, 1),
                         (ms2_read, 1), (ya_stored, 16), (yb_stored, 16)):
                dve.sem_inc(s, n)
            own.link(nc.vector.memset(eps[:], EPS))
            own.link(nc.vector.memset(state[:], 0.0))
            own.link(nc.vector.memset(hst[:], 0.0))
            own.link(nc.vector.memset(score[:], 0.0))
            for lv in range(NL):
                dve.wait_ge(mask_sem, 3 * lv + 3)
                nc.vector.tensor_copy(mask[lv][:].rearrange("p (a h) -> p a h", h=HALF),
                                      mask_f[:].unsqueeze(1).to_broadcast([P, NH, HALF])).then_inc(mask_ready, 1)
            dve.wait_ge(mask_ready, NL)
            own.link(nc.vector.tensor_copy(mask_d[:].rearrange("p (a h) -> p a h", h=CH),
                                           ident[:].unsqueeze(1).to_broadcast([P, 4, CH])))
            dve.wait_ge(const_ready, 3 + NL)
            START = own.n

            def ssm_sum(p, b):
                tail.turn(p, TAIL_LINKS)
                dve.wait_ge(inter_used, p + 2)
                dve.wait_ge(intra_ready, p + 1)
                nc.vector.tensor_tensor(yt[:], intra_ps.rearrange("p (k t) -> p k t", t=CH), yt[:], ALU.add).then_inc(intra_used, 1)
                dve.wait_ge(intra_used, p + 2)
                dve.wait_ge(xd_ready, p + 1)
                tail.link(nc.vector.tensor_tensor(yt[:], yt[:], xd[:], ALU.add))
                nc.vector.tensor_tensor(yt[:], yt[:], z_in[b][:], ALU.mult).then_inc(yt_ready, 1)

            def gla_hgrn_out(p):
                dve.wait_ge(rs_ready, p + 1)
                dve.wait_ge(ya_stored, 16 * p + 16)
                ya = y_out[:, 0:8, :]
                nc.vector.tensor_tensor(ya, o_ps.rearrange("p (k t) -> p k t", t=CH), rs[:].rearrange("p (k t) -> p k t", t=CH),
                                        ALU.mult).then_inc(o_used, 1)
                dve.wait_ge(o_used, p + 1)
                dve.wait_ge(gw_ready, p + 1)
                nc.vector.tensor_tensor(ya, ya, gw[:], ALU.mult).then_inc(ya_ready, 1)

            def ssm_state(p, b):
                dve.wait_ge(hupd_ready, p + 1)
                tail.link(nc.vector.tensor_tensor(hst[:], hst[:], wd[b][:, 2, :].unsqueeze(2).to_broadcast([P, SSM_HEADS, SSM_HD]),
                                                  ALU.mult))
                nc.vector.tensor_tensor(hst[:], hst[:], o_ps.rearrange("p (h e) -> p h e", e=SSM_HD), ALU.add).then_inc(hst_ready, 1)

            def ssm_out(p):
                dve.wait_ge(rs2_ready, p + 1)
                dve.wait_ge(yb_stored, 16 * p + 16)
                yb = y_out[:, 8:16, :]
                tail.link(nc.vector.tensor_tensor(yb.rearrange("p (g a) t -> p g a t", a=2), yt[:].rearrange("p (g a) t -> p g a t", a=2),
                                                  rs2[:].unsqueeze(2).to_broadcast([P, SSM_GROUPS, 2, CH]), ALU.mult))
                nc.vector.tensor_tensor(yb, yb, nw_s[:].unsqueeze(2).to_broadcast([P, 8, CH]), ALU.mult).then_inc(yb_ready, 1)

            def body(c, b, turn):
                own.turn(c, LINKS)
                own.n = START
                dve.wait_ge(loaded[b], 16 * N_LOADS * turn + 16 * N_LOADS)
                def factors(lv):
                    h = LEVELS[lv]
                    dve.wait_ge(e_ready, NE * c + (lv + 1 + E0))
                    v = lambda x: x.rearrange("p (n w) -> p n w", w=2 * h)
                    k6 = v(k_in[b][:].rearrange("p a t -> p (a t)"))
                    q8 = q_in[b][:].rearrange("p a (n w) -> p a n w", w=2 * h)
                    e6 = ex[lv % 2][:].rearrange("p (a n w) -> p a n w", a=CT, w=2 * h)
                    ql = q_lv[lv % 2][:].rearrange("p (a n h) -> p a n h", a=QT, h=h)
                    nc.vector.tensor_tensor(v(k_lv[lv][:])[:, :, 0:h], k6[:, :, 0:h], v(ex[lv % 2][:])[:, :, 0:h], ALU.mult)
                    nc.vector.tensor_tensor(ql[:, 0:2], q8[:, 0:2, :, h:2 * h], e6[:, 0:2, :, h:2 * h], ALU.mult)
                    nc.vector.tensor_tensor(ql[:, 2:8], q8[:, 2:8, :, h:2 * h], e6[:, :, :, h:2 * h], ALU.mult).then_inc(qk_ready, 1)

                def scores_in(lv):
                    h = LEVELS[lv]
                    dve.wait_ge(sc_ready, NEV * c + (lv + 1))
                    if lv:
                        dve.wait_ge(score_ready, NEV * c + lv)
                    dve.sem_inc(passed, 1)
                    v = lambda x: x.rearrange("p (n h) -> p n h", h=h)
                    nc.vector.copy_predicated(score[:].rearrange("p (n w) -> p n w", w=2 * h)[:, :, h:2 * h],
                                              v(mask[lv][:]), v(sc_ps[lv % 2])).then_inc(score_ready, 1)

                def decay_args():
                    for h in range(SSM_HEADS):
                        ins = nc.vector.tensor_scalar(wmat[:, h, :], bb_in[b][:, h, :], tok_in[b][:, 0, h:h + 1], 0.0,
                                                      ALU.subtract, ALU.min)
                    ins.then_inc(seg_ready, 1)
                    nc.vector.tensor_tensor(wd[b][:, 0, :], bb_in[b][:, :, CH - 1], tok_in[b][:, 0, :], ALU.subtract)\
                        .then_inc(wdarg_ready, 1)

                def level(lv):
                    factors(lv)
                    scores_in(lv - 1)

                factors(0)
                if not first(c):
                    ssm_sum(c - 1, 1 - b)
                    gla_hgrn_out(c - 1)
                level(1)
                decay_args()
                level(2)
                dve.wait_ge(cb_ready, c + 1)
                nc.vector.tensor_tensor(cbm[:], cb_ps.rearrange("p (g t) -> p g t", t=CH), tri[:], ALU.mult).then_inc(cbm_ready, 1)
                level(3)
                if not first(c):
                    ssm_state(c - 1, 1 - b)
                level(4)
                level(5)
                dve.wait_ge(xT_ready, c + 1)
                nc.vector.tensor_tensor(xdt[:], mid_ps.rearrange("p (h e) -> p h e", e=SSM_HD),
                                        tok_in[b][:, 1, :].unsqueeze(2).to_broadcast([P, SSM_HEADS, SSM_HD]),
                                        ALU.mult).then_inc(xdt_ready, 1)
                if not first(c):
                    ssm_out(c - 1)
                level(6)
                dve.wait_ge(e_ready, NE * c + (NE + E0))
                nc.vector.tensor_tensor(k_dec[:], k_in[b][:], ex[NL % 2][:].rearrange("p (a t) -> p a t", t=CH), ALU.mult)\
                    .then_inc(qk_ready, 1)
                scores_in(NL - 1)
                dve.wait_ge(eb6_ready, c + 1)
                nc.vector.tensor_tensor(q_dec[:, 0:2, :], q_in[b][:, 0:2, :], eb6[:, 0:2, :], ALU.mult)
                own.link(nc.vector.tensor_tensor(q_dec[:, 2:8, :], q_in[b][:, 2:8, :], eb6[:], ALU.mult))
                for a in range(2):
                    dve.wait_ge(sc_ready, NEV * c + (NL + 1 + a))
                    dve.wait_ge(score_ready, NEV * c + (NL + a))
                    dve.sem_inc(passed, 1)
                    nc.vector.copy_predicated(score[:, a * 512:(a + 1) * 512], mask_d[:], sc_ps[a]).then_inc(score_ready, 1)
                dve.wait_ge(small_ready, c + 1)
                dve.wait_ge(inter_ready, c + 1)
                nc.vector.tensor_tensor(yt[:], inter_ps.rearrange("p (k t) -> p k t", t=CH), eb_in[b][:], ALU.mult).then_inc(inter_used, 1)
                dve.wait_ge(upd_ready, c + 1)
                own.link(nc.vector.tensor_tensor(state[:], state[:], eb6[:, :, CH - 1:CH].to_broadcast([P, CT, P]), ALU.mult))
                nc.vector.tensor_tensor(state[:], state[:], mid_ps[:, 0:CT * P].rearrange("p (a e) -> p a e", e=P), ALU.add)\
                    .then_inc(state_ready, 1)
                assert own.n - START == LINKS
            LINKS = 2
            TAIL_LINKS = 3
            chunks(dve, body)
            ssm_sum(LAST, LAST % 2)
            gla_hgrn_out(LAST)
            ssm_state(LAST, LAST % 2)
            ssm_out(LAST)

        @block.tensor
        def _(pe):
            pe.wait_ge(const_ready, 3 + NL)

            def ssm_state(p, b):
                pe.wait_ge(xw_ready, p + 1)
                pe.wait_ge(o_used, p + 1)
                for g in range(SSM_GROUPS):
                    ins = nc.tensor.matmul(o_ps[:, g * 256:(g + 1) * 256], bT[:, g, :], xw[:, g * GH:(g + 1) * GH, :], start=True, stop=True)
                ins.then_inc(hupd_ready, 1)

            def ssm_means(p):
                pe.wait_ge(sq2_ready, p + 1)
                pe.wait_ge(ms_read, p + 1)
                s2 = sq[:].rearrange("p (g a t) -> p a g t", a=2, t=CH)
                for a in range(2):
                    ins = nc.tensor.matmul(mid_ps[:, 0:512], mean_b[:], s2[:, a], start=a == 0, stop=a == 1)
                ins.then_inc(ms2_ready, 1)

            def body(c, b, turn):
                pe.wait_ge(loaded[b], 16 * N_LOADS * turn + 16 * N_LOADS)
                pe.wait_ge(intra_used, c + 1)
                for g in range(SSM_GROUPS):
                    ins = nc.tensor.matmul(cb_ps[:, g * CH:(g + 1) * CH], bc_in[b][:, g, :], bc_in[b][:, 4 + g, :], start=True, stop=True)
                ins.then_inc(cb_ready, 1)
                for g in range(SSM_GROUPS):
                    ins = nc.tensor.transpose(bT_ps[:, g * P:(g + 1) * P], bc_in[b][:, g, :], ident[:])
                ins.then_inc(bT_ps_ready, 1)
                def heads():
                    for h in range(GLA_HEADS):
                        yield h, h // 2 + 2 * (h % 2), h // 2, slice(HALF * (h % 2), HALF * (h % 2) + HALF)
                    for h in range(HG_HEADS):
                        yield GLA_HEADS + h, 4 + h, 2 + h, slice(0, P)

                pe.wait_ge(inter_used, c + 1)
                for lv in range(NL):
                    pe.wait_ge(qk_ready, NE * c + (lv + 1 + QK0))
                    if lv >= 2:
                        pe.wait_ge(score_ready, NEV * c + (lv - 1))
                    for h, qa, a, r in heads():
                        ins = nc.tensor.matmul(sc_ps[lv % 2][:, h * HALF:(h + 1) * HALF], k_lv[lv][:, a * CH:(a + 1) * CH],
                                               q_lv[lv % 2][:, qa * HALF:(qa + 1) * HALF], start=True, stop=True)
                    ins.then_inc(sc_ready, 1)
                    if lv == 1 and not first(c):
                        ssm_state(c - 1, 1 - b)
                    if lv == 3 and not first(c):
                        ssm_means(c - 1)
                    if lv == 4:
                        pe.wait_ge(ms2_read, c + 1)
                        for k in range(8):
                            ins = nc.tensor.transpose(mid_ps[:, k * P:(k + 1) * P], x_in[b][:, k, :], ident[:])
                        ins.then_inc(xT_ready, 1)
                for half in range(2):
                    pe.wait_ge(score_ready, NEV * c + NL)
                    for h, qa, a, r in heads():
                        if h // 4 == half:
                            ins = nc.tensor.matmul(sc_ps[half][:, (h % 4) * CH:(h % 4 + 1) * CH], k_in[b][:, a, :], q_in[b][:, qa, :],
                                                   start=True, stop=True)
                    ins.then_inc(sc_ready, 1)
                pe.wait_ge(qk_ready, NE * c + (NE + QK0))
                pe.wait_ge(xdt_ready, c + 1)
                for a in range(CT):
                    ins = nc.tensor.transpose(mid_ps[:, a * P:(a + 1) * P], k_dec[:, a, :], ident[:])
                ins.then_inc(kT_ps_ready, 1)
                pe.wait_ge(score_ready, NEV * c + NEV)
                pe.wait_ge(state_ready, c + 1)
                pe.wait_ge(hst_ready, c + 1)
                for h, qa, a, r in heads():
                    nc.tensor.matmul(o_ps[:, h * CH:(h + 1) * CH], v_in[b][:, h, :], score[:, h * CH:(h + 1) * CH], start=True, stop=False)
                    ins = nc.tensor.matmul(o_ps[:, h * CH:(h + 1) * CH], state[:, a, :], q_dec[:, qa, :], start=False, stop=True)
                ins.then_inc(o_ready, 1)
                hs = hst[:].rearrange("p h e -> p (h e)")
                for k in range(8):
                    ins = nc.tensor.matmul(inter_ps[:, k * CH:(k + 1) * CH], hs[:, k * P:(k + 1) * P], bc_in[b][:, 4 + k // 2, :],
                                           start=True, stop=True)
                ins.then_inc(inter_ready, 1)
                pe.wait_ge(kT_ready, c + 1)
                for h, qa, a, r in heads():
                    ins = nc.tensor.matmul(mid_ps[r, a * P:(a + 1) * P], kT[:, a, r], v_in[b][:, h, :], start=True, stop=True,
                                           skip_group_check=True)
                ins.then_inc(upd_ready, 1)
                pe.wait_ge(w_ready, c + 1)
                pe.wait_ge(bT_ready, c + 1)
                for h in range(SSM_HEADS):
                    r = slice(HALF * (h % 2), HALF * (h % 2) + HALF)
                    ins = nc.tensor.matmul(intra_ps[r, (h // 2) * CH:(h // 2 + 1) * CH], xdt[:, h, :], wmat[:, h, :], start=True, stop=True,
                                           skip_group_check=True)
                ins.then_inc(intra_ready, 1)
                pe.wait_ge(state_ready, c + 2)
                pe.wait_ge(sq_ready, c + 1)
                for half in range(2):
                    ins = nc.tensor.matmul(mid_ps[:, half * 512:(half + 1) * 512], mean_a[:], sq[:, half * 512:(half + 1) * 512],
                                           start=True, stop=True)
                ins.then_inc(ms_ready, 1)
            chunks(pe, body)
            ssm_state(LAST, LAST % 2)
            ssm_means(LAST)


def merge(nc, io, dr, m_hi, m_lo):
    HT = T // 2
    YK = 16
    BRANCH = ((0, 4), (4, 8), (8, 16))
    DM = D // P
    PIECES, PK = 8, YK // 8
    LINKS = 6
    with ExitStack() as ctx:
        sb = lambda name, shape, dt=F32: ctx.enter_context(nc.sbuf_tensor(name, shape, dt))
        sem = semaphores(nc, ctx)
        y_raw = [sb(f"y_raw{b}", [P, PK, HT]) for b in range(2)]
        y_hi = sb("y_hi", [P, YK, HT], F32R)
        y_lo = sb("y_lo", [P, YK, HT], F32R)
        w_raw = [sb(f"wb_raw{b}", [P, YK, P]) for b in range(2)]
        w_hi = [sb(f"wb_hi{b}", [P, YK, P], F32R) for b in range(2)]
        w_lo = [sb(f"wb_lo{b}", [P, YK, P], F32R) for b in range(2)]
        gate = [sb(f"gate{b}", [P, 3, HT]) for b in range(2)]
        part = sb("part", [P, 2, HT])
        ps = [ctx.enter_context(nc.psum_tensor(f"br{b}", [P, 3, HT], F32)) for b in range(2)]
        y_loaded = [sem(f"y_loaded{b}") for b in range(2)]
        y_hi_ready = sem("y_hi_ready")
        y_ready = sem("y_ready")
        w_loaded = [sem(f"w_loaded{b}") for b in range(2)]
        gate_loaded = [sem(f"gate_loaded{b}") for b in range(2)]
        w_hi_ready = sem("w_hi_ready")
        w_ready = sem("w_ready")
        gate_ready = sem("gate_ready")
        mm_done = sem("mm_done")
        merged_ready = sem("merged_ready")
        dve_own = sem("dve_own")
        block = ctx.enter_context(nc.Block())
        TWO = 2

        def tiles(eng, body):
            with eng.Fori(0, 2) as half:
                with eng.Fori(0, DM // 2) as i:
                    for b in range(2):
                        body(DM * half + 2 * i + b, b, half, 2 * i + b, (DM // 2) * half + i)

        @block.sync
        def _(sp):
            def body(n, b, half, d, turn):
                sp.wait_ge(w_ready, n + TWO - 1)
                col = bass.ds(d * P, P)
                for name, (k0, k1) in zip(("w_br_gla", "w_br_hgrn", "w_br_ssm"), BRANCH):
                    sp.dma_start(w_raw[b][:, k0:k1, :], io[name][:, col].rearrange("(k p) n -> p k n", p=P)).then_inc(w_loaded[b], 16)
                sp.wait_ge(merged_ready, n + TWO - 1)
                sp.dma_start(gate[b][:], dr["gates"].rearrange("(g r) t -> r g t", g=3)[col, :, bass.ds(half * HT, HT)])\
                    .then_inc(gate_loaded[b], 16)
            tiles(sp, body)

        @block.gpsimd
        def _(pool):
            for half in range(2):
                for p in range(PIECES):
                    if half or p >= 2:
                        pool.wait_ge(y_ready, PIECES * half + p - 1)
                    pool.dma_start(y_raw[p % 2][:], dr["y"][p * PK * P:(p + 1) * PK * P, half * HT:(half + 1) * HT]
                                   .rearrange("(k p) t -> p k t", p=P)).then_inc(y_loaded[p % 2], 16)

        @block.scalar
        def _(act):
            nc.scalar.preload_act_table(ACT.Sigmoid)

            def split(n, b, turn):
                act.wait_ge(w_loaded[b], 48 * turn + 48)
                act.wait_ge(mm_done, n + TWO - 1)
                nc.scalar.copy(w_hi[b][:], w_raw[b][:]).then_inc(w_hi_ready, 1)

            def gates(b, turn):
                act.wait_ge(gate_loaded[b], 16 * turn + 16)
                nc.scalar.activation(gate[b][:], gate[b][:], ACT.Sigmoid).then_inc(gate_ready, 1)

            with act.Fori(0, 2) as half:
                split(DM * half, 0, (DM // 2) * half)
                act.wait_ge(mm_done, DM * half + TWO)
                for p in range(PIECES):
                    act.wait_ge(y_loaded[p % 2], 8 * PIECES * half + 16 * (p // 2 + 1))
                    nc.scalar.copy(y_hi[:, p * PK:(p + 1) * PK, :], y_raw[p % 2][:]).then_inc(y_hi_ready, 1)
                with act.Fori(0, DM // 2 - 1) as i:
                    turn = (DM // 2) * half + i
                    gates(0, turn)
                    split(DM * half + 2 * i + 1, 1, turn)
                    gates(1, turn)
                    split(DM * half + 2 * i + 2, 0, turn + 1)
                turn = (DM // 2) * half + (DM // 2 - 1)
                gates(0, turn)
                split(DM * half + (DM - 1), 1, turn)
                gates(1, turn)

        @block.vector
        def _(dve):
            own = Chain(dve, dve_own)
            dve.sem_inc(merged_ready, TWO)
            dve.sem_inc(w_ready, TWO)

            def before(half):
                dve.wait_ge(mm_done, DM * half + TWO)
                for p in range(PIECES):
                    dve.wait_ge(y_hi_ready, PIECES * half + (p + 1))
                    ks = slice(p * PK, (p + 1) * PK)
                    nc.vector.tensor_tensor(y_lo[:, ks, :], y_raw[p % 2][:], y_hi[:, ks, :].bitcast(F32), ALU.subtract).then_inc(y_ready, 1)

            def split(n, b):
                dve.wait_ge(w_hi_ready, n + 1)
                nc.vector.tensor_tensor(w_lo[b][:], w_raw[b][:], w_hi[b][:].bitcast(F32), ALU.subtract).then_inc(w_ready, 1)

            def gated(n, b, half, d):
                own.turn(n, LINKS)
                dve.wait_ge(gate_ready, n + 1)
                dve.wait_ge(mm_done, n + 1 + TWO)
                nc.vector.tensor_tensor(part[:, 0, :], ps[b][:, 0, :], gate[b][:, 0, :], ALU.mult).then_inc(dve_own, 1)
                own.n += 1
                own.link(nc.vector.tensor_tensor(part[:, 1, :], ps[b][:, 1, :], gate[b][:, 1, :], ALU.mult))
                own.link(nc.vector.tensor_tensor(part[:, 0, :], part[:, 0, :], part[:, 1, :], ALU.add))
                own.link(nc.vector.tensor_tensor(part[:, 1, :], ps[b][:, 2, :], gate[b][:, 2, :], ALU.mult))
                own.link(nc.vector.tensor_tensor(part[:, 0, :], part[:, 0, :], part[:, 1, :], ALU.add))
                ts = bass.ds(half * HT, HT)
                own.link(nc.vector.tensor_copy(m_hi[:, bass.ds(d, 1), ts], part[:, 0:1, :]))
                nc.vector.tensor_tensor(m_lo[:, bass.ds(d, 1), ts], part[:, 0:1, :], m_hi[:, bass.ds(d, 1), ts].bitcast(F32), ALU.subtract)\
                    .then_inc(merged_ready, 1)
                dve.wait_ge(merged_ready, n + 1 + TWO)
                assert own.n == LINKS

            with dve.Fori(0, 2) as half:
                split(DM * half, 0)
                before(half)
                with dve.Fori(0, DM // 2 - 1) as i:
                    for b in range(2):
                        n = DM * half + 2 * i + b
                        split(n + 1, 1 - b)
                        gated(n, b, half, 2 * i + b)
                split(DM * half + (DM - 1), 1)
                gated(DM * half + (DM - 2), 0, half, DM - 2)
                gated(DM * half + (DM - 1), 1, half, DM - 1)

        @block.tensor
        def _(pe):
            pe.sem_inc(mm_done, TWO)

            def body(n, b, half, d, turn):
                pe.wait_ge(w_ready, n + 1 + TWO)
                pe.wait_ge(merged_ready, n + TWO - 1)
                for br, (k0, k1) in enumerate(BRANCH):
                    for k in range(k0, k1):
                        if k % PK == 0:
                            pe.wait_ge(y_ready, PIECES * half + (k // PK + 1))
                        for q, (w, y) in enumerate(((w_hi[b], y_hi), (w_hi[b], y_lo), (w_lo[b], y_hi))):
                            ins = nc.tensor.matmul(ps[b][:, br, :], w[:, k, :], y[:, k, :], start=k == k0 and q == 0, stop=k == k1 - 1 and q == 2)
                ins.then_inc(mm_done, 1)
            tiles(pe, body)


def output_and_route(nc, io, dr, ident, m_hi, m_lo):
    NL = N_GROUPS + N_EXPERTS
    BIG = 3e38
    with ExitStack() as ctx:
        sb = lambda name, shape, dt=F32: ctx.enter_context(nc.sbuf_tensor(name, shape, dt))
        sem = semaphores(nc, ctx)
        w_raw = [sb(f"wo_raw{b}", [P, 2, D]) for b in range(2)]
        w_hi = sb("wo_hi", [P, KT, D], F32R)
        w_lo = sb("wo_lo", [P, KT, D], F32R)
        x_in = [sb(f"xr{b}", [P, D]) for b in range(2)]
        x2 = [sb(f"x2_{b}", [P, D]) for b in range(2)]
        h2 = [sb(f"h2_{b}", [P, D]) for b in range(2)]
        h2T = sb("h2T", [P, KT, P])
        n2 = sb("n2", [P, D])
        stat = sb("stat2", [P, NCH, 2])
        cst = sb("cst2", [P, 1])
        rw = sb("rw", [P, KT, NL])
        rb = sb("rb", [P, NL])
        lg = sb("lg", [P, NCH, NL])
        fill = sb("fill", [P, 1024], U32)
        it32 = sb("it32", [P, N_EXPERTS])
        itg = sb("itg", [P, N_GROUPS])
        grp = sb("grp", [P, N_EXPERTS])
        tok = sb("tok", [P, NCH])
        upper = sb("upper", [P, P])
        ones = sb("ones", [P, P])
        big = lambda name: sb(name, [P, NCH, N_EXPERTS])
        ml, oh1, oh2, tmp, oh, ohp = big("ml"), big("oh1"), big("oh2"), big("tmp"), big("oh"), big("ohp")
        col = lambda name: sb(name, [P, NCH])
        gmax, gsum, gidx, m1, m2, i1, i2, e2, w1, w2, r1, r2 = (col(f"rt_{n}") for n in range(12))
        gt = sb("gt", [P, NCH, N_GROUPS])
        slot = sb("slot", [P, 2, NCH], U32)
        rec = sb("rec", [P, 2, NCH, 4], U32)
        cnt = sb("cnt", [P, N_EXPERTS])
        slab = sb("slab", [P, N_EXPERTS, 7])
        fl, pos, wk, idv = (sb(n, [P, N_EXPERTS * 7]) for n in ("fl", "pos", "wk", "idv"))
        onesf = sb("onesf", [P, N_EXPERTS * 7])
        nth = sb("nth", [P, 1])
        work = sb("work_f", [P, 2])
        work_i = sb("work_i", [P, 2], I32)
        o_ps = [ctx.enter_context(nc.psum_tensor(f"xo{b}", [P, D], F32)) for b in range(2)]
        t_ps = ctx.enter_context(nc.psum_tensor("h2t", [P, D], F32))
        l_ps = ctx.enter_context(nc.psum_tensor("lgp", [P, 512], F32))
        r_ps = ctx.enter_context(nc.psum_tensor("rkp", [P, 512], F32))

        par_in = sem("par_in")
        w_loaded = [sem(f"w_loaded{b}") for b in range(2)]
        x_loaded = [sem(f"x_loaded{b}") for b in range(2)]
        w_hi_ready = sem("w_hi_ready")
        w_ready = sem("w_ready")
        mm_done = sem("mm_done")
        x2_ready = sem("x2_ready")
        rstd_ready = sem("rstd_ready")
        h2_ready = sem("h2_ready")
        h2_scaled = sem("h2_scaled")
        x2_stored = [sem(f"x2_stored{b}") for b in range(2)]
        h2_stored = [sem(f"h2_stored{b}") for b in range(2)]
        hT_ready = sem("hT_ready")
        hT_sb = sem("hT_sb")
        lg_ready = sem("lg_ready")
        lg_in = sem("lg_in")
        pool_own = sem("pool_own")
        const_ready = sem("const_ready")
        filled = sem("filled")
        gate_arg = sem("gate_arg")
        gate_exp = sem("gate_exp")
        pick_arg = sem("pick_arg")
        pick_exp = sem("pick_exp")
        oh_ready = sem("oh_ready")
        rank_ready = sem("rank_ready")
        cnt_ready = sem("cnt_ready")
        rank_read = sem("rank_read")
        rec_ready = sem("rec_ready")
        scattered = sem("scattered")
        work_ready = sem("work_ready")
        work_stored = sem("work_stored")
        dve_own = sem("dve_own")
        act_own = sem("act_own")
        block = ctx.enter_context(nc.Block())

        @block.sync
        def _(sp):
            for p in range(KT // 2):
                if p >= 2:
                    sp.wait_ge(w_ready, p - 1)
                sp.dma_start(w_raw[p % 2][:], io["w_out"][p * 2 * P:(p + 1) * 2 * P, :].rearrange("(k p) n -> p k n", p=P))\
                    .then_inc(w_loaded[p % 2], 16)
            sp.dma_start(n2[:], io["norm2_w"].unsqueeze(0).to_broadcast([P, D])).then_inc(par_in, 16)
            sp.dma_start(rw[:, :, 0:N_GROUPS], io["router_group_w"].rearrange("(k p) n -> p k n", p=P)).then_inc(par_in, 16)
            sp.dma_start(rw[:, :, N_GROUPS:NL], io["router_expert_w"].rearrange("(k p) n -> p k n", p=P)).then_inc(par_in, 16)
            sp.dma_start(rb[:, 0:N_GROUPS], io["router_group_b"].unsqueeze(0).to_broadcast([P, N_GROUPS])).then_inc(par_in, 16)
            sp.dma_start(rb[:, N_GROUPS:NL], io["router_expert_b"].unsqueeze(0).to_broadcast([P, N_EXPERTS])).then_inc(par_in, 16)
            sp.wait_ge(const_ready, 1)
            sp.dma_start(dr["table"].rearrange("(p n) w -> p (n w)", p=P), fill[:]).then_inc(filled, 16)
            for c in range(NCH):
                if c >= 2:
                    sp.wait_ge(x2_ready, c - 1)
                sp.dma_start(x_in[c % 2][:], io["x"][c * CH:(c + 1) * CH, :]).then_inc(x_loaded[c % 2], 16)
                if c >= 1:
                    p = c - 1
                    sp.wait_ge(x2_ready, p + 1)
                    sp.dma_start(dr["x2"][p * CH:(p + 1) * CH, :], x2[p % 2][:]).then_inc(x2_stored[p % 2], 16)
                    sp.wait_ge(h2_ready, p + 1)
                    sp.dma_start(dr["h2"][p * CH:(p + 1) * CH, :], h2[p % 2][:]).then_inc(h2_stored[p % 2], 16)
            p = NCH - 1
            sp.wait_ge(x2_ready, p + 1)
            sp.dma_start(dr["x2"][p * CH:(p + 1) * CH, :], x2[p % 2][:]).then_inc(x2_stored[p % 2], 16)
            sp.wait_ge(h2_ready, p + 1)
            sp.dma_start(dr["h2"][p * CH:(p + 1) * CH, :], h2[p % 2][:]).then_inc(h2_stored[p % 2], 16)
            sp.wait_ge(work_ready, 1)
            sp.dma_start(dr["work"], work_i[0:16, :]).then_inc(work_stored, 16)
            sp.wait_ge(work_stored, 16)
            for b in range(2):
                sp.wait_ge(x2_stored[b], 16 * NCH // 2)
                sp.wait_ge(h2_stored[b], 16 * NCH // 2)

        @block.gpsimd
        def _(pool):
            nc.gpsimd.memset(fill[:], EMPTY).then_inc(const_ready, 1)
            nc.gpsimd.iota(it32[:], pattern=[[1, N_EXPERTS]], base=0, channel_multiplier=0, allow_small_or_imprecise_dtypes=True).then_inc(const_ready, 1)
            nc.gpsimd.iota(itg[:], pattern=[[1, N_GROUPS]], base=0, channel_multiplier=0, allow_small_or_imprecise_dtypes=True).then_inc(const_ready, 1)
            nc.gpsimd.iota(grp[:], pattern=[[1, N_GROUPS], [0, PER_GROUP]], base=0, channel_multiplier=0, allow_small_or_imprecise_dtypes=True).then_inc(const_ready, 1)
            nc.gpsimd.iota(tok[:], pattern=[[CH, NCH]], base=0, channel_multiplier=1, allow_small_or_imprecise_dtypes=True).then_inc(const_ready, 1)
            nc.gpsimd.iota(nth[:], pattern=[[0, 1]], base=1, channel_multiplier=1, allow_small_or_imprecise_dtypes=True).then_inc(const_ready, 1)
            nc.gpsimd.iota(slab[:], pattern=[[0, N_EXPERTS], [SLAB, 7]], base=SLAB, channel_multiplier=0, allow_small_or_imprecise_dtypes=True).then_inc(const_ready, 1)
            nc.gpsimd.iota(idv[:].rearrange("p (e s) -> p e s", s=7), pattern=[[T, N_EXPERTS], [SLAB, 7]], base=SLAB, channel_multiplier=0,
                           allow_small_or_imprecise_dtypes=True).then_inc(const_ready, 1)
            nc.gpsimd.memset(ones[:], 1.0).then_inc(const_ready, 1)
            nc.gpsimd.memset(onesf[:], 1.0).then_inc(const_ready, 1)
            nc.gpsimd.memset(cst[:], EPS).then_inc(const_ready, 1)
            nc.gpsimd.memset(rec[:], 0).then_inc(const_ready, 1)
            nc.gpsimd.memset(upper[:], 1.0).then_inc(pool_own, 1)
            pool.wait_ge(pool_own, 1)
            nc.gpsimd.affine_select(out=upper[:], in_=upper[:], compare_op=ALU.is_gt, fill=0.0, base=0,
                                    pattern=[[1, P]], channel_multiplier=-1).then_inc(const_ready, 1)
            pool.wait_ge(filled, 16)
            pool.wait_ge(rec_ready, 2)
            for pick in range(2):
                for c in range(NCH):
                    pool.indirect_dma_start(out=dr["table"], out_offset=bass.IndirectOffsetOnAxis(ap=slot[:, pick, c:c + 1], axis=0),
                                            in_=rec[:, pick, c, :], in_offset=None).then_inc(scattered, 16)
            pool.wait_ge(scattered, 16 * 2 * NCH)

        N_CONST = 13

        @block.scalar
        def _(act):
            own = Chain(act, act_own)
            nc.scalar.preload_act_table_set(EXP_LN_SET)
            for p in range(KT // 2):
                act.wait_ge(w_loaded[p % 2], 16 * (p // 2 + 1))
                nc.scalar.copy(w_hi[:, 2 * p:2 * p + 2, :], w_raw[p % 2][:]).then_inc(w_hi_ready, 1)
            act.wait_ge(const_ready, N_CONST)
            for c in range(NCH):
                act.wait_ge(x2_ready, c + 1)
                if c >= 2:
                    act.wait_ge(h2_stored[c % 2], 16 * (c // 2))
                    act.wait_ge(hT_ready, c - 1)
                own.link(nc.scalar.activation(h2[c % 2][:], x2[c % 2][:], ACT.Square, accum_out=stat[:, c, 0:1]))
                own.link(nc.scalar.activation(stat[:, c, 0:1], stat[:, c, 0:1], ACT.Ln, scale=1.0 / D, bias=cst[:]))
                nc.scalar.activation(stat[:, c, 1:2], stat[:, c, 0:1], ACT.Exp, scale=-0.5).then_inc(rstd_ready, 1)
                act.wait_ge(hT_ready, c + 1)
                nc.scalar.copy(h2T[:].rearrange("p k t -> p (k t)"), t_ps[:]).then_inc(hT_sb, 1)
            act.wait_ge(gate_arg, 1)
            nc.scalar.activation(gt[:], gt[:], ACT.Exp).then_inc(gate_exp, 1)
            act.wait_ge(pick_arg, 1)
            nc.scalar.activation(e2[:], e2[:], ACT.Exp).then_inc(pick_exp, 1)

        @block.vector
        def _(dve):
            own = Chain(dve, dve_own)
            L = own.link
            tt, ts = nc.vector.tensor_tensor, nc.vector.tensor_scalar
            for p in range(KT // 2):
                dve.wait_ge(w_hi_ready, p + 1)
                tt(w_lo[:, 2 * p:2 * p + 2, :], w_raw[p % 2][:], w_hi[:, 2 * p:2 * p + 2, :].bitcast(F32), ALU.subtract).then_inc(w_ready, 1)
            dve.wait_ge(par_in, 16 * 5)
            dve.wait_ge(const_ready, N_CONST)
            for c in range(NCH):
                b = c % 2
                dve.wait_ge(x_loaded[b], 16 * (c // 2 + 1))
                dve.wait_ge(mm_done, c + 1)
                if c >= 2:
                    dve.wait_ge(x2_stored[b], 16 * (c // 2))
                tt(x2[b][:], o_ps[b][:], x_in[b][:], ALU.add).then_inc(x2_ready, 1)
                dve.wait_ge(rstd_ready, c + 1)
                nc.vector.scalar_tensor_tensor(h2[b][:], x2[b][:], stat[:, c, 1:2], n2[:], ALU.mult, ALU.mult).then_inc(h2_ready, 1)
                dve.wait_ge(lg_ready, c + 1)
                tt(lg[:, c, :], l_ps[:, 0:NL], rb[:], ALU.add).then_inc(lg_in, 1)
            dve.wait_ge(lg_in, NCH)
            g4, e32 = lg[:, :, 0:N_GROUPS], lg[:, :, N_GROUPS:NL]
            b4 = lambda x: x[:].unsqueeze(2).to_broadcast([P, NCH, N_GROUPS])
            b32 = lambda x: x[:].unsqueeze(2).to_broadcast([P, NCH, N_EXPERTS])
            bc = lambda x, n: x[:].unsqueeze(1).to_broadcast([P, NCH, n])
            red = lambda out, in_, op: nc.vector.tensor_reduce(out[:], in_, AX.X, op)
            L(red(gmax, g4, ALU.max))
            tt(gt[:], g4, b4(gmax), ALU.subtract).then_inc(gate_arg, 1)
            dve.wait_ge(gate_exp, 1)
            L(red(gsum, gt[:], ALU.add))
            L(nc.vector.reciprocal(gsum[:], gsum[:]))

            def first_max(index, values, top, iota, n, scratch, wide):
                L(tt(scratch, values, wide(top), ALU.is_equal))
                L(ts(scratch, scratch, -1000.0, 1000.0, ALU.mult, ALU.add))
                L(tt(scratch, scratch, bc(iota, n), ALU.add))
                L(red(index, scratch, ALU.min))

            first_max(gidx, g4, gmax, itg, N_GROUPS, gt[:], b4)
            L(tt(tmp[:], bc(grp, N_EXPERTS), b32(gidx), ALU.is_equal))
            L(tt(ml[:], e32, tmp[:], ALU.mult))
            L(ts(tmp[:], tmp[:], BIG, -BIG, ALU.mult, ALU.add))
            L(tt(ml[:], ml[:], tmp[:], ALU.add))
            L(red(m1, ml[:], ALU.max))
            first_max(i1, ml[:], m1, it32, N_EXPERTS, tmp[:], b32)
            L(tt(oh1[:], bc(it32, N_EXPERTS), b32(i1), ALU.is_equal))
            L(ts(tmp[:], oh1[:], -BIG, None, ALU.mult))
            L(tt(ml[:], ml[:], tmp[:], ALU.add))
            L(red(m2, ml[:], ALU.max))
            first_max(i2, ml[:], m2, it32, N_EXPERTS, tmp[:], b32)
            L(tt(oh2[:], bc(it32, N_EXPERTS), b32(i2), ALU.is_equal))
            L(tt(oh[:], oh1[:], oh2[:], ALU.add))
            L(nc.vector.memset(ohp[:, 0, :], 0.0))
            for c in range(1, NCH):
                L(tt(ohp[:, c, :], ohp[:, c - 1, :], oh[:, c - 1, :], ALU.add))
            tt(e2[:], m2[:], m1[:], ALU.subtract).then_inc(pick_arg, 1)
            tt(cnt[:], ohp[:, NCH - 1, :], oh[:, NCH - 1, :], ALU.add).then_inc(oh_ready, 1)
            dve.wait_ge(pick_exp, 1)
            L(nc.vector.tensor_scalar_add(w1[:], e2[:], 1.0))
            L(nc.vector.reciprocal(w1[:], w1[:]))
            L(tt(w1[:], w1[:], gsum[:], ALU.mult))
            L(tt(w2[:], w1[:], e2[:], ALU.mult))
            dve.wait_ge(rank_ready, 1)
            rank = r_ps[:, 0:NCH * N_EXPERTS].rearrange("p (c e) -> p c e", e=N_EXPERTS)
            for pick, (o1, ix, r, w) in enumerate(((oh1, i1, r1, w1), (oh2, i2, r2, w2))):
                L(tt(ml[:], rank, o1[:], ALU.mult))
                L(red(r, ml[:], ALU.add))
                L(nc.vector.scalar_tensor_tensor(r[:], ix[:], float(T), r[:], ALU.mult, ALU.add))
                L(nc.vector.tensor_copy(slot[:, pick, :], r[:]))
                L(nc.vector.tensor_copy(rec[:, pick, :, 0], tok[:]))
                L(nc.vector.tensor_scalar_add(rec[:, pick, :, 1], tok[:], float(pick * T)))
                nc.vector.tensor_copy(rec[:, pick, :, 2].bitcast(F32), w[:]).then_inc(rec_ready, 1)
            dve.wait_ge(cnt_ready, 1)
            L(nc.vector.tensor_copy(cnt[:], l_ps[:, 0:N_EXPERTS]))
            f3 = fl[:].rearrange("p (e s) -> p e s", s=7)
            L(tt(f3, cnt[:].unsqueeze(2).to_broadcast([P, N_EXPERTS, 7]), slab[:], ALU.is_gt))
            L(nc.vector.tensor_tensor_scan(pos[:], onesf[:], fl[:], 0.0, ALU.mult, ALU.add))
            L(ts(pos[:], pos[:], nth[:], None, ALU.is_equal))
            L(tt(fl[:], fl[:], pos[:], ALU.mult))
            L(tt(wk[:], fl[:], idv[:], ALU.mult))
            L(nc.vector.reduce_sum(work[:, 0:1], wk[:], AX.X))
            L(tt(wk[:].rearrange("p (e s) -> p e s", s=7), f3, it32[:].unsqueeze(2).to_broadcast([P, N_EXPERTS, 7]), ALU.mult))
            L(nc.vector.reduce_sum(work[:, 1:2], wk[:], AX.X))
            nc.vector.tensor_copy(work_i[:], work[:]).then_inc(work_ready, 1)

        @block.tensor
        def _(pe):
            def product(c):
                if c >= 2:
                    pe.wait_ge(x2_ready, c - 1)
                cs = slice(c * CH, (c + 1) * CH)
                for k in range(KT):
                    if c == 0 and k % 2 == 0:
                        pe.wait_ge(w_ready, k // 2 + 1)
                    for q, (m, w) in enumerate(((m_hi, w_hi), (m_hi, w_lo), (m_lo, w_hi))):
                        for half in range(2):
                            hs = slice(half * 512, half * 512 + 512)
                            ins = nc.tensor.matmul(o_ps[c % 2][:, hs], m[:, k, cs], w[:, k, hs],
                                                   start=k == 0 and q == 0, stop=k == KT - 1 and q == 2)
                ins.then_inc(mm_done, 1)

            def route(c):
                pe.wait_ge(h2_ready, c + 1)
                if c >= 1:
                    pe.wait_ge(hT_sb, c)
                for k in range(KT):
                    ins = nc.tensor.transpose(t_ps[:, k * P:(k + 1) * P], h2[c % 2][:, k * P:(k + 1) * P], ident[:])
                ins.then_inc(hT_ready, 1)
                pe.wait_ge(hT_sb, c + 1)
                if c >= 1:
                    pe.wait_ge(lg_in, c)
                for k in range(KT):
                    ins = nc.tensor.matmul(l_ps[:, 0:NL], h2T[:, k, :], rw[:, k, :], start=k == 0, stop=k == KT - 1)
                ins.then_inc(lg_ready, 1)

            product(0)
            pe.wait_ge(const_ready, N_CONST)
            pe.wait_ge(par_in, 16 * 5)
            for c in range(1, NCH):
                product(c)
                route(c - 1)
            route(NCH - 1)
            pe.wait_ge(oh_ready, 1)
            n = NCH * N_EXPERTS
            nc.tensor.matmul(r_ps[:, 0:n], upper[:], oh[:].rearrange("p c e -> p (c e)"), start=True, stop=False)
            nc.tensor.matmul(r_ps[:, 0:n], ones[:], ohp[:].rearrange("p c e -> p (c e)"), start=False, stop=True).then_inc(rank_ready, 1)
            nc.tensor.matmul(l_ps[:, 0:N_EXPERTS], ones[:], cnt[:], start=True, stop=True).then_inc(cnt_ready, 1)


def experts_first_slabs(nc, io, dr, ident):
    LAST = N_EXPERTS - 1
    FK = FF // P
    GU, DN = 4, 2
    GK, DK = 2 * KT // GU, FK // DN
    with ExitStack() as ctx:
        sb = lambda name, shape, dt=F32: ctx.enter_context(nc.sbuf_tensor(name, shape, dt))
        sem = semaphores(nc, ctx)
        many = lambda n, name, shape, dt=F32: [sb(f"{name}{b}", shape, dt) for b in range(n)]
        gu_raw = many(GU, "gu_raw", [P, GK, FF])
        gu_hi, gu_lo = many(GU, "gu_hi", [P, GK, FF], F32R), many(GU, "gu_lo", [P, GK, FF], F32R)
        dn_raw = many(DN, "dn_raw", [P, DK, D])
        dn_hi, dn_lo = many(DN, "dn_hi", [P, DK, D], F32R), many(DN, "dn_lo", [P, DK, D], F32R)
        recs = sb("recs", [P, N_EXPERTS, 4], U32)
        g_idx, s_idx = many(2, "g_idx", [P, 1], U32), many(2, "s_idx", [P, 1], U32)
        xe, ye = many(2, "xe", [P, D]), many(2, "ye", [P, D])
        xT_hi, xT_lo = many(2, "xeT_hi", [P, KT, P], F32R), many(2, "xeT_lo", [P, KT, P], F32R)
        sg = sb("sg", [P, FF])
        hid = sb("hid", [P, FF])
        hT_hi, hT_lo = sb("hidT_hi", [P, FK, P], F32R), sb("hidT_lo", [P, FK, P], F32R)
        g_ps = ctx.enter_context(nc.psum_tensor("g_ps", [P, FF], F32))
        u_ps = ctx.enter_context(nc.psum_tensor("u_ps", [P, FF], F32))
        y_ps = ctx.enter_context(nc.psum_tensor("y_ps", [P, D], F32))
        xT_ps = ctx.enter_context(nc.psum_tensor("xT_ps", [P, D], F32))
        hT_ps = ctx.enter_context(nc.psum_tensor("hT_ps", [P, FF], F32))
        recs_in = sem("recs_in")
        zeroed = sem("xe_zeroed")
        gu_in = [sem(f"gu_in{p}") for p in range(GU)]
        dn_in = [sem(f"dn_in{p}") for p in range(DN)]
        gu_hi_ready = sem("gu_hi_ready")
        gu_ready = sem("gu_ready")
        gu_used = sem("gu_used")
        dn_hi_ready = sem("dn_hi_ready")
        dn_ready = sem("dn_ready")
        dn_used = sem("dn_used")
        gi_ready = sem("gi_ready")
        si_ready = sem("si_ready")
        gathered = [sem(f"gathered{b}") for b in range(2)]
        scattered = [sem(f"scattered{b}") for b in range(2)]
        xT_ready = sem("xT_ready")
        xT_hi_ready = sem("xT_hi_ready")
        xT_split = sem("xT_split")
        silu_ready = sem("silu_ready")
        hid_ready = sem("hid_ready")
        hT_ready = sem("hT_ready")
        hT_hi_ready = sem("hT_hi_ready")
        hT_split = sem("hT_split")
        y_ready = sem("y_ready")
        passed = sem("passed")
        block = ctx.enter_context(nc.Block())

        def experts(eng, body):
            for e in range(2):
                body(e, e, 0)
            with eng.Fori(0, (N_EXPERTS - 4) // 2) as i:
                for b in range(2):
                    body(2 * i + (2 + b), b, i + 1)
            for e in (LAST - 1, LAST):
                body(e, e % 2, e // 2)

        first = lambda e: isinstance(e, int) and e == 0
        last = lambda e: isinstance(e, int) and e == LAST

        @block.sync
        def _(sp):
            sp.dma_start(recs[:], dr["table"].rearrange("(e s) w -> s e w", s=T)[0:SLAB]).then_inc(recs_in, 16)

            def gate_up(e):
                for p in range(GU):
                    wait_past(sp, gu_ready, GU * e + (p + 1 - GU))
                    w = io["moe_w_gate" if p < GU // 2 else "moe_w_up"][bass.ds(e, 1)]
                    k = p % (GU // 2) * GK * P
                    sp.dma_start(gu_raw[p][:], w[:, k:k + GK * P, :].rearrange("o (k p) f -> p (o k) f", p=P)).then_inc(gu_in[p], 16)

            def down(e):
                for p in range(DN):
                    wait_past(sp, dn_ready, DN * e + (p + 1 - DN))
                    w = io["moe_w_down"][bass.ds(e, 1)]
                    sp.dma_start(dn_raw[p][:], w[:, p * DK * P:(p + 1) * DK * P, :].rearrange("o (k p) d -> p (o k) d", p=P))\
                        .then_inc(dn_in[p], 16)

            def body(e, b, turn):
                if not last(e):
                    gate_up(e + 1)
                down(e)
            gate_up(0)
            experts(sp, body)

        @block.gpsimd
        def _(pool):
            for b in range(2):
                nc.gpsimd.memset(xe[b][:], 0.0).then_inc(zeroed, 1)
            pool.wait_ge(zeroed, 2)
            pool.wait_ge(recs_in, 16)

            def gather(e, b):
                wait_past(pool, xT_ready, e - 1)
                pool.sem_inc(passed, 1)
                nc.gpsimd.tensor_copy(g_idx[b][:], recs[:, bass.ds(e, 1), 0]).then_inc(gi_ready, 1)
                pool.wait_ge(gi_ready, e + 1)
                pool.sem_inc(passed, 1)
                pool.indirect_dma_start(out=xe[b][:], out_offset=None, in_=dr["h2"],
                                        in_offset=bass.IndirectOffsetOnAxis(ap=g_idx[b][:], axis=0),
                                        bounds_check=T - 1, oob_is_err=False).then_inc(gathered[b], 16)

            def scatter(e, b, turn):
                wait_past(pool, scattered[b], 16 * turn)
                pool.sem_inc(passed, 1)
                nc.gpsimd.tensor_copy(s_idx[b][:], recs[:, bass.ds(e, 1), 1]).then_inc(si_ready, 1)
                pool.wait_ge(si_ready, e + 1)
                pool.wait_ge(y_ready, e + 1)
                pool.sem_inc(passed, 1)
                pool.indirect_dma_start(out=dr["pairs"], out_offset=bass.IndirectOffsetOnAxis(ap=s_idx[b][:], axis=0),
                                        in_=ye[b][:], in_offset=None, bounds_check=2 * T - 1, oob_is_err=False)\
                    .then_inc(scattered[b], 16)

            def body(e, b, turn):
                if not last(e):
                    gather(e + 1, 1 - b)
                if not first(e):
                    scatter(e - 1, 1 - b, turn - 1 + b)
            gather(0, 0)
            experts(pool, body)
            scatter(LAST, 1, LAST // 2)
            for b in range(2):
                pool.wait_ge(scattered[b], 16 * N_EXPERTS // 2)

        @block.scalar
        def _(act):
            nc.scalar.preload_act_table(ACT.Silu)

            def gate_up(e, p):
                act.wait_ge(gu_in[p], 16 * e + 16)
                wait_past(act, gu_used, GU * e + (p + 1 - GU))
                nc.scalar.copy(gu_hi[p][:], gu_raw[p][:]).then_inc(gu_hi_ready, 1)

            def down(e, p):
                act.wait_ge(dn_in[p], 16 * e + 16)
                wait_past(act, dn_used, DN * e + (p + 1 - DN))
                nc.scalar.copy(dn_hi[p][:], dn_raw[p][:]).then_inc(dn_hi_ready, 1)

            def rows(e, b):
                act.wait_ge(xT_ready, e + 1)
                wait_past(act, gu_used, GU * e - GU)
                nc.scalar.copy(xT_hi[b][:].rearrange("p k t -> p (k t)"), xT_ps[:]).then_inc(xT_hi_ready, 1)

            def body(e, b, turn):
                if not last(e):
                    gate_up(e + 1, 0)
                    gate_up(e + 1, 1)
                act.wait_ge(gu_used, GU * e + GU // 2)
                wait_past(act, hid_ready, e)
                nc.scalar.activation(sg[:], g_ps[:], ACT.Silu).then_inc(silu_ready, 1)
                if not last(e):
                    gate_up(e + 1, 2)
                    gate_up(e + 1, 3)
                    rows(e + 1, 1 - b)
                for p in range(DN):
                    down(e, p)
                act.wait_ge(hT_ready, e + 1)
                wait_past(act, dn_used, DN * e)
                nc.scalar.copy(hT_hi[:].rearrange("p k t -> p (k t)"), hT_ps[:]).then_inc(hT_hi_ready, 1)
            for p in range(GU):
                gate_up(0, p)
            rows(0, 0)
            experts(act, body)

        @block.vector
        def _(dve):
            dve.wait_ge(recs_in, 16)

            def gate_up(e, p):
                dve.wait_ge(gu_hi_ready, GU * e + (p + 1))
                nc.vector.tensor_tensor(gu_lo[p][:], gu_raw[p][:], gu_hi[p][:].bitcast(F32), ALU.subtract).then_inc(gu_ready, 1)

            def down(e, p):
                dve.wait_ge(dn_hi_ready, DN * e + (p + 1))
                nc.vector.tensor_tensor(dn_lo[p][:], dn_raw[p][:], dn_hi[p][:].bitcast(F32), ALU.subtract).then_inc(dn_ready, 1)

            def rows(e, b):
                dve.wait_ge(xT_hi_ready, e + 1)
                nc.vector.tensor_tensor(xT_lo[b][:].rearrange("p k t -> p (k t)"), xT_ps[:],
                                        xT_hi[b][:].rearrange("p k t -> p (k t)").bitcast(F32), ALU.subtract).then_inc(xT_split, 1)

            def weigh(e, b, turn):
                dve.wait_ge(dn_used, DN * e + DN)
                wait_past(dve, scattered[b], 16 * turn)
                w = recs[:, bass.ds(e, 1), 2].bitcast(F32).to_broadcast([P, D])
                nc.vector.tensor_tensor(ye[b][:], y_ps[:], w, ALU.mult).then_inc(y_ready, 1)

            def body(e, b, turn):
                if not last(e):
                    for p in range(3):
                        gate_up(e + 1, p)
                dve.wait_ge(silu_ready, e + 1)
                dve.wait_ge(gu_used, GU * e + GU)
                wait_past(dve, hT_ready, e)
                nc.vector.tensor_tensor(hid[:], u_ps[:], sg[:], ALU.mult).then_inc(hid_ready, 1)
                if not last(e):
                    gate_up(e + 1, 3)
                    rows(e + 1, 1 - b)
                for p in range(DN):
                    down(e, p)
                if not first(e):
                    weigh(e - 1, 1 - b, turn - 1 + b)
                dve.wait_ge(hT_hi_ready, e + 1)
                nc.vector.tensor_tensor(hT_lo[:].rearrange("p k t -> p (k t)"), hT_ps[:],
                                        hT_hi[:].rearrange("p k t -> p (k t)").bitcast(F32), ALU.subtract).then_inc(hT_split, 1)
            for p in range(GU):
                gate_up(0, p)
            rows(0, 0)
            experts(dve, body)
            weigh(LAST, 1, LAST // 2)

        @block.tensor
        def _(pe):
            def rows(e, b, turn):
                pe.wait_ge(gathered[b], 16 * turn + 16)
                wait_past(pe, xT_split, e)
                for k in range(KT):
                    ins = nc.tensor.transpose(xT_ps[:, k * P:(k + 1) * P], xe[b][:, k * P:(k + 1) * P], ident[:])
                ins.then_inc(xT_ready, 1)

            def down(e):
                pe.wait_ge(hT_split, e + 1)
                wait_past(pe, y_ready, e)
                for p in range(DN):
                    pe.wait_ge(dn_ready, DN * e + (p + 1))
                    for k in range(DK):
                        for q, (h, w) in enumerate(((hT_hi, dn_hi[p]), (hT_hi, dn_lo[p]), (hT_lo, dn_hi[p]))):
                            for half in range(2):
                                hs = slice(half * 512, half * 512 + 512)
                                ins = nc.tensor.matmul(y_ps[:, hs], h[:, p * DK + k, :], w[:, k, hs],
                                                       start=p == 0 and k == 0 and q == 0, stop=p == DN - 1 and k == DK - 1 and q == 2)
                    ins.then_inc(dn_used, 1)

            def body(e, b, turn):
                pe.wait_ge(xT_split, e + 1)
                for p in range(GU):
                    ps, at = (g_ps, 0) if p < GU // 2 else (u_ps, GU // 2)
                    if p == 0:
                        wait_past(pe, silu_ready, e)
                    if p == GU // 2:
                        wait_past(pe, hid_ready, e)
                    pe.wait_ge(gu_ready, GU * e + (p + 1))
                    for k in range(GK):
                        for q, (x, w) in enumerate(((xT_hi[b], gu_hi[p]), (xT_hi[b], gu_lo[p]), (xT_lo[b], gu_hi[p]))):
                            ins = nc.tensor.matmul(ps[:], x[:, (p - at) * GK + k, :], w[:, k, :],
                                                   start=p == at and k == 0 and q == 0,
                                                   stop=p == at + GU // 2 - 1 and k == GK - 1 and q == 2)
                    ins.then_inc(gu_used, 1)
                if not last(e):
                    rows(e + 1, 1 - b, turn + b)
                if not first(e):
                    down(e - 1)
                pe.wait_ge(hid_ready, e + 1)
                wait_past(pe, hT_split, e)
                for k in range(FK):
                    ins = nc.tensor.transpose(hT_ps[:, k * P:(k + 1) * P], hid[:, k * P:(k + 1) * P], ident[:])
                ins.then_inc(hT_ready, 1)
            rows(0, 0, 0)
            experts(pe, body)
            down(LAST)


def experts_further_slabs(nc, io, dr, ident):
    FK = FF // P
    with ExitStack() as ctx:
        sb = lambda name, shape, dt=F32: ctx.enter_context(nc.sbuf_tensor(name, shape, dt))
        sem = semaphores(nc, ctx)
        wg, wu, wdn = sb("xwg", [P, KT, FF]), sb("xwu", [P, KT, FF]), sb("xwd", [P, FK, D])
        todo = sb("todo", [1, 2 * 16], I32)
        rec = sb("xrec", [P, 4], U32)
        xe, ye = sb("xxe", [P, D]), sb("xye", [P, D])
        xT = sb("xxT", [P, KT, P])
        sg, hid = sb("xsg", [P, FF]), sb("xhid", [P, FF])
        hT = sb("xhT", [P, FK, P])
        g_ps = ctx.enter_context(nc.psum_tensor("xg_ps", [P, FF], F32))
        u_ps = ctx.enter_context(nc.psum_tensor("xu_ps", [P, FF], F32))
        y_ps = ctx.enter_context(nc.psum_tensor("xy_ps", [P, D], F32))
        xT_ps = ctx.enter_context(nc.psum_tensor("xxT_ps", [P, D], F32))
        hT_ps = ctx.enter_context(nc.psum_tensor("xhT_ps", [P, FF], F32))
        todo_in = sem("todo_in")
        zeroed = sem("xe_zeroed")
        rec_in = sem("rec_in")
        w_in = sem("w_in")
        gathered = sem("gathered")
        xT_ready = sem("xT_ready")
        xT_sb = sem("xT_sb")
        gu_done = sem("gu_done")
        silu_ready = sem("silu_ready")
        hid_ready = sem("hid_ready")
        hT_ready = sem("hT_ready")
        hT_sb = sem("hT_sb")
        d_done = sem("d_done")
        y_ready = sem("y_ready")
        scattered = sem("scattered")
        slab_done = sem("slab_done")
        passed = sem("passed")
        block = ctx.enter_context(nc.Block())

        def slabs(eng, body):
            eng.wait_ge(todo_in, 16)
            any_place = eng.value_load(todo[0:1, 0:1], min_val=0, max_val=N_EXPERTS * T - SLAB)
            with eng.If(any_place > 0):
                with eng.Fori(0, N_EXTRA) as n:
                    place = eng.value_load(todo[0:1, bass.ds(2 * n, 1)], min_val=0, max_val=N_EXPERTS * T - SLAB)
                    expert = eng.value_load(todo[0:1, bass.ds(2 * n + 1, 1)], min_val=0, max_val=N_EXPERTS - 1)
                    with eng.If(place > 0):
                        body(n, place, expert)

        @block.sync
        def _(sp):
            sp.sem_inc(slab_done, 1)
            sp.dma_start(todo[:], dr["work"].rearrange("(o n) w -> o (n w)", o=1)).then_inc(todo_in, 16)

            def body(n, place, expert):
                sp.wait_ge(slab_done, n + 1)
                sp.dma_start(rec[:], dr["table"][bass.ds(place, SLAB), :]).then_inc(rec_in, 16)
                one = bass.ds(expert, 1)
                sp.dma_start(wg[:], io["moe_w_gate"][one].rearrange("o (k p) f -> p (o k) f", p=P)).then_inc(w_in, 16)
                sp.dma_start(wu[:], io["moe_w_up"][one].rearrange("o (k p) f -> p (o k) f", p=P)).then_inc(w_in, 16)
                sp.dma_start(wdn[:], io["moe_w_down"][one].rearrange("o (k p) d -> p (o k) d", p=P)).then_inc(w_in, 16)
            slabs(sp, body)

        @block.gpsimd
        def _(pool):
            nc.gpsimd.memset(xe[:], 0.0).then_inc(zeroed, 1)
            pool.wait_ge(zeroed, 1)

            def body(n, place, expert):
                pool.wait_ge(rec_in, 16 * n + 16)
                pool.sem_inc(passed, 1)
                pool.indirect_dma_start(out=xe[:], out_offset=None, in_=dr["h2"],
                                        in_offset=bass.IndirectOffsetOnAxis(ap=rec[:, 0:1], axis=0),
                                        bounds_check=T - 1, oob_is_err=False).then_inc(gathered, 16)
                pool.wait_ge(y_ready, n + 1)
                pool.sem_inc(passed, 1)
                pool.indirect_dma_start(out=dr["pairs"], out_offset=bass.IndirectOffsetOnAxis(ap=rec[:, 1:2], axis=0),
                                        in_=ye[:], in_offset=None, bounds_check=2 * T - 1, oob_is_err=False)\
                    .then_inc(scattered, 16)
                pool.wait_ge(scattered, 16 * n + 16)
                pool.sem_inc(slab_done, 1)
            slabs(pool, body)

        @block.scalar
        def _(act):
            nc.scalar.preload_act_table(ACT.Silu)

            def body(n, place, expert):
                act.wait_ge(xT_ready, n + 1)
                nc.scalar.copy(xT[:].rearrange("p k t -> p (k t)"), xT_ps[:]).then_inc(xT_sb, 1)
                act.wait_ge(gu_done, n + 1)
                nc.scalar.activation(sg[:], g_ps[:], ACT.Silu).then_inc(silu_ready, 1)
                act.wait_ge(hT_ready, n + 1)
                nc.scalar.copy(hT[:].rearrange("p k t -> p (k t)"), hT_ps[:]).then_inc(hT_sb, 1)
            slabs(act, body)

        @block.vector
        def _(dve):
            def body(n, place, expert):
                dve.wait_ge(silu_ready, n + 1)
                nc.vector.tensor_tensor(hid[:], u_ps[:], sg[:], ALU.mult).then_inc(hid_ready, 1)
                dve.wait_ge(d_done, n + 1)
                nc.vector.tensor_tensor(ye[:], y_ps[:], rec[:, 2:3].bitcast(F32).to_broadcast([P, D]), ALU.mult).then_inc(y_ready, 1)
            slabs(dve, body)

        @block.tensor
        def _(pe):
            def body(n, place, expert):
                pe.wait_ge(gathered, 16 * n + 16)
                for k in range(KT):
                    ins = nc.tensor.transpose(xT_ps[:, k * P:(k + 1) * P], xe[:, k * P:(k + 1) * P], ident[:])
                ins.then_inc(xT_ready, 1)
                pe.wait_ge(xT_sb, n + 1)
                pe.wait_ge(w_in, 48 * n + 48)
                for ps, w in ((g_ps, wg), (u_ps, wu)):
                    for k in range(KT):
                        ins = nc.tensor.matmul(ps[:], xT[:, k, :], w[:, k, :], start=k == 0, stop=k == KT - 1)
                ins.then_inc(gu_done, 1)
                pe.wait_ge(hid_ready, n + 1)
                for k in range(FK):
                    ins = nc.tensor.transpose(hT_ps[:, k * P:(k + 1) * P], hid[:, k * P:(k + 1) * P], ident[:])
                ins.then_inc(hT_ready, 1)
                pe.wait_ge(hT_sb, n + 1)
                for k in range(FK):
                    for half in range(2):
                        hs = slice(half * 512, half * 512 + 512)
                        ins = nc.tensor.matmul(y_ps[:, hs], hT[:, k, :], wdn[:, k, hs], start=k == 0, stop=k == FK - 1)
                ins.then_inc(d_done, 1)
            slabs(pe, body)


def finish(nc, io, dr, out):
    with ExitStack() as ctx:
        sb = lambda name, shape, dt=F32: ctx.enter_context(nc.sbuf_tensor(name, shape, dt))
        sem = semaphores(nc, ctx)
        NB = 4
        rows = [sb(f"rows{b}", [P, 3, D]) for b in range(NB)]
        sq = sb("fsq", [P, D])
        fw = sb("fw", [P, D])
        stat = sb("fstat", [P, NCH, 2])
        cst = sb("fcst", [P, 1])
        loaded = [sem(f"loaded{b}") for b in range(NB)]
        fw_in = sem("fw_in")
        c_ready = sem("c_ready")
        sum_ready = sem("sum_ready")
        rstd_ready = sem("rstd_ready")
        y_ready = sem("y_ready")
        stored = [sem(f"stored{b}") for b in range(NB)]
        dve_own = sem("dve_own")
        act_own = sem("act_own")
        block = ctx.enter_context(nc.Block())

        @block.sync
        def _(sp):
            for c in range(NCH):
                b, cs = c % NB, slice(c * CH, (c + 1) * CH)
                if c >= NB:
                    sp.wait_ge(stored[b], 16 * (c // NB))
                sp.dma_start(rows[b][:, 0, :], dr["x2"][cs, :]).then_inc(loaded[b], 16)
                sp.dma_start(rows[b][:, 1:3, :], dr["pairs"].rearrange("(a t) d -> t a d", a=2)[cs]).then_inc(loaded[b], 16)
                if c == 0:
                    sp.dma_start(fw[:], io["final_norm_w"].unsqueeze(0).to_broadcast([P, D])).then_inc(fw_in, 16)

        @block.vector
        def _(dve):
            own = Chain(dve, dve_own)
            nc.vector.memset(cst[:], EPS).then_inc(c_ready, 1)
            dve.wait_ge(fw_in, 16)

            def add(c):
                b = c % NB
                dve.wait_ge(loaded[b], 32 * (c // NB + 1))
                own.link(nc.vector.tensor_tensor(rows[b][:, 1, :], rows[b][:, 1, :], rows[b][:, 2, :], ALU.add))
                nc.vector.tensor_tensor(rows[b][:, 0, :], rows[b][:, 0, :], rows[b][:, 1, :], ALU.add).then_inc(sum_ready, 1)

            add(0)
            for c in range(NCH):
                if c + 1 < NCH:
                    add(c + 1)
                b = c % NB
                dve.wait_ge(rstd_ready, c + 1)
                nc.vector.scalar_tensor_tensor(rows[b][:, 2, :], rows[b][:, 0, :], stat[:, c, 1:2], fw[:], ALU.mult, ALU.mult)\
                    .then_inc(y_ready, 1)

        @block.scalar
        def _(act):
            own = Chain(act, act_own)
            nc.scalar.preload_act_table_set(EXP_LN_SET)
            act.wait_ge(c_ready, 1)
            for c in range(NCH):
                b = c % NB
                act.wait_ge(sum_ready, c + 1)
                own.link(nc.scalar.activation(sq[:], rows[b][:, 0, :], ACT.Square, accum_out=stat[:, c, 0:1]))
                own.link(nc.scalar.activation(stat[:, c, 0:1], stat[:, c, 0:1], ACT.Ln, scale=1.0 / D, bias=cst[:]))
                nc.scalar.activation(stat[:, c, 1:2], stat[:, c, 0:1], ACT.Exp, scale=-0.5).then_inc(rstd_ready, 1)
                act.wait_ge(y_ready, c + 1)
                act.dma_start(out[c * CH:(c + 1) * CH, :], rows[b][:, 2, :]).then_inc(stored[b], 16)
            for b in range(NB):
                act.wait_ge(stored[b], 16 * NCH // NB)


def build(nc, io, out):
    dr = {name: nc.dram_tensor(f"s_{name}", shape, dt).ap() for name, shape, dt in (
        ("qk", [512, T], F32),
        ("silu_a", [1024, T], F32),
        ("silu_b", [1536, T], F32),
        ("v", [T, 1024], F32),
        ("xbc", [2048, T], F32),
        ("gates", [3072, T], F32),
        ("k_hg", [512, T], F32),
        ("cum", [768, T], F32),
        ("dt", [16, T], F32), ("b_ssm", [16, T], F32),
        ("y", [2048, T], F32),
        ("x2", [T, D], F32), ("h2", [T, D], F32),
        ("table", [N_EXPERTS * T, 4], U32),
        ("work", [16, 2], I32),
        ("pairs", [2 * T, D], F32))}
    with ExitStack() as ctx:
        ctx.enter_context(nc.allow_non_contiguous_dma(reason="small parameters, one element for a partition"))
        ident = ctx.enter_context(nc.sbuf_tensor("ident", [P, P], F32))
        with nc.sbuf_tensor("h_hi", [P, KT, T], F32R) as h_hi, nc.sbuf_tensor("h_lo", [P, KT, T], F32R) as h_lo:
            with ExitStack() as pairs:
                two = lambda name, dt: [pairs.enter_context(nc.sbuf_tensor(f"{name}{b}", [P, KT, PAIR], dt)) for b in range(2)]
                w_parts = two("w_raw", F32), two("w_hi", F32R), two("w_lo", F32R)
                norm1_and_decays(nc, io, dr, ident, h_hi, h_lo, *w_parts)
                project(nc, io, dr, h_hi, h_lo, *w_parts)
        mixers(nc, io, dr, ident)
        with nc.sbuf_tensor("m_hi", [P, KT, T], F32R) as m_hi, nc.sbuf_tensor("m_lo", [P, KT, T], F32R) as m_lo:
            merge(nc, io, dr, m_hi, m_lo)
            output_and_route(nc, io, dr, ident, m_hi, m_lo)
        experts_first_slabs(nc, io, dr, ident)
        experts_further_slabs(nc, io, dr, ident)
        finish(nc, io, dr, out)


def kernel(**inputs):
    import concourse.bacc as bacc
    from concourse.bass_utils import run_bass_kernel_spmd

    layer = {name: np.ascontiguousarray(a[0]) for name, a in inputs.items() if name != "final_norm_w"}
    layer["final_norm_w"] = np.ascontiguousarray(inputs["final_norm_w"])
    layer["taps"] = np.ascontiguousarray(np.concatenate([layer.pop("ssm_conv_w"), layer.pop("ssm_conv_b")[None]]).T)
    nc = bacc.Bacc("TRN2", target_bir_lowering=False, num_devices=1)
    io = {name: nc.dram_tensor(name, a.shape, mybir.dt.from_np(a.dtype), kind="ExternalInput").ap() for name, a in layer.items()}
    out = nc.dram_tensor("out", (T, D), F32, kind="ExternalOutput").ap()
    build(nc, io, out)
    r = run_bass_kernel_spmd(nc, [layer], core_ids=[0])
    return r.results[0]["out"].reshape(1, T, D)
```
